# Optimizing a Trainium2 kernel written in Bass

```python
import jax, jax.numpy as jnp
from jax import lax
import numpy as np
import math

D_MODEL = 2048
BATCH = 1
SEQ = 256
DEPTH = 1

CHUNK = 64
EPS = 1e-6
MIX_WIDTH = D_MODEL

SSD_HEAD_DIM = 64
SSD_INNER = MIX_WIDTH // 2
SSD_HEADS = SSD_INNER // SSD_HEAD_DIM
SSD_GROUPS = 2
SSD_STATE = 128
SSD_CONV = 4
SSD_CONV_DIM = SSD_INNER + 2 * SSD_GROUPS * SSD_STATE

FOX_HEAD_DIM = 64
FOX_INNER = MIX_WIDTH - SSD_INNER
FOX_HEADS = FOX_INNER // FOX_HEAD_DIM
Q_BLOCK = 128

PEER_HEADS = 8
PEER_N_KEYS = 128
PEER_N_EXPERTS = PEER_N_KEYS * PEER_N_KEYS
PEER_KEY_DIM = 256
PEER_TOPK = 16
PEER_TOKEN_BLOCK = 128

IN_SPLITS = (SSD_INNER, SSD_CONV_DIM, SSD_HEADS, FOX_INNER, FOX_INNER, FOX_INNER, FOX_HEADS)
IN_PROJ_DIM = sum(IN_SPLITS)


def rmsnorm(x, w):
    xf = x.astype(jnp.float32)
    xf = xf * lax.rsqrt(jnp.mean(xf * xf, axis=-1, keepdims=True) + EPS)
    return (xf * w.astype(jnp.float32)).astype(x.dtype)

def ssd_chunked(xs, dt, A, Bm, Cm):
    b, l = xs.shape[:2]
    nc = l // CHUNK
    R = SSD_HEADS // SSD_GROUPS
    x = xs.astype(jnp.float32).reshape(b, nc, CHUNK, SSD_GROUPS, R, SSD_HEAD_DIM)
    dtc = dt.reshape(b, nc, CHUNK, SSD_GROUPS, R)
    Bc = Bm.astype(jnp.float32).reshape(b, nc, CHUNK, SSD_GROUPS, SSD_STATE)
    Cc = Cm.astype(jnp.float32).reshape(b, nc, CHUNK, SSD_GROUPS, SSD_STATE)
    a = dtc * A.reshape(SSD_GROUPS, R)
    a_cum = jnp.cumsum(a, axis=2)
    xdt = x * dtc[..., None]
    seg = a_cum[:, :, :, None] - a_cum[:, :, None]
    tri = jnp.tril(jnp.ones((CHUNK, CHUNK), dtype=bool))[None, None, :, :, None, None]
    L = jnp.exp(jnp.where(tri, seg, -jnp.inf))
    cb = jnp.einsum('bctgn,bcsgn->bctsg', Cc, Bc)
    y_diag = jnp.einsum('bctsg,bctsgr,bcsgrp->bctgrp', cb, L, xdt)
    decay_states = jnp.exp(a_cum[:, :, -1:] - a_cum)
    states = jnp.einsum('bcsgn,bcsgr,bcsgrp->bcgrpn', Bc, decay_states, xdt)
    chunk_decay = jnp.exp(a_cum[:, :, -1])

    def step(h, inp):
        s_c, d_c = inp
        return h * d_c[..., None, None] + s_c, h

    h0 = jnp.zeros((b, SSD_GROUPS, R, SSD_HEAD_DIM, SSD_STATE), jnp.float32)
    _, prev = lax.scan(step, h0, (jnp.moveaxis(states, 1, 0), jnp.moveaxis(chunk_decay, 1, 0)))
    prev = jnp.moveaxis(prev, 0, 1)
    y_off = jnp.einsum('bctgn,bcgrpn,bctgr->bctgrp', Cc, prev, jnp.exp(a_cum))
    return (y_diag + y_off).reshape(b, l, SSD_HEADS, SSD_HEAD_DIM)

def ssd_group(z, xbc, dt_raw, conv_w, conv_b, dt_bias, a_log, d_skip, ssd_norm_w):
    b, l = z.shape[:2]
    xbc = lax.conv_general_dilated(
        xbc, conv_w[:, None, :], window_strides=(1,), padding=[(SSD_CONV - 1, 0)],
        dimension_numbers=('NWC', 'WIO', 'NWC'), feature_group_count=SSD_CONV_DIM) + conv_b
    xbc = jax.nn.silu(xbc)
    xs, Bm, Cm = jnp.split(xbc, [SSD_INNER, SSD_INNER + SSD_GROUPS * SSD_STATE], axis=-1)
    xs = xs.reshape(b, l, SSD_HEADS, SSD_HEAD_DIM)
    Bm = Bm.reshape(b, l, SSD_GROUPS, SSD_STATE)
    Cm = Cm.reshape(b, l, SSD_GROUPS, SSD_STATE)
    dt = jax.nn.softplus(dt_raw.astype(jnp.float32) + dt_bias.astype(jnp.float32))
    A = -jnp.exp(a_log.astype(jnp.float32))
    y = ssd_chunked(xs, dt, A, Bm, Cm)
    y = y + d_skip.astype(jnp.float32)[:, None] * xs.astype(jnp.float32)
    y = y.reshape(b, l, SSD_INNER) * jax.nn.silu(z.astype(jnp.float32))
    y = y.reshape(b, l, SSD_GROUPS, SSD_INNER // SSD_GROUPS)
    y = y * lax.rsqrt(jnp.mean(y * y, axis=-1, keepdims=True) + EPS)
    y = y.reshape(b, l, SSD_INNER) * ssd_norm_w.astype(jnp.float32)
    return y.astype(z.dtype)

def fox_group(q, k, v, f_raw, fox_f_bias):
    b, l = q.shape[:2]
    q = q.reshape(b, l, FOX_HEADS, FOX_HEAD_DIM) * (FOX_HEAD_DIM ** -0.5)
    k = k.reshape(b, l, FOX_HEADS, FOX_HEAD_DIM)
    v = v.reshape(b, l, FOX_HEADS, FOX_HEAD_DIM)
    log_f = jax.nn.log_sigmoid(f_raw.astype(jnp.float32) + fox_f_bias.astype(jnp.float32))
    cum = jnp.transpose(jnp.cumsum(log_f, axis=1), (0, 2, 1))
    outs = []
    for i in range(l // Q_BLOCK):
        qs, qe = i * Q_BLOCK, (i + 1) * Q_BLOCK
        s = jnp.einsum('bqhd,bkhd->bhqk', q[:, qs:qe], k[:, :qe]).astype(jnp.float32)
        s = s + cum[:, :, qs:qe, None] - cum[:, :, None, :qe]
        mask = (qs + jnp.arange(Q_BLOCK))[:, None] >= jnp.arange(qe)[None, :]
        p = jax.nn.softmax(jnp.where(mask, s, -jnp.inf), axis=-1)
        outs.append(jnp.einsum('bhqk,bkhd->bqhd', p.astype(v.dtype), v[:, :qe]))
    return jnp.concatenate(outs, axis=1).reshape(b, l, FOX_INNER)

def peer(h, wq, k1, k2, u, v):
    b, l, d = h.shape
    t = h.reshape(-1, d)
    T = t.shape[0]
    q = (t @ wq).reshape(T, PEER_HEADS, 2, PEER_KEY_DIM // 2)
    s1 = jnp.einsum('thd,hnd->thn', q[:, :, 0], k1).astype(jnp.float32)
    s2 = jnp.einsum('thd,hnd->thn', q[:, :, 1], k2).astype(jnp.float32)
    v1, i1 = lax.top_k(s1, PEER_TOPK)
    v2, i2 = lax.top_k(s2, PEER_TOPK)
    cand = (v1[..., :, None] + v2[..., None, :]).reshape(T, PEER_HEADS, PEER_TOPK * PEER_TOPK)
    cand_idx = (i1[..., :, None] * PEER_N_KEYS + i2[..., None, :]).reshape(T, PEER_HEADS, PEER_TOPK * PEER_TOPK)
    sc, pos = lax.top_k(cand, PEER_TOPK)
    idx = jnp.take_along_axis(cand_idx, pos, axis=-1)
    g = jax.nn.softmax(sc, axis=-1).astype(t.dtype)

    def block(args):
        tb, ib, gb = args
        act = jax.nn.gelu(jnp.einsum('thkd,td->thk', u[ib], tb), approximate=False)
        return jnp.einsum('thk,thkd->td', gb * act, v[ib])

    nb = T // PEER_TOKEN_BLOCK
    out = lax.map(block, (t.reshape(nb, PEER_TOKEN_BLOCK, d),
                          idx.reshape(nb, PEER_TOKEN_BLOCK, PEER_HEADS, PEER_TOPK),
                          g.reshape(nb, PEER_TOKEN_BLOCK, PEER_HEADS, PEER_TOPK)))
    return out.reshape(b, l, d)

def first_inputs(seed: int = 0) -> dict:
    key = jax.random.key(seed)
    ks = jax.random.split(key, 20)
    f32 = jnp.float32
    nrm = lambda k, shape: jax.random.normal(k, shape, f32)
    dt0 = jnp.exp(jax.random.uniform(ks[5], (SSD_HEADS,), f32, np.log(1e-3), np.log(1e-1)))
    return {
        "x": nrm(ks[0], (BATCH, SEQ, D_MODEL)),
        "ln1_w": 1.0 + 0.02 * nrm(ks[1], (D_MODEL,)),
        "w_in": nrm(ks[2], (D_MODEL, IN_PROJ_DIM)) * D_MODEL ** -0.5,
        "conv_w": nrm(ks[3], (SSD_CONV, SSD_CONV_DIM)) * SSD_CONV ** -0.5,
        "conv_b": 0.02 * nrm(ks[4], (SSD_CONV_DIM,)),
        "dt_bias": dt0 + jnp.log(-jnp.expm1(-dt0)),
        "a_log": jnp.log(jax.random.uniform(ks[6], (SSD_HEADS,), f32, 1.0, 16.0)),
        "d_skip": 1.0 + 0.1 * nrm(ks[7], (SSD_HEADS,)),
        "ssd_norm_w": 1.0 + 0.02 * nrm(ks[8], (SSD_INNER,)),
        "fox_f_bias": jnp.linspace(1.0, 6.0, FOX_HEADS, dtype=f32) + 0.1 * nrm(ks[9], (FOX_HEADS,)),
        "w_out": nrm(ks[10], (MIX_WIDTH, D_MODEL)) * MIX_WIDTH ** -0.5,
        "ln2_w": 1.0 + 0.02 * nrm(ks[11], (D_MODEL,)),
        "peer_wq": nrm(ks[12], (D_MODEL, PEER_HEADS * PEER_KEY_DIM)) * D_MODEL ** -0.5,
        "peer_k1": nrm(ks[13], (PEER_HEADS, PEER_N_KEYS, PEER_KEY_DIM // 2)) * (PEER_KEY_DIM // 2) ** -0.5,
        "peer_k2": nrm(ks[14], (PEER_HEADS, PEER_N_KEYS, PEER_KEY_DIM // 2)) * (PEER_KEY_DIM // 2) ** -0.5,
        "peer_u": nrm(ks[15], (PEER_N_EXPERTS, D_MODEL)) * D_MODEL ** -0.5,
        "peer_v": nrm(ks[16], (PEER_N_EXPERTS, D_MODEL)) * PEER_HEADS ** -0.5,
        "lnf_w": 1.0 + 0.02 * nrm(ks[17], (D_MODEL,)),
    }

def first_block(x, ln1_w, w_in, conv_w, conv_b, dt_bias, a_log, d_skip, ssd_norm_w,
              fox_f_bias, w_out, ln2_w, peer_wq, peer_k1, peer_k2, peer_u, peer_v, lnf_w):
    split_at = [int(s) for s in np.cumsum(IN_SPLITS)[:-1]]
    for _ in range(DEPTH):
        h = rmsnorm(x, ln1_w)
        proj = h @ w_in
        z, xbc, dt_raw, q, k, v, f_raw = jnp.split(proj, split_at, axis=-1)
        y_ssd = ssd_group(z, xbc, dt_raw, conv_w, conv_b, dt_bias, a_log, d_skip, ssd_norm_w)
        y_fox = fox_group(q, k, v, f_raw, fox_f_bias)
        x = x + jnp.concatenate([y_ssd, y_fox], axis=-1) @ w_out
        x = x + peer(rmsnorm(x, ln2_w), peer_wq, peer_k1, peer_k2, peer_u, peer_v)
    return rmsnorm(x, lnf_w)


N_MEM = 256
HEAD_DIM = 128
N_ATTN_HEADS = 8
ATTN_WIDTH = N_ATTN_HEADS * HEAD_DIM
CONV_CH = D_MODEL // 2
MIX_WIDTH_2 = ATTN_WIDTH + CONV_CH
IN_WIDTH = 3 * ATTN_WIDTH + 2 * CONV_CH
CONV_K = 31
MOBA_BLOCK = 256
MOBA_TOPK = 3
Q_CHUNK = 64
N_BUCKETS = 32
MAX_DISTANCE = 2048
N_CROSS_HEADS = 4
CROSS_HEAD_DIM = 128
CROSS_WIDTH = N_CROSS_HEADS * CROSS_HEAD_DIM
D_FF = 4 * D_MODEL


def rmsnorm_2(x, g):
    xf = x.astype(jnp.float32)
    y = xf * lax.rsqrt(jnp.mean(xf * xf, axis=-1, keepdims=True) + EPS)
    return (y * g.astype(jnp.float32)).astype(x.dtype)

def layernorm(x, g, b):
    xf = x.astype(jnp.float32)
    mu = jnp.mean(xf, axis=-1, keepdims=True)
    xc = xf - mu
    var = jnp.mean(xc * xc, axis=-1, keepdims=True)
    y = xc * lax.rsqrt(var + EPS) * g.astype(jnp.float32) + b.astype(jnp.float32)
    return y.astype(x.dtype)

def t5_bucket(dist):
    max_exact = N_BUCKETS // 2
    nf = jnp.maximum(dist, max_exact).astype(jnp.float32)
    large = max_exact + (jnp.log(nf / max_exact) / math.log(MAX_DISTANCE / max_exact)
                         * (N_BUCKETS - max_exact)).astype(jnp.int32)
    large = jnp.minimum(large, N_BUCKETS - 1)
    return jnp.where(dist < max_exact, dist, large)

def moba_attention(q, k, v, dist_bias):
    B, H, S, Dh = q.shape
    nb = -(-S // MOBA_BLOCK)
    pad = nb * MOBA_BLOCK - S
    kp = jnp.pad(k, ((0, 0), (0, 0), (0, pad), (0, 0)))
    vp = jnp.pad(v, ((0, 0), (0, 0), (0, pad), (0, 0)))
    kb = kp.reshape(B, H, nb, MOBA_BLOCK, Dh)
    vb = vp.reshape(B, H, nb, MOBA_BLOCK, Dh)
    kbar = jnp.mean(kb.astype(jnp.float32), axis=3)
    k_eff = min(MOBA_TOPK, nb)
    scale = HEAD_DIM ** -0.5
    bi = jnp.arange(B)[:, None, None, None]
    hi = jnp.arange(H)[None, :, None, None]
    blk_offs = jnp.arange(MOBA_BLOCK)

    def chunk(ci):
        start = ci * Q_CHUNK
        qc = lax.dynamic_slice_in_dim(q, start, Q_CHUNK, axis=2)
        own = start // MOBA_BLOCK
        qpos = start + jnp.arange(Q_CHUNK)
        gate = jnp.einsum('bhqd,bhnd->bhqn', qc.astype(jnp.float32), kbar)
        gate = jnp.where(jnp.arange(nb) < own, gate, -jnp.inf)
        _, idx = lax.top_k(gate, k_eff)
        valid = jnp.arange(k_eff) < own
        ks = kb[bi, hi, idx]
        vs = vb[bi, hi, idx]
        kpos = idx[..., None] * MOBA_BLOCK + blk_offs
        d_sel = jnp.maximum(qpos[:, None, None] - kpos, 0)
        s_sel = (jnp.einsum('bhqd,bhqjkd->bhqjk', qc, ks).astype(jnp.float32) * scale
                 + dist_bias[hi[..., None], d_sel])
        s_sel = jnp.where(valid[:, None], s_sel, -jnp.inf)
        s_sel = s_sel.reshape(B, H, Q_CHUNK, k_eff * MOBA_BLOCK)
        ko = lax.dynamic_slice_in_dim(kp, own * MOBA_BLOCK, MOBA_BLOCK, axis=2)
        vo = lax.dynamic_slice_in_dim(vp, own * MOBA_BLOCK, MOBA_BLOCK, axis=2)
        d_own = qpos[:, None] - (own * MOBA_BLOCK + blk_offs)[None, :]
        s_own = (jnp.einsum('bhqd,bhkd->bhqk', qc, ko).astype(jnp.float32) * scale
                 + dist_bias[:, jnp.maximum(d_own, 0)][None])
        s_own = jnp.where(d_own >= 0, s_own, -jnp.inf)
        p = jax.nn.softmax(jnp.concatenate([s_sel, s_own], axis=-1), axis=-1)
        p_sel = p[..., :k_eff * MOBA_BLOCK].reshape(B, H, Q_CHUNK, k_eff, MOBA_BLOCK)
        p_own = p[..., k_eff * MOBA_BLOCK:]
        out = (jnp.einsum('bhqjk,bhqjkd->bhqd', p_sel.astype(vs.dtype), vs)
               + jnp.einsum('bhqk,bhkd->bhqd', p_own.astype(vo.dtype), vo))
        return out.astype(q.dtype)

    outs = lax.map(chunk, jnp.arange(S // Q_CHUNK))
    return outs.transpose(1, 0, 3, 2, 4).reshape(B, S, H * Dh)

def conformer_conv(u, conv_w, conv_b, ln_g, ln_b):
    val, gt = jnp.split(u, 2, axis=-1)
    h = val * jax.nn.sigmoid(gt)
    h = lax.conv_general_dilated(h, conv_w[:, None, :].astype(h.dtype), window_strides=(1,),
                                 padding=[(CONV_K - 1, 0)],
                                 dimension_numbers=('NWC', 'WIO', 'NWC'),
                                 feature_group_count=CONV_CH) + conv_b
    h = layernorm(h, ln_g, ln_b)
    return jax.nn.silu(h)

def cross_attention(n, m, wq, wk, wv, wo):
    B, S, _ = n.shape
    M = m.shape[1]
    q = (n @ wq).reshape(B, S, N_CROSS_HEADS, CROSS_HEAD_DIM)
    k = (m @ wk).reshape(B, M, N_CROSS_HEADS, CROSS_HEAD_DIM)
    v = (m @ wv).reshape(B, M, N_CROSS_HEADS, CROSS_HEAD_DIM)
    s = jnp.einsum('bshd,bmhd->bhsm', q, k).astype(jnp.float32) * CROSS_HEAD_DIM ** -0.5
    p = jax.nn.softmax(s, axis=-1).astype(v.dtype)
    o = jnp.einsum('bhsm,bmhd->bshd', p, v).reshape(B, S, CROSS_WIDTH)
    return o @ wo

def second_inputs(seed: int = 0) -> dict:
    key = jax.random.key(seed)
    ks = jax.random.split(key, 24)
    f32 = jnp.float32
    nrm = lambda k, shape, s: jax.random.normal(k, shape, f32) * s
    gain = lambda k, shape: 1.0 + 0.02 * jax.random.normal(k, shape, f32)
    L = DEPTH
    return {
        "x": jax.random.normal(ks[0], (BATCH, SEQ, D_MODEL), f32),
        "mem": jax.random.normal(ks[1], (BATCH, N_MEM, D_MODEL), f32),
        "g_mix": gain(ks[2], (L, D_MODEL)),
        "w_in": nrm(ks[3], (L, D_MODEL, IN_WIDTH), D_MODEL ** -0.5),
        "conv_w": nrm(ks[4], (L, CONV_K, CONV_CH), CONV_K ** -0.5),
        "conv_b": nrm(ks[5], (L, CONV_CH), 0.02),
        "conv_ln_g": gain(ks[6], (L, CONV_CH)),
        "conv_ln_b": nrm(ks[7], (L, CONV_CH), 0.02),
        "w_out": nrm(ks[8], (L, MIX_WIDTH_2, D_MODEL), MIX_WIDTH_2 ** -0.5),
        "rel_bias": nrm(ks[9], (N_BUCKETS, N_ATTN_HEADS), 0.5),
        "g_cross": gain(ks[10], (L, D_MODEL)),
        "g_mem": gain(ks[11], (L, D_MODEL)),
        "wq_c": nrm(ks[12], (L, D_MODEL, CROSS_WIDTH), D_MODEL ** -0.5),
        "wk_c": nrm(ks[13], (L, D_MODEL, CROSS_WIDTH), D_MODEL ** -0.5),
        "wv_c": nrm(ks[14], (L, D_MODEL, CROSS_WIDTH), D_MODEL ** -0.5),
        "wo_c": nrm(ks[15], (L, CROSS_WIDTH, D_MODEL), CROSS_WIDTH ** -0.5),
        "g_mlp": gain(ks[16], (L, D_MODEL)),
        "w1": nrm(ks[17], (L, D_MODEL, D_FF), D_MODEL ** -0.5),
        "w2": nrm(ks[18], (L, D_FF, D_MODEL), D_FF ** -0.5),
        "g_final": gain(ks[19], (D_MODEL,)),
    }

def second_block(x, mem, g_mix, w_in, conv_w, conv_b, conv_ln_g, conv_ln_b, w_out, rel_bias,
              g_cross, g_mem, wq_c, wk_c, wv_c, wo_c, g_mlp, w1, w2, g_final):
    B, S, _ = x.shape
    dist_bias = rel_bias[t5_bucket(jnp.arange(S))].T.astype(jnp.float32)

    def to_heads(t):
        return t.reshape(B, S, N_ATTN_HEADS, HEAD_DIM).transpose(0, 2, 1, 3)

    h = x
    for l in range(DEPTH):
        n = rmsnorm_2(h, g_mix[l])
        z = n @ w_in[l]
        q, k, v, u = jnp.split(z, [ATTN_WIDTH, 2 * ATTN_WIDTH, 3 * ATTN_WIDTH], axis=-1)
        a = moba_attention(to_heads(q), to_heads(k), to_heads(v), dist_bias)
        c = conformer_conv(u, conv_w[l], conv_b[l], conv_ln_g[l], conv_ln_b[l])
        h = h + jnp.concatenate([a, c], axis=-1) @ w_out[l]
        h = h + cross_attention(rmsnorm_2(h, g_cross[l]), rmsnorm_2(mem, g_mem[l]),
                                wq_c[l], wk_c[l], wv_c[l], wo_c[l])
        nm = rmsnorm_2(h, g_mlp[l])
        h = h + jnp.square(jax.nn.relu(nm @ w1[l])) @ w2[l]
    return rmsnorm_2(h, g_final)


def setup_inputs(seed=0):
    out = dict(first_inputs(seed))
    for name, value in second_inputs(seed + 1).items():
        if name != "x":
            out[name + "_2"] = value
    return out


def reference(
    x, ln1_w, w_in, conv_w, conv_b, dt_bias, a_log, d_skip, ssd_norm_w, fox_f_bias, w_out,
    ln2_w, peer_wq, peer_k1, peer_k2, peer_u, peer_v, lnf_w, mem_2, g_mix_2, w_in_2, conv_w_2,
    conv_b_2, conv_ln_g_2, conv_ln_b_2, w_out_2, rel_bias_2, g_cross_2, g_mem_2, wq_c_2, wk_c_2,
    wv_c_2, wo_c_2, g_mlp_2, w1_2, w2_2, g_final_2,
):
    x = first_block(
        x, ln1_w, w_in, conv_w, conv_b, dt_bias, a_log, d_skip, ssd_norm_w, fox_f_bias, w_out,
        ln2_w, peer_wq, peer_k1, peer_k2, peer_u, peer_v, lnf_w,
    )
    return second_block(
        x, mem_2, g_mix_2, w_in_2, conv_w_2, conv_b_2, conv_ln_g_2, conv_ln_b_2, w_out_2,
        rel_bias_2, g_cross_2, g_mem_2, wq_c_2, wk_c_2, wv_c_2, wo_c_2, g_mlp_2, w1_2, w2_2,
        g_final_2,
    )


_drawn_inputs = setup_inputs


def setup_inputs(seed=0):
    import zlib

    import numpy as np

    out = dict(_drawn_inputs(seed))
    spreads = {}
    factors = {'g_mix_2': 5.426,
     'conv_b_2': 3.152,
     'conv_ln_g_2': 5.822,
     'conv_ln_b_2': 6.466,
     'g_cross_2': 8.0,
     'g_mem_2': 8.0,
     'g_mlp_2': 9.465,
     'g_final_2': 7.911}
    for name, (base, spread) in spreads.items():
        noise = np.random.default_rng([zlib.crc32(name.encode()), seed]).standard_normal(out[name].shape)
        drawn = base * np.exp(spread * noise) if base else spread * noise
        out[name] = __import__('jax').numpy.asarray(drawn.astype(out[name].dtype))
    for name, factor in factors.items():
        out[name] = (out[name] * factor).astype(out[name].dtype)
    return out
```

```python
import numpy as np
import concourse.bass as bass
from concourse import mybir
from concourse.alu_op_type import AluOpType as ALU
from contextlib import ExitStack

F32 = mybir.dt.float32
F32R = mybir.dt.float32r
U32 = mybir.dt.uint32
ACT = mybir.ActivationFunctionType
AX = mybir.AxisListType

P = 128
D = 2048
T = 256
TT = T // P
KT = D // P
UNIT = 2048
EPS = 1e-6
RAW = 4
SPLIT = 2
NEG = -3.0e38

SSD_INNER, SSD_HEADS, SSD_CONV, XBC_TILES, Z_TILES = 1024, 16, 4, 12, 8
FOX_HEADS = 16
PEER_HEADS, PEER_KEYS, TOPK = 8, 128, 16
PICKS = PEER_HEADS * TOPK
ATTN_HEADS, CONV_TILES, CONV_K, CROSS_HEADS = 8, 8, 31, 4
BUCKETS, REL = 32, 2 * T - 1
FF_ROUNDS = 4

STREAM = [("in1", "F", 36), ("v1", "R", 8), ("out1", "R", 16), ("wq", "F", 16),
          ("in2", "F", 32), ("v2", "R", 8), ("out2", "R", 16),
          ("ck", "F", 4), ("cv", "C", 4), ("cq", "F", 4), ("co", "O", 4)]
for _r in range(FF_ROUNDS):
    STREAM += [(f"up{_r}", "F", 16), (f"down{_r}", "R", 16)]
UNIT0, ROUND0 = {}, {}
_u = _g = 0
for _name, _kind, _n in STREAM:
    UNIT0[_name], ROUND0[_name] = _u, _g
    _u += _n
    _g += {"F": _n // 4, "R": _n // 8, "C": 1, "O": 2}[_kind]
UNITS = _u

COLS = {}
_c = 0
for _name, _n in [("ln1", KT), ("gmix", KT), ("gcross", KT), ("gmem", KT), ("gmlp", KT),
                  ("cw1", XBC_TILES * SSD_CONV), ("cb1", XBC_TILES), ("nw1", Z_TILES), ("dskip", Z_TILES),
                  ("cw2", CONV_K * CONV_TILES), ("cb2", CONV_TILES), ("lg2", CONV_TILES), ("lb2", CONV_TILES)]:
    COLS[_name] = (_c, _c + _n)
    _c += _n
NCOLS = _c
CONSTS = {}
_c = 0
for _name, _n in [("ident", P), ("tri", P), ("ones", P), ("ntri", P), ("gt", P), ("flip", P),
                  ("mask", 2 * P), ("iota", TOPK)]:
    CONSTS[_name] = (_c, _c + _n)
    _c += _n
NCONST = _c


class Steps:

    def __init__(self, eng, sem):
        self.eng, self.sem, self.n, self.off = eng, sem, 0, None

    def did(self, inst):
        inst.then_inc(self.sem, 1)
        self.n += 1

    def wait(self):
        self.eng.wait_ge(self.sem, self.n if self.off is None else self.off + self.n)

    def do(self, inst):
        self.did(inst)
        self.wait()

    def enter(self, i, per):
        self.first, self.per = self.n, per
        self.off = i * per

    def leave(self, times):
        assert self.n - self.first == self.per, (self.n - self.first, self.per)
        self.n = self.first + self.per * times
        self.off = None


def build(nc, x_in, mem_in, stream, cols_in, consts_in, rows_in, wide_in, wdtf_in, keys_in,
          rel_in, onehot_in, peer_u, peer_v, out):
    ctx = ExitStack()
    with ctx:
        base = [-(-nc.sbuf_base // 32) * 32]

        def at(name, shape, dt, offset):
            return nc.alloc_sbuf_tensor_at(name, shape, dt, offset=offset)

        def sb(name, shape, dt=F32):
            size = int(np.prod(shape[1:])) * 4
            t = at(name, shape, dt, base[0])
            base[0] += -(-size // 32) * 32
            return t

        def psum(name):
            return ctx.enter_context(nc.psum_tensor(name, [P, 512], F32))

        def sem(name):
            return ctx.enter_context(nc.semaphore(name))

        raw = sb("raw", [P, RAW, UNIT])
        w_hi = [sb(f"w_hi{i}", [P, UNIT], F32R) for i in range(SPLIT)]
        w_lo = [sb(f"w_lo{i}", [P, UNIT], F32R) for i in range(SPLIT)]
        a1_at = base[0]
        a1 = [sb("a1_hi", [P, KT, T], F32R), sb("a1_lo", [P, KT, T], F32R)]
        a2_at = base[0]
        a2 = [sb("a2_hi", [P, KT, T], F32R), sb("a2_lo", [P, KT, T], F32R)]
        x = sb("x", [P, TT, D])
        work_at = base[0]
        WORK = 47104
        base[0] += WORK
        consts = sb("consts", [P, NCONST])
        cols = sb("cols", [P, NCOLS])
        rows = sb("rows", [P, 48])
        wdtf = sb("wdtf", [P, KT, 32])
        tmp = sb("tmp", [P, 4, T])
        sp = sb("sp", [P, 6, TT, 32])
        acum = sb("acum", [P, 4, SSD_HEADS])
        stat = sb("stat", [P, 16])
        amax = sb("amax", [P, 2, TT])
        asum = sb("asum", [P, 2, TT])
        idx_slot = sb("idx_slot", [P, RAW, 1], U32)
        assert base[0] <= nc.sbuf_usable_end, (base[0], nc.sbuf_usable_end)

        def C(name, a=0, b=None):
            lo, hi = CONSTS[name]
            return consts[:, lo + a:(hi if b is None else lo + b)]

        def col(name, i):
            return cols[:, COLS[name][0] + i:COLS[name][0] + i + 1]

        inT = at("inT", [P, 36, T], F32, work_at)
        v1 = at("v1", [P, TT, 1024], F32, work_at + 36864)
        xdt = at("xdt", [P, TT, SSD_INNER], F32, a1_at)
        yT = at("yT", [P, Z_TILES, T], F32, a1_at + 8192)
        cbm = at("cbm", [P, 2, 384], F32, a1_at + 16384)
        seg = at("seg", [P, 2, 384], F32, a1_at + 19456)
        seg_m = at("seg_m", [P, 2, 384], F32, a1_at + 22528)
        pbuf = at("pbuf", [P, 2, 512], F32, a1_at + 16384)
        ptbuf = at("ptbuf", [P, 2, 512], F32, a1_at + 20480)
        brev = at("brev", [P, ATTN_HEADS, T], F32, a1_at + 24576)
        h2 = at("h2", [P, TT, D], F32, work_at)
        wide = at("wide", [P, D], F32, work_at + 16384)
        cand = at("cand", [P, PEER_HEADS, 256], F32, work_at + 24576)
        pk = work_at + 32768
        top_v = at("top_v", [P, 16, TOPK], F32, pk)
        top_i = at("top_i", [P, 16, TOPK], U32, pk + 1024)
        top_f = at("top_f", [P, 16, TOPK], F32, pk + 2048)
        sc = at("sc", [P, PEER_HEADS, TOPK], F32, pk + 3072)
        pos = at("pos", [P, PEER_HEADS, TOPK], U32, pk + 3584)
        posab = at("posab", [P, 2, PICKS], U32, pk + 4096)
        posf = at("posf", [P, 2, PICKS], F32, pk + 5120)
        picked = at("picked", [P, 2, PICKS], F32, pk + 6144)
        idx = at("idx", [P, TT, PICKS], U32, pk + 7168)
        gate = at("gate", [P, TT, PICKS], F32, pk + 8192)
        dots = at("dots", [P, TT, PICKS], F32, pk + 9216)
        gsum = at("gsum", [P, PEER_HEADS], F32, pk + 10240)
        pkt = at("pkt", [P, PICKS], F32, pk + 10272)
        qT = at("qT", [P, 16, T], F32, a2_at)
        keys = at("keys", [P, 16, P], F32, a2_at + 16384)
        s_sb = at("s_sb", [P, 16, P], F32, a2_at + 24576)
        onehot = at("onehot", [P, PICKS, TOPK], F32, work_at + 24576)
        junk = at("junk", [P, D], F32, a2_at)
        rowbuf = at("rowbuf", [P, RAW, D], F32, a1_at)
        inT2 = at("inT2", [P, 32, T], F32, work_at)
        v2 = at("v2", [P, TT, 1024], F32, work_at + 32768)
        padded = at("padded", [P, CONV_TILES, T + CONV_K - 1], F32, a2_at)
        conv = at("conv", [P, CONV_TILES, T], F32, a1_at)
        relT = at("relT", [ATTN_HEADS, REL + 1], F32, a1_at + 16384)
        rel_sb = at("rel_sb", [BUCKETS, ATTN_HEADS], F32, a1_at + 18496)
        oneh_sb = at("oneh_sb", [BUCKETS, REL], F32, a1_at + 20480)
        mem = at("mem", [P, TT, D], F32, work_at)
        ckT = at("ckT", [P, 4, T], F32, work_at + 16384)
        cqT = at("cqT", [P, 4, T], F32, work_at + 20480)
        cv = at("cv", [P, TT, 512], F32, work_at + 24576)
        norm = at("norm", [P, TT, D], F32, work_at)

        bank = [psum(f"bank{i}") for i in range(8)]

        raw_full = [sem(f"raw_full{i}") for i in range(RAW)]
        hi_done = sem("hi_done")
        split_done = sem("split_done")
        mm_done = sem("mm_done")
        bank_free = sem("bank_free")
        act_own = sem("act_own")
        dve_own = sem("dve_own")
        pool_own = sem("pool_own")
        s_x = sem("s_x")
        s_small = sem("s_small")
        s_rel = sem("s_rel")
        sq_done = sem("sq_done")
        rs_done = sem("rs_done")
        normed = sem("normed")
        tr_done = sem("tr_done")
        tmp_full = sem("tmp_full")
        tmp_split = sem("tmp_split")
        a2_ready = sem("a2_ready")
        s_sp = sem("s_sp")
        sp_dve = sem("sp_dve")
        sp_act = sem("sp_act")
        s_cum = sem("s_cum")
        cum_dve = sem("cum_dve")
        conv_done = sem("conv_done")
        xbc_done = sem("xbc_done")
        cb_done = sem("cb_done")
        cbm_done = sem("cbm_done")
        xs_done = sem("xs_done")
        xdt_done = sem("xdt_done")
        arow_done = sem("arow_done")
        seg_done = sem("seg_done")
        exp_done = sem("exp_done")
        m_done = sem("m_done")
        y_done = sem("y_done")
        y_out = sem("y_out")
        ysq_done = sem("ysq_done")
        ms_done = sem("ms_done")
        rv_done = sem("rv_done")
        rt_done = sem("rt_done")
        at_s = sem("at_s")
        at_max = sem("at_max")
        at_exp = sem("at_exp")
        at_p = sem("at_p")
        at_t = sem("at_t")
        at_tc = sem("at_tc")
        at_o = sem("at_o")
        at_oc = sem("at_oc")
        resid = sem("resid")
        s_wide = sem("s_wide")
        s_keys = sem("s_keys")
        sk_done = sem("sk_done")
        sk_copied = sem("sk_copied")
        s_used = sem("s_used")
        sm_dve = sem("sm_dve")
        sm_act = sem("sm_act")
        idx_done = sem("idx_done")
        row_full = [sem(f"row_full{i}") for i in range(RAW)]
        row_used = sem("row_used")
        dots_done = sem("dots_done")
        gelu_done = sem("gelu_done")
        s_relT = sem("s_relT")
        relT_done = sem("relT_done")
        s_relw = sem("s_relw")
        s_brev = sem("s_brev")
        sig_done = sem("sig_done")
        pad_zero = sem("pad_zero")
        cv_done = sem("cv_done")
        mu_done = sem("mu_done")
        cen_done = sem("cen_done")
        csq_done = sem("csq_done")
        var_done = sem("var_done")
        cn_done = sem("cn_done")
        cn_done2 = sem("cn_done2")
        seg_raw = sem("seg_raw")
        idx_taken = sem("idx_taken")
        s_mem = sem("s_mem")
        ck_done = sem("ck_done")
        cq_done = sem("cq_done")
        cv_copied = sem("cv_copied")
        in1_copied = sem("in1_copied")
        in2_copied = sem("in2_copied")
        wq_copied = sem("wq_copied")
        mix_free = sem("mix_free")
        s_out = sem("s_out")
        fin = sem("fin")

        rel_d = nc.dram_tensor("rel_scratch", (ATTN_HEADS, 512), F32, kind="Internal").ap()

        NORMS = ["ln1", "ln2", "lnf", "gmix", "gmem", "gcross", "gmlp", "final"]
        NQ = {n: i for i, n in enumerate(NORMS)}
        BUILDS = ["ln1", "ln2", "gmix", "gmem", "gcross", "gmlp", "up0", "up1", "up2", "up3"]
        BQ = {n: 16 * i for i, n in enumerate(BUILDS)}
        TRQ = {n: 16 * i for i, n in enumerate(BUILDS[:6])}
        HEAD0 = {"fox": 0, "moba": FOX_HEADS, "cross": FOX_HEADS + ATTN_HEADS}
        CAUSAL = dict(segs=[(0, P), (P, 2 * P)], turns=[(0, 0), (P, P), (2 * P, 2 * P)],
                      pv=[(0, 0, 2 * P, 0), (1, 2 * P, P, P)])
        FULL = dict(segs=[(0, 2 * P), (2 * P, 2 * P)], turns=[(0, 0), (2 * P, P), (P, 2 * P), (3 * P, 3 * P)],
                    pv=[(0, 0, 2 * P, 0), (1, 2 * P, 2 * P, 0)])

        block = ctx.enter_context(nc.Block())

        @block.sync
        def _(sp_eng):
            eng = nc.sync
            for tt in range(TT):
                eng.dma_start(x[:, tt, :], x_in[tt * P:(tt + 1) * P, :]).then_inc(s_x, 16)
            for j in range(RAW):
                eng.dma_start(raw[:, j, :], stream[j, :, :]).then_inc(raw_full[j], 16)
            with eng.Fori(1, UNITS // RAW) as g:
                for j in range(RAW):
                    eng.wait_ge(split_done, g * RAW + (j - RAW + 1))
                    eng.dma_start(raw[:, j, :], stream[bass.ds(g * RAW + j, 1), :, :].rearrange("a p n -> p (a n)"))\
                        .then_inc(raw_full[j], 16)
            for tt in range(TT):
                eng.wait_ge(fin, tt + 1)
                eng.dma_start(out[tt * P:(tt + 1) * P, :], x[:, tt, :]).then_inc(s_out, 16)
            eng.wait_ge(s_out, 32)

        @block.gpsimd
        def _(pool):
            eng = nc.gpsimd
            own = Steps(eng, pool_own)
            eng.dma_start(consts[:, :], consts_in).then_inc(s_small, 16)
            eng.dma_start(cols[:, :], cols_in).then_inc(s_small, 16)
            eng.dma_start(rows[:, :], rows_in.partition_broadcast(P)).then_inc(s_small, 16)
            eng.dma_start(wdtf[:, :, :], wdtf_in).then_inc(s_small, 16)
            own.do(eng.memset(stat[:, 12:14], -0.5))

            def rsqrt(name):
                eng.wait_ge(sq_done, TT * (NQ[name] + 1))
                own.do(eng.tensor_scalar(stat[:, 4:6], stat[:, 0:2], 1.0 / D, EPS, ALU.mult, ALU.add))
                eng.tensor_tensor(stat[:, 2:4], stat[:, 4:6], stat[:, 12:14], ALU.pow).then_inc(rs_done, 1)

            rsqrt("ln1")
            eng.wait_ge(mm_done, UNIT0["out1"] + 4)
            eng.dma_start(wide[:, :], wide_in[0:1, :].partition_broadcast(P)).then_inc(s_wide, 16)
            rsqrt("ln2")
            eng.wait_ge(mm_done, UNIT0["wq"])
            eng.dma_start(keys[:, :, :], keys_in).then_inc(s_keys, 16)

            def gather(table, tt, n0):
                with eng.Fori(0, PICKS // RAW) as g:
                    own.enter(g, RAW)
                    for j in range(RAW):
                        eng.wait_ge(row_used, g * RAW + (n0 + j))
                        own.do(eng.tensor_copy(idx_slot[:, j, :], idx[:, tt, bass.ds(g * RAW + j, 1)]))
                        eng.sem_inc(idx_taken, 1)
                        eng.indirect_dma_start(rowbuf[:, j, :], None, table,
                                               bass.IndirectOffsetOnAxis(ap=idx_slot[:, j, :], axis=0))\
                            .then_inc(row_full[j], 16)
                    own.leave(PICKS // RAW)

            for tt in range(TT):
                eng.wait_ge(idx_done, tt + 1)
                if tt == 0:
                    eng.wait_ge(mm_done, UNIT0["in2"])
                gather(peer_u, tt, tt * PICKS)
            eng.wait_ge(normed, 2)
            eng.dma_start(wide[:, :], wide_in[1:2, :].partition_broadcast(P)).then_inc(s_wide, 16)
            for tt in range(TT):
                gather(peer_v, tt, (TT + tt) * PICKS)
            rsqrt("lnf")
            rsqrt("gmix")
            eng.wait_ge(mm_done, UNIT0["in2"] + 1)
            eng.memset(padded[:, :, 0:CONV_K - 1], 0.0).then_inc(pad_zero, 1)
            eng.wait_ge(mm_done, UNIT0["out2"])
            eng.dma_start(rel_sb[:, :], rel_in).then_inc(s_rel, 16)
            eng.dma_start(oneh_sb[:, :], onehot_in).then_inc(s_rel, 16)
            eng.wait_ge(relT_done, 1)
            eng.dma_start(rel_d[:, 0:REL], relT[:, 0:REL]).then_inc(s_relw, 16)
            eng.wait_ge(s_relw, 16)
            hankel = bass.AP(tensor=rel_d.tensor, offset=0, ap=[[1, P], [512, ATTN_HEADS], [1, T]])
            eng.dma_start(brev[:, :, :], hankel).then_inc(s_brev, 16)
            eng.wait_ge(mm_done, UNIT0["out2"] + 1)
            eng.dma_start(mem[:, :, :], mem_in.rearrange("(t p) d -> p t d", p=P)).then_inc(s_mem, 16)
            rsqrt("gmem")
            rsqrt("gcross")
            rsqrt("gmlp")
            eng.wait_ge(mm_done, UNIT0["up0"] + 1)
            eng.dma_start(wide[:, :], wide_in[2:3, :].partition_broadcast(P)).then_inc(s_wide, 16)
            rsqrt("final")

        @block.scalar
        def _(act):
            eng = nc.scalar
            own = Steps(eng, act_own)

            def hi(u, j):
                eng.wait_ge(raw_full[j % RAW], u)
                eng.activation(w_hi[j % SPLIT][:, :], raw[:, j % RAW, :], ACT.Copy).then_inc(hi_done, 1)

            def ahead(u0, j, g=None, per=4):
                u = u0 + j
                k = u + 2
                if g is None:
                    eng.wait_ge(mm_done, u + 1)
                    hi(16 * (k // RAW + 1), k)
                else:
                    eng.wait_ge(mm_done, g * per + (u + 1))
                    hi(g * (16 * per // RAW) + 16 * (k // RAW + 1), k)

            def feature(name, n, first, evict):
                u0 = UNIT0[name] + first
                with eng.Fori(0, n // 4) as g:
                    for j in range(4):
                        ahead(u0, j, g)
                        evict(g, j)

            def row_units(u0, pairs, evict=None, last=False):
                loops = pairs - 1 if last else pairs
                with eng.Fori(0, loops) as g:
                    for j in range(8):
                        ahead(u0, j, g, 8)
                        if evict and j % 4 == 3:
                            evict(g, j // 4)
                if last:
                    for j in range(6):
                        ahead(u0 + 8 * loops, j)

            def squares(name, src):
                for tt in range(TT):
                    eng.activation(junk_act[:, :], src[:, tt, :], ACT.Square, accum_out=stat[:, tt:tt + 1])\
                        .then_inc(sq_done, 1)
                    eng.wait_ge(sq_done, TT * NQ[name] + tt + 1)

            def scaled_tiles(name, weight):
                for kt in range(KT):
                    eng.wait_ge(tr_done, TRQ[name] + kt + 1)
                    n = BQ[name] + kt
                    if n >= 4:
                        eng.wait_ge(tmp_split, n - 3)
                    if weight is None:
                        eng.activation(tmp[:, n % 4, :], bank[4 + kt % 4][:, 0:T], ACT.Copy).then_inc(tmp_full, 1)
                    else:
                        eng.activation(tmp[:, n % 4, :], bank[4 + kt % 4][:, 0:T], ACT.Copy,
                                       scale=col(weight, kt)).then_inc(tmp_full, 1)

            def attention(name, heads, plan, masked):
                width = plan["turns"][-1][1] + P
                for i in range(heads + 1):
                    if i < heads:
                        h = HEAD0[name] + i
                        eng.wait_ge(at_max, h + 1)
                        for q, (c, n) in enumerate(plan["segs"]):
                            src = pbuf[:, h % 2, c:c + n] if masked else bank[4 + h % 2][:, c:c + n]
                            last = eng.activation(pbuf[:, h % 2, c:c + n], src, ACT.Exp, bias=amax[:, h % 2, q:q + 1],
                                                  accum_out=asum[:, h % 2, q:q + 1])
                            last.then_inc(at_exp, 1)
                    if i >= 1:
                        h = HEAD0[name] + i - 1
                        eng.wait_ge(at_t, h + 1)
                        if h >= 2:
                            eng.wait_ge(at_o, h - 1)
                        eng.activation(ptbuf[:, h % 2, 0:width], bank[6][:, 0:width], ACT.Copy).then_inc(at_tc, 1)

            junk_act = at("junk_act", [P, D], F32, work_at + 36864)
            eng.wait_ge(s_x, 32)
            squares("ln1", x)
            eng.sem_inc(bank_free, 4)
            for j in range(SPLIT):
                hi(16, j)
            eng.wait_ge(s_small, 64)
            scaled_tiles("ln1", "ln1")

            eng.wait_ge(sp_dve, 1)
            eng.activation(sp[:, 1, :, :], sp[:, 2, :, :], ACT.Exp).then_inc(sp_act, 1)
            eng.activation(rows[:, 32:48], rows[:, 32:48], ACT.Exp).then_inc(sp_act, 1)
            eng.wait_ge(sp_dve, 2)
            eng.activation(sp[:, 3, :, :], sp[:, 2, :, :], ACT.Ln).then_inc(sp_act, 1)

            def copy_in(first, scale=1.0, func=ACT.Copy):
                def evict(g, j):
                    eng.activation(inT[:, bass.ds(g * 4 + (first + j), 1), :].rearrange("p a t -> p (a t)"),
                                   bank[j][:, 0:T], func, scale=scale).then_inc(bank_free, 1)
                return evict
            feature("in1", 12, 0, copy_in(0))
            feature("in1", 8, 12, copy_in(12, func=ACT.Silu))
            feature("in1", 8, 20, copy_in(20, scale=64 ** -0.5))
            feature("in1", 8, 28, copy_in(28))

            def copy_v(dst):
                def evict(g, c):
                    for tt in range(TT):
                        eng.activation(dst[:, tt, bass.ds(g * 1024 + c * 512, 512)], bank[2 * c + tt][:, :],
                                       ACT.Copy).then_inc(bank_free, 1)
                return evict
            row_units(UNIT0["v1"], 1, copy_v(v1))

            for i in range(XBC_TILES):
                eng.wait_ge(conv_done, i + 1)
                eng.activation(inT[:, i, :], tmp[:, i % 4, :], ACT.Silu, bias=col("cb1", i)).then_inc(xbc_done, 1)
            for h in range(SSD_HEADS):
                eng.wait_ge(seg_done, h + 1)
                eng.activation(seg[:, h % 2, :], seg[:, h % 2, :], ACT.Exp).then_inc(exp_done, 1)
            for i in range(Z_TILES):
                eng.wait_ge(y_out, i + 1)
                if i >= 4:
                    eng.wait_ge(ms_done, i - 3)
                eng.activation(tmp[:, i % 4, :], yT[:, i, :], ACT.Square).then_inc(ysq_done, 1)
            for g in range(2):
                eng.wait_ge(rv_done, g + 1)
                eng.activation(seg[:, g, 0:T], seg[:, g, 0:T], ACT.Sqrt).then_inc(rt_done, 1)

            attention("fox", FOX_HEADS, CAUSAL, True)

            row_units(UNIT0["out1"], 2)

            eng.wait_ge(resid, 2)
            squares("ln2", x)
            scaled_tiles("ln2", None)

            def copy_q(g, j):
                eng.activation(qT[:, bass.ds(g * 4 + j, 1), :].rearrange("p a t -> p (a t)"),
                               bank[j][:, 0:T], ACT.Copy).then_inc(bank_free, 1)
            feature("wq", 16, 0, copy_q)
            for tt in range(TT):
                if tt:
                    eng.wait_ge(s_used, tt)
                for g in range(4):
                    eng.wait_ge(sk_done, 4 * tt + g + 1)
                    eng.activation(s_sb[:, 4 * g:4 * g + 4, :], bank[4 + g][:, :].rearrange("p (a n) -> p a n", a=4),
                                   ACT.Copy).then_inc(sk_copied, 1)
                eng.wait_ge(sm_dve, tt + 1)
                eng.activation(sc[:, :, :], sc[:, :, :], ACT.Exp).then_inc(sm_act, 1)
            for tt in range(TT):
                eng.wait_ge(dots_done, tt + 1)
                eng.activation(dots[:, tt, :], dots[:, tt, :], ACT.Gelu).then_inc(gelu_done, 1)
            eng.wait_ge(resid, 4)
            squares("lnf", x)
            eng.wait_ge(resid, 6)
            squares("gmix", x)
            scaled_tiles("gmix", "gmix")

            def copy2(first, scale=1.0, func=ACT.Copy):
                def evict(g, j):
                    eng.activation(inT2[:, bass.ds(g * 4 + (first + j), 1), :].rearrange("p a t -> p (a t)"),
                                   bank[j][:, 0:T], func, scale=scale).then_inc(bank_free, 1)
                return evict
            feature("in2", 8, 0, copy2(0))
            feature("in2", 8, 8, copy2(8, func=ACT.Sigmoid))
            feature("in2", 8, 16, copy2(16, scale=128 ** -0.5))
            feature("in2", 8, 24, copy2(24))
            row_units(UNIT0["v2"], 1, copy_v(v2))
            eng.wait_ge(s_relT, 1)
            eng.activation(relT[:, 0:REL], bank[5][0:ATTN_HEADS, 0:REL], ACT.Copy).then_inc(relT_done, 1)
            for i in range(CONV_TILES):
                eng.wait_ge(cen_done, i + 1)
                if i >= 4:
                    eng.wait_ge(var_done, i - 3)
                eng.activation(tmp[:, i % 4, :], conv[:, i, :], ACT.Square).then_inc(csq_done, 1)
            eng.wait_ge(rv_done, 3)
            eng.activation(pbuf[:, 0, 0:T], pbuf[:, 0, 0:T], ACT.Sqrt).then_inc(rt_done, 1)
            for i in range(CONV_TILES):
                eng.wait_ge(cn_done, i + 1)
                eng.activation(conv[:, i, :], conv[:, i, :], ACT.Silu, scale=col("lg2", i), bias=col("lb2", i))\
                    .then_inc(cn_done2, 1)
            attention("moba", ATTN_HEADS, CAUSAL, True)
            row_units(UNIT0["out2"], 2)

            eng.wait_ge(s_mem, 16)
            squares("gmem", mem)
            scaled_tiles("gmem", "gmem")

            def copy_small(dst, scale=1.0):
                def evict(g, j):
                    eng.activation(dst[:, bass.ds(g * 4 + j, 1), :].rearrange("p a t -> p (a t)"),
                                   bank[j][:, 0:T], ACT.Copy, scale=scale).then_inc(bank_free, 1)
                return evict
            feature("ck", 4, 0, copy_small(ckT))
            for j in range(4):
                ahead(UNIT0["cv"], j)
            for tt in range(TT):
                eng.activation(cv[:, tt, :], bank[tt][:, :], ACT.Copy).then_inc(bank_free, 2)
            squares("gcross", x)
            scaled_tiles("gcross", "gcross")
            feature("cq", 4, 0, copy_small(cqT, 128 ** -0.5))
            attention("cross", CROSS_HEADS, FULL, False)
            for j in range(4):
                ahead(UNIT0["co"], j)
            eng.wait_ge(resid, 10)
            squares("gmlp", x)
            scaled_tiles("gmlp", "gmlp")

            for r in range(FF_ROUNDS):
                def relu(g, j, n0=BQ[f"up{r}"]):
                    eng.wait_ge(tmp_split, g * 4 + (n0 + j - 3))
                    eng.activation(tmp[:, j, :], bank[j][:, 0:T], ACT.Relu).then_inc(tmp_full, 1)
                    eng.wait_ge(tmp_full, g * 4 + (n0 + j + 1))
                    eng.sem_inc(bank_free, 1)
                feature(f"up{r}", 16, 0, relu)
                row_units(UNIT0[f"down{r}"], 2, last=(r == FF_ROUNDS - 1))
            eng.wait_ge(resid, 12)
            squares("final", x)

        @block.vector
        def _(dve):
            eng = nc.vector
            own = Steps(eng, dve_own)

            def lo(u1, j):
                eng.wait_ge(hi_done, u1)
                eng.tensor_tensor(w_lo[j % SPLIT][:, :], raw[:, j % RAW, :], w_hi[j % SPLIT][:, :].bitcast(F32),
                                  ALU.subtract).then_inc(split_done, 1)

            def ahead(u0, j, g=None, per=4):
                k = u0 + j + 2
                lo(k + 1 if g is None else g * per + (k + 1), k)

            def split(dst, kt, src, sig, ap=None):
                h = dst[0][:, kt, :] if ap is None else dst[0][:, ap, :].rearrange("p a t -> p (a t)")
                l = dst[1][:, kt, :] if ap is None else dst[1][:, ap, :].rearrange("p a t -> p (a t)")
                own.do(eng.tensor_copy(h, src))
                eng.tensor_tensor(l, src, h.bitcast(F32), ALU.subtract).then_inc(sig, 1)

            def from_tmp(name, dst):
                for kt in range(KT):
                    n = BQ[name] + kt
                    eng.wait_ge(tmp_full, n + 1)
                    split(dst, kt, tmp[:, n % 4, :], tmp_split)

            def feature(name, n, first=0, extra=None, steps=0):
                u0 = UNIT0[name] + first
                with eng.Fori(0, n // 4) as g:
                    own.enter(g, steps)
                    for j in range(4):
                        ahead(u0, j, g)
                        if extra:
                            extra(g, j)
                    own.leave(n // 4)

            def add_chunk(c, c2, u_end):
                eng.wait_ge(mm_done, u_end)
                for tt in range(TT):
                    xs = x[:, tt, bass.ds(c, 512)]
                    eng.tensor_tensor(xs, bank[2 * c2 + tt][:, :], xs, ALU.add).then_inc(bank_free, 1)

            def row_units(u0, pairs, add=True, last=False):
                loops = pairs - 1 if last else pairs
                with eng.Fori(0, loops) as g:
                    for j in range(8):
                        ahead(u0, j, g, 8)
                        if add and j % 4 == 3:
                            add_chunk(g * 1024 + (j // 4) * 512, j // 4, g * 8 + (u0 + j + 1))
                if last:
                    for j in range(8):
                        if j < 6:
                            ahead(u0 + 8 * loops, j)
                        if j % 4 == 3:
                            add_chunk(loops * 1024 + (j // 4) * 512, j // 4, u0 + 8 * loops + j + 1)

            resid_n = [0]

            def resid_ready():
                own.do(eng.memset(stat[:, 8:9], 0.0))
                eng.memset(stat[:, 9:10], 0.0).then_inc(resid, 2)

            def normalise(name, src, dst, wide_n=None):
                eng.wait_ge(rs_done, NQ[name] + 1)
                if wide_n:
                    eng.wait_ge(s_wide, 16 * wide_n)
                for tt in range(TT):
                    if wide_n:
                        i = eng.scalar_tensor_tensor(dst[:, tt, :], src[:, tt, :], stat[:, 2 + tt:3 + tt], wide[:, :],
                                                     ALU.mult, ALU.mult)
                    else:
                        i = eng.tensor_scalar(dst[:, tt, :], src[:, tt, :], stat[:, 2 + tt:3 + tt], None, ALU.mult)
                    i.then_inc(fin if name == "final" else (resid if name == "lnf" else normed), 1)

            def attention(name, heads, plan, masked):
                pair = name == "fox"
                for i in range(heads + 2):
                    if i < heads:
                        h = HEAD0[name] + i
                        s = bank[4 + h % 2]
                        eng.wait_ge(at_s, h + 1)
                        for q, (c, n) in enumerate(plan["segs"]):
                            m = amax[:, h % 2, q:q + 1]
                            if masked:
                                own.did(eng.tensor_tensor_reduce(pbuf[:, h % 2, c:c + n], s[:, c:c + n], C("mask", 2 * P - n),
                                                                 1.0, NEG, ALU.add, ALU.max, m))
                            else:
                                own.did(eng.tensor_reduce(m, s[:, c:c + n], AX.X, ALU.max))
                        own.wait()
                        eng.tensor_scalar(amax[:, h % 2, :], amax[:, h % 2, :], -1.0, None, ALU.mult).then_inc(at_max, 1)
                    if 1 <= i <= heads:
                        h = HEAD0[name] + i - 1
                        eng.wait_ge(at_exp, 2 * (h + 1))
                        own.do(eng.reciprocal(asum[:, h % 2, :], asum[:, h % 2, :]))
                        for q, (c, n) in enumerate(plan["segs"]):
                            eng.tensor_scalar(pbuf[:, h % 2, c:c + n], pbuf[:, h % 2, c:c + n], asum[:, h % 2, q:q + 1],
                                              None, ALU.mult).then_inc(at_p, 1)
                    if i >= 2:
                        h = HEAD0[name] + i - 2
                        if pair and h % 2 == 0:
                            continue
                        eng.wait_ge(at_o, h + 1)
                        kt = Z_TILES + (i - 2) // 2 if pair else i - 2
                        split(a2, kt, bank[7][:, 0:T], at_oc)

            for j in range(SPLIT):
                lo(j + 1, j)
            eng.wait_ge(s_x, 32)
            normalise("ln1", x, norm)
            eng.wait_ge(s_small, 64)
            from_tmp("ln1", a1)

            eng.wait_ge(s_sp, 2)
            for tt in range(TT):
                own.did(eng.tensor_tensor(sp[:, 0, tt, :], bank[6 + tt][:, 0:32], rows[:, 0:32], ALU.add))
            own.wait()
            own.do(eng.tensor_scalar(sp[:, 0, :, 16:32], sp[:, 0, :, 16:32], -1.0, None, ALU.mult))
            eng.scalar_tensor_tensor(sp[:, 2, :, :], sp[:, 0, :, :], -1.0, sp[:, 0, :, :], ALU.mult, ALU.min).then_inc(sp_dve, 1)
            eng.wait_ge(sp_act, 1)
            eng.tensor_scalar(sp[:, 2, :, :], sp[:, 1, :, :], 1.0, None, ALU.add).then_inc(sp_dve, 1)
            eng.wait_ge(sp_dve, 2)
            own.do(eng.tensor_scalar(sp[:, 4, :, :], sp[:, 2, :, :], -1.0, None, ALU.add))
            own.did(eng.tensor_scalar(sp[:, 5, :, :], sp[:, 4, :, :], 1e-30, None, ALU.max))
            own.wait()
            own.do(eng.reciprocal(sp[:, 5, :, :], sp[:, 5, :, :]))
            own.do(eng.tensor_tensor(sp[:, 5, :, :], sp[:, 5, :, :], sp[:, 1, :, :], ALU.mult))
            eng.wait_ge(sp_act, 3)
            own.do(eng.tensor_tensor(sp[:, 5, :, :], sp[:, 5, :, :], sp[:, 3, :, :], ALU.mult))
            own.do(eng.scalar_tensor_tensor(sp[:, 4, :, :], sp[:, 4, :, :], 0.0, sp[:, 1, :, :], ALU.is_equal, ALU.mult))
            own.do(eng.tensor_tensor(sp[:, 5, :, :], sp[:, 5, :, :], sp[:, 4, :, :], ALU.add))
            own.do(eng.scalar_tensor_tensor(sp[:, 0, :, :], sp[:, 0, :, :], 0.0, sp[:, 5, :, :], ALU.max, ALU.add))
            own.did(eng.tensor_scalar(sp[:, 1, :, 16:32], sp[:, 0, :, 16:32], -1.0, None, ALU.mult))
            for tt in range(TT):
                own.did(eng.scalar_tensor_tensor(sp[:, 1, tt, 0:16], sp[:, 0, tt, 0:16], -1.0, rows[:, 32:48],
                                                 ALU.mult, ALU.mult))
            own.wait()
            eng.memset(stat[:, 10:11], 0.0).then_inc(sp_dve, 1)

            feature("in1", 36)
            row_units(UNIT0["v1"], 1, add=False)

            eng.wait_ge(s_cum, 1)
            for tt in range(TT):
                own.did(eng.tensor_scalar(acum[:, tt, :], bank[7][:, 16 * tt:16 * tt + 16], -1.0, None, ALU.mult))
            own.wait()
            own.did(eng.tensor_tensor(acum[:, 2, :], bank[7][:, 32:48], acum[:, 0, :], ALU.add))
            own.wait()
            eng.memset(stat[:, 11:12], 0.0).then_inc(cum_dve, 1)

            eng.wait_ge(mm_done, UNIT0["out1"])
            eng.wait_ge(bank_free, 4 * ROUND0["out1"] + 4)
            for i in range(XBC_TILES):
                t = tmp[:, i % 4, :]
                if i >= 4:
                    eng.wait_ge(xbc_done, i - 3)
                w = [cols[:, COLS["cw1"][0] + i * SSD_CONV + k:COLS["cw1"][0] + i * SSD_CONV + k + 1] for k in range(SSD_CONV)]
                own.do(eng.tensor_scalar(t, inT[:, i, :], w[3], None, ALU.mult))
                for s in (1, 2, 3):
                    inst = eng.scalar_tensor_tensor(t[:, s:T], inT[:, i, 0:T - s], w[3 - s], t[:, s:T], ALU.mult, ALU.add)
                    if s < 3:
                        own.do(inst)
                    else:
                        inst.then_inc(conv_done, 1)

            for g in range(2):
                eng.wait_ge(cb_done, g + 1)
                own.did(eng.tensor_tensor(cbm[:, g, 0:T], bank[4 + g][:, 0:T], C("tri", 0, T), ALU.mult))
                own.did(eng.tensor_tensor(cbm[:, g, T:T + P], bank[4 + g][:, T:T + P], C("tri"), ALU.mult))
            own.wait()
            eng.memset(stat[:, 11:12], 0.0).then_inc(cbm_done, 1)
            for n in range(4):
                tt, half = n // 2, n % 2
                eng.wait_ge(xs_done, n + 1)
                eng.tensor_tensor(xdt[:, tt, half * 512:half * 512 + 512].rearrange("p (h c) -> p h c", c=64),
                                  bank[6 + n % 2][:, :].rearrange("p (h c) -> p h c", c=64),
                                  sp[:, 0, tt, half * 8:half * 8 + 8].unsqueeze(2).to_broadcast([P, 8, 64]),
                                  ALU.mult).then_inc(xdt_done, 1)

            def segments(h):
                b, c = bank[4 + (h // 2) % 2], (h % 2) * T
                eng.wait_ge(arow_done, h // 2 + 1)
                if h >= 2:
                    eng.wait_ge(m_done, h - 1)
                for k, (dst, src, bias) in enumerate([(0, 0, 0), (P, P, 2), (T, P, 1)]):
                    eng.tensor_scalar(seg[:, h % 2, dst:dst + P], b[:, c + src:c + src + P], acum[:, bias, h:h + 1], 0.0,
                                      ALU.add, ALU.min).then_inc(seg_raw, 1)
                eng.wait_ge(seg_raw, 3 * (h + 1))
                eng.memset(stat[:, 11:12], 0.0).then_inc(seg_done, 1)

            def decay(h):
                eng.wait_ge(exp_done, h + 1)
                if h >= 2:
                    eng.wait_ge(y_done, h - 1)
                eng.tensor_tensor(seg_m[:, h % 2, :], seg[:, h % 2, :], cbm[:, h // 8, :], ALU.mult).then_inc(m_done, 1)

            def gated(i):
                eng.wait_ge(y_done, 2 * i + 2)
                own.do(eng.scalar_tensor_tensor(yT[:, i, :], inT[:, i, :], col("dskip", i), bank[6 + i % 2][:, 0:T],
                                                ALU.mult, ALU.add))
                eng.tensor_tensor(yT[:, i, :], yT[:, i, :], inT[:, XBC_TILES + i, :], ALU.mult).then_inc(y_out, 1)

            for h in range(SSD_HEADS + 2):
                if h < SSD_HEADS:
                    segments(h)
                if 1 <= h <= SSD_HEADS:
                    decay(h - 1)
                if h >= 3 and h % 2 == 1:
                    gated((h - 3) // 2)
            for g in range(2):
                eng.wait_ge(ms_done, 4 * (g + 1))
                eng.tensor_scalar(seg[:, g, 0:T], bank[4 + g][:, 0:T], 1.0 / 512, EPS, ALU.mult, ALU.add).then_inc(rv_done, 1)
            for g in range(2):
                eng.wait_ge(rt_done, g + 1)
                own.do(eng.reciprocal(seg[:, g, 0:T], seg[:, g, 0:T]))
            for i in range(Z_TILES):
                own.do(eng.scalar_tensor_tensor(yT[:, i, :], yT[:, i, :], col("nw1", i), seg[:, i // 4, 0:T], ALU.mult, ALU.mult))
                split(a2, i, yT[:, i, :], a2_ready)

            attention("fox", FOX_HEADS, CAUSAL, True)

            row_units(UNIT0["out1"], 2)
            resid_ready()

            normalise("ln2", x, h2, 1)
            from_tmp("ln2", a1)
            feature("wq", 16)
            for tt in range(TT):
                eng.wait_ge(sk_copied, 4 * (tt + 1))

                def best(n, src, v, i):
                    for h in range(n):
                        own.did(eng.max(v[:, h, 0:8], src[:, h, :]))
                    own.wait()
                    for h in range(n):
                        own.did(eng.max_index(i[:, h, 0:8], v[:, h, 0:8], src[:, h, :]))
                    own.wait()
                    for h in range(n):
                        own.did(eng.match_replace(src[:, h, :], v[:, h, 0:8], src[:, h, :], NEG))
                    own.wait()
                    for h in range(n):
                        own.did(eng.max(v[:, h, 8:16], src[:, h, :]))
                    own.wait()
                    for h in range(n):
                        own.did(eng.max_index(i[:, h, 8:16], v[:, h, 8:16], src[:, h, :]))
                    own.wait()

                best(16, s_sb, top_v, top_i)
                eng.memset(stat[:, 11:12], 0.0).then_inc(s_used, 1)
                own.did(eng.tensor_copy(top_f[:, :, :], top_i[:, :, :]))
                tv = top_v[:, :, :].rearrange("p (h two) k -> p h two k", two=2)
                tf = top_f[:, :, :].rearrange("p (h two) k -> p h two k", two=2)
                own.did(eng.tensor_tensor(cand[:, :, :].rearrange("p h (a b) -> p h a b", a=TOPK),
                                          tv[:, :, 0, :].unsqueeze(3).to_broadcast([P, PEER_HEADS, TOPK, TOPK]),
                                          tv[:, :, 1, :].unsqueeze(2).to_broadcast([P, PEER_HEADS, TOPK, TOPK]), ALU.add))
                own.wait()
                best(PEER_HEADS, cand, sc, pos)
                own.did(eng.tensor_copy(pkt[:, 0:PEER_HEADS], sc[:, :, 0]))
                own.wait()
                eng.tensor_tensor(sc[:, :, :], sc[:, :, :],
                                  pkt[:, 0:PEER_HEADS].unsqueeze(2).to_broadcast([P, PEER_HEADS, TOPK]),
                                  ALU.subtract).then_inc(sm_dve, 1)
                pf = pos[:, :, :].rearrange("p h k -> p (h k)")
                own.did(eng.tensor_scalar(posab[:, 0, :], pf, 4, None, ALU.logical_shift_right))
                own.did(eng.tensor_scalar(posab[:, 1, :], pf, 15, None, ALU.bitwise_and))
                own.wait()
                own.do(eng.tensor_copy(posf[:, :, :], posab[:, :, :]))
                for half in range(2):
                    own.do(eng.tensor_tensor(onehot[:, :, :], C("iota").unsqueeze(1).to_broadcast([P, PICKS, TOPK]),
                                             posf[:, half, :].unsqueeze(2).to_broadcast([P, PICKS, TOPK]), ALU.is_equal))
                    oh = onehot[:, :, :].rearrange("p (h k) a -> p h k a", h=PEER_HEADS)
                    own.do(eng.tensor_tensor(oh, oh, tf[:, :, half, :].unsqueeze(2).to_broadcast([P, PEER_HEADS, TOPK, TOPK]),
                                             ALU.mult))
                    own.do(eng.tensor_reduce(picked[:, half, :], onehot[:, :, :], AX.X, ALU.add))
                eng.scalar_tensor_tensor(idx[:, tt, :], picked[:, 0, :], float(PEER_KEYS), picked[:, 1, :],
                                         ALU.mult, ALU.add).then_inc(idx_done, 1)
                eng.wait_ge(sm_act, tt + 1)
                own.do(eng.tensor_reduce(gsum[:, :], sc[:, :, :], AX.X, ALU.add))
                own.do(eng.reciprocal(gsum[:, :], gsum[:, :]))
                own.do(eng.tensor_tensor(gate[:, tt, :].rearrange("p (h k) -> p h k", h=PEER_HEADS), sc[:, :, :],
                                         gsum[:, :].unsqueeze(2).to_broadcast([P, PEER_HEADS, TOPK]), ALU.mult))

            per_slot = PICKS // RAW
            for tt in range(TT):
                with eng.Fori(0, per_slot) as g:
                    own.enter(g, RAW)
                    for j in range(RAW):
                        eng.wait_ge(row_full[j], g * 16 + 16 * (tt * per_slot + 1))
                        own.did(eng.scalar_tensor_tensor(junk[:, :], rowbuf[:, j, :], 1.0, h2[:, tt, :], ALU.mult, ALU.mult,
                                                         accum_out=dots[:, tt, bass.ds(g * RAW + j, 1)]))
                        own.wait()
                        eng.sem_inc(row_used, 1)
                    own.leave(per_slot)
                eng.sem_inc(dots_done, 1)
            for tt in range(TT):
                eng.wait_ge(gelu_done, tt + 1)
                own.do(eng.tensor_tensor(gate[:, tt, :], gate[:, tt, :], dots[:, tt, :], ALU.mult))
                with eng.Fori(0, per_slot) as g:
                    own.enter(g, RAW)
                    for j in range(RAW):
                        eng.wait_ge(row_full[j], g * 16 + 16 * ((TT + tt) * per_slot + 1))
                        own.did(eng.scalar_tensor_tensor(x[:, tt, :], rowbuf[:, j, :], gate[:, tt, bass.ds(g * RAW + j, 1)],
                                                         x[:, tt, :], ALU.mult, ALU.add))
                        own.wait()
                        eng.sem_inc(row_used, 1)
                    own.leave(per_slot)
            resid_ready()
            normalise("lnf", x, x, 2)

            eng.wait_ge(resid, 6)
            normalise("gmix", x, norm)
            from_tmp("gmix", a1)
            feature("in2", 32)
            row_units(UNIT0["v2"], 1, add=False)
            eng.wait_ge(pad_zero, 1)
            eng.wait_ge(bank_free, 4 * ROUND0["out2"] + 4)
            for i in range(CONV_TILES):
                own.did(eng.tensor_tensor(padded[:, i, CONV_K - 1:], inT2[:, i, :], inT2[:, CONV_TILES + i, :], ALU.mult))
            own.wait()
            for i in range(CONV_TILES):
                own.did(eng.tensor_scalar(conv[:, i, :], padded[:, i, 0:T], col("cw2", i), col("cb2", i), ALU.mult, ALU.add))
            own.wait()
            with eng.Fori(1, CONV_K) as k:
                own.enter(k - 1, CONV_TILES)
                for i in range(CONV_TILES):
                    if i == 0:
                        own.wait()
                    own.did(eng.scalar_tensor_tensor(
                        conv[:, i, :], padded[:, i, bass.ds(k, T)],
                        cols[:, bass.ds(k * CONV_TILES + (COLS["cw2"][0] + i), 1)], conv[:, i, :], ALU.mult, ALU.add))
                own.leave(CONV_K - 1)
            own.wait()
            eng.sem_inc(cv_done, 1)
            eng.wait_ge(mu_done, 1)
            eng.wait_ge(s_brev, 16)
            own.do(eng.tensor_scalar(pbuf[:, 1, 0:T], bank[4][:, 0:T], 1.0 / 1024, None, ALU.mult))
            for i in range(CONV_TILES):
                eng.tensor_tensor(conv[:, i, :], conv[:, i, :], pbuf[:, 1, 0:T], ALU.subtract).then_inc(cen_done, 1)
            eng.wait_ge(var_done, CONV_TILES)
            eng.tensor_scalar(pbuf[:, 0, 0:T], bank[4][:, 0:T], 1.0 / 1024, EPS, ALU.mult, ALU.add).then_inc(rv_done, 1)
            eng.wait_ge(rt_done, 3)
            own.do(eng.reciprocal(pbuf[:, 0, 0:T], pbuf[:, 0, 0:T]))
            for i in range(CONV_TILES):
                eng.tensor_tensor(conv[:, i, :], conv[:, i, :], pbuf[:, 0, 0:T], ALU.mult).then_inc(cn_done, 1)
            for i in range(CONV_TILES):
                eng.wait_ge(cn_done2, i + 1)
                split(a2, ATTN_HEADS + i, conv[:, i, :], a2_ready)
            attention("moba", ATTN_HEADS, CAUSAL, True)
            row_units(UNIT0["out2"], 2)
            resid_ready()

            normalise("gmem", mem, norm)
            from_tmp("gmem", a1)
            feature("ck", 4)
            for j in range(4):
                ahead(UNIT0["cv"], j)
            normalise("gcross", x, norm)
            from_tmp("gcross", a1)
            feature("cq", 4)
            attention("cross", CROSS_HEADS, FULL, False)
            for j in range(4):
                ahead(UNIT0["co"], j)
                add_chunk(j * 512, j % 2, UNIT0["co"] + j + 1)
            resid_ready()

            normalise("gmlp", x, norm)
            from_tmp("gmlp", a1)
            for r in range(FF_ROUNDS):
                def square(g, j, n0=BQ[f"up{r}"]):
                    eng.wait_ge(tmp_full, g * 4 + (n0 + j + 1))
                    own.do(eng.tensor_tensor(tmp[:, j, :], tmp[:, j, :], tmp[:, j, :], ALU.mult))
                    split(a2, None, tmp[:, j, :], tmp_split, ap=bass.ds(g * 4 + j, 1))
                feature(f"up{r}", 16, 0, square, 8)
                row_units(UNIT0[f"down{r}"], 2, last=(r == FF_ROUNDS - 1))
            resid_ready()
            normalise("final", x, x, 3)

        @block.tensor
        def _(pe):
            eng = nc.tensor
            mm = nc.tensor.matmul

            def feature(name, n, act_t, first=0, ready=None):
                u0, r0 = UNIT0[name] + first, ROUND0[name] + first // 4
                with eng.Fori(0, n // 4) as g:
                    for j in range(4):
                        eng.wait_ge(split_done, g * 4 + (u0 + j + 1))
                        eng.wait_ge(bank_free, g * 4 + (4 * r0 + j + 1))
                        hi, lo = w_hi[j % SPLIT], w_lo[j % SPLIT]
                        for kt in range(KT):
                            ks = slice(kt * P, kt * P + P)
                            o = bank[j][:, 0:T]
                            mm(o, hi[:, ks], act_t[0][:, kt, :], start=kt == 0, stop=False)
                            mm(o, hi[:, ks], act_t[1][:, kt, :], start=False, stop=False)
                            last = mm(o, lo[:, ks], act_t[0][:, kt, :], start=False, stop=kt == KT - 1)
                        last.then_inc(mm_done, 1)

            def row_unit(j, banks, act_t, k0, first, end):
                hi, lo = w_hi[j % SPLIT], w_lo[j % SPLIT]
                for k in range(4):
                    ns = slice(k * 512, k * 512 + 512)
                    for tt in range(TT):
                        o = banks[tt][:, :]
                        ts = slice(tt * P, tt * P + P)
                        mm(o, act_t[0][:, k0 + k, ts], hi[:, ns], start=first and k == 0, stop=False)
                        mm(o, act_t[0][:, k0 + k, ts], lo[:, ns], start=False, stop=False)
                        last = mm(o, act_t[1][:, k0 + k, ts], hi[:, ns], start=False, stop=end and k == 3)
                last.then_inc(mm_done, 1)

            def row_units(name, pairs, act_t):
                u0, r0 = UNIT0[name], ROUND0[name]
                with eng.Fori(0, pairs) as g:
                    for j in range(8):
                        c = j // 4
                        eng.wait_ge(split_done, g * 8 + (u0 + j + 1))
                        if j % 4 == 0:
                            eng.wait_ge(bank_free, g * 4 + (4 * r0 + 2 * c + 2))
                        row_unit(j, bank[2 * c:2 * c + 2], act_t, 4 * (j % 4), j % 4 == 0, j % 4 == 3)

            def turn(name, src):
                if name != "ln1" :
                    pass
                for kt in range(KT):
                    if kt >= 4:
                        eng.wait_ge(tmp_full, BQ[name] + kt - 3)
                    for tt in range(TT):
                        last = eng.transpose(bank[4 + kt % 4][:, tt * P:tt * P + P], src[:, tt, kt * P:kt * P + P], C("ident"))
                    last.then_inc(tr_done, 1)

            def attention(name, heads, plan, scores, values, d):
                for i in range(heads + 2):
                    if i < heads:
                        h = HEAD0[name] + i
                        if i >= 2:
                            eng.wait_ge(at_exp, 2 * (h - 1))
                        scores(i, bank[4 + h % 2]).then_inc(at_s, 1)
                    if 1 <= i <= heads:
                        h = HEAD0[name] + i - 1
                        eng.wait_ge(at_p, 2 * (h + 1))
                        if h >= 1:
                            eng.wait_ge(at_tc, h)
                        for src, dst in plan["turns"]:
                            last = eng.transpose(bank[6][:, dst:dst + P], pbuf[:, h % 2, src:src + P], C("ident"))
                        last.then_inc(at_t, 1)
                    if i >= 2:
                        h = HEAD0[name] + i - 2
                        eng.wait_ge(at_tc, h + 1)
                        if d == P or h % 2 == 0:
                            done = h // 2 if d == 64 else FOX_HEADS // 2 + (h - FOX_HEADS)
                            if done > 0:
                                eng.wait_ge(at_oc, done)
                        p0 = 64 * (h % 2) if d == 64 else 0
                        for n, (kb, src, w, dst) in enumerate(plan["pv"]):
                            last = mm(bank[7][p0:p0 + d, dst:dst + w], values(i - 2, kb), ptbuf[:, h % 2, src:src + w],
                                      start=n == 0, stop=n == len(plan["pv"]) - 1)
                        last.then_inc(at_o, 1)

            eng.wait_ge(s_small, 64)
            eng.wait_ge(normed, 2)
            turn("ln1", norm)
            eng.wait_ge(tmp_split, 16)
            for tt in range(TT):
                for kt in range(KT):
                    for part in range(2):
                        last = mm(bank[6 + tt][:, 0:32], a1[part][:, kt, tt * P:tt * P + P].bitcast(F32), wdtf[:, kt, :],
                                  start=kt == 0 and part == 0, stop=kt == KT - 1 and part == 1)
                last.then_inc(s_sp, 1)
            feature("in1", 36, a1)
            row_units("v1", 1, a1)

            eng.wait_ge(sp_dve, 3)
            for tt in range(TT):
                mm(bank[7][:, 16 * tt:16 * tt + 16], C("tri"), sp[:, 1, tt, 0:16], start=True, stop=True)
            mm(bank[7][:, 32:48], C("ones"), sp[:, 1, 0, 0:16], start=True, stop=True).then_inc(s_cum, 1)

            eng.wait_ge(xbc_done, XBC_TILES)
            for g in range(2):
                bT, cT = inT[:, 8 + g, :], inT[:, 10 + g, :]
                mm(bank[4 + g][:, 0:T], bT[:, 0:P], cT, start=True, stop=True)
                mm(bank[4 + g][:, T:T + P], bT[:, P:T], cT[:, P:T], start=True, stop=True).then_inc(cb_done, 1)
            eng.wait_ge(cum_dve, 1)
            for n in range(4):
                tt, half = n // 2, n % 2
                if n >= 2:
                    eng.wait_ge(xdt_done, n - 1)
                for i in range(4):
                    last = eng.transpose(bank[6 + n % 2][:, i * P:i * P + P], inT[:, half * 4 + i, tt * P:tt * P + P], C("ident"))
                last.then_inc(xs_done, 1)

            def arow(n):
                if n == 0:
                    eng.wait_ge(cbm_done, 1)
                if n >= 2:
                    eng.wait_ge(seg_done, 2 * n - 2)
                for h in range(2):
                    for tt in range(TT):
                        last = mm(bank[4 + n % 2][:, h * T + tt * P:h * T + tt * P + P],
                                  sp[:, 1, tt, 2 * n + h:2 * n + h + 1].to_broadcast([P, P]), C("tri"), start=True, stop=True)
                last.then_inc(arow_done, 1)

            def ssd_head(h):
                i, p0 = h // 2, 64 * (h % 2)
                if h == 0:
                    eng.wait_ge(xdt_done, 4)
                if h % 2 == 0 and i >= 2:
                    eng.wait_ge(y_out, i - 1)
                eng.wait_ge(m_done, h + 1)
                o = bank[6 + i % 2]
                mm(o[p0:p0 + 64, 0:T], xdt[:, 0, h * 64:h * 64 + 64], seg_m[:, h % 2, 0:T], start=True, stop=False)
                mm(o[p0:p0 + 64, P:T], xdt[:, 1, h * 64:h * 64 + 64], seg_m[:, h % 2, T:T + P], start=False, stop=True)\
                    .then_inc(y_done, 1)

            arow(0)
            for n in range(SSD_HEADS // 2):
                if n + 1 < SSD_HEADS // 2:
                    arow(n + 1)
                ssd_head(2 * n)
                ssd_head(2 * n + 1)
            for i in range(Z_TILES):
                eng.wait_ge(ysq_done, i + 1)
                mm(bank[4 + i // 4][:, 0:T], C("ones"), tmp[:, i % 4, :], start=i % 4 == 0, stop=i % 4 == 3).then_inc(ms_done, 1)

            def fox_scores(i, b):
                t, p0 = i // 2, 64 * (i % 2)
                q, k = inT[p0:p0 + 64, 20 + t, :], inT[p0:p0 + 64, 28 + t, :]
                f = [sp[:, 1, tt, 16 + i:17 + i] for tt in range(TT)]
                mm(b[:, 0:P], q[:, 0:P], k[:, 0:P], start=True, stop=False)
                mm(b[:, 0:P], C("tri"), f[0].to_broadcast([P, P]), start=False, stop=False)
                mm(b[:, 0:P], f[0].to_broadcast([P, P]), C("ntri"), start=False, stop=True)
                mm(b[:, P:3 * P], q[:, P:T], k, start=True, stop=False)
                mm(b[:, P:2 * P], f[0].to_broadcast([P, P]), C("gt"), start=False, stop=False, skip_group_check=True)
                mm(b[:, 2 * P:3 * P], f[1].to_broadcast([P, P]), C("ntri"), start=False, stop=False, skip_group_check=True)
                return mm(b[:, P:3 * P], C("tri"), f[1].to_broadcast([P, T]), start=False, stop=True)

            eng.wait_ge(rv_done, 2)
            eng.wait_ge(a2_ready, Z_TILES)
            attention("fox", FOX_HEADS, CAUSAL, fox_scores, lambda i, kb: v1[:, kb, i * 64:i * 64 + 64], 64)

            eng.wait_ge(at_oc, FOX_HEADS // 2)
            row_units("out1", 2, a2)

            eng.wait_ge(normed, 4)
            turn("ln2", h2)
            eng.wait_ge(tmp_split, BQ["ln2"] + 16)
            feature("wq", 16, a1)
            eng.wait_ge(s_keys, 16)
            eng.wait_ge(bank_free, 4 * ROUND0["in2"] + 4)
            for tt in range(TT):
                for g in range(4):
                    if tt:
                        eng.wait_ge(sk_copied, 4 * (tt - 1) + g + 1)
                    for i in range(4):
                        last = mm(bank[4 + g][:, i * P:i * P + P], qT[:, 4 * g + i, tt * P:tt * P + P], keys[:, 4 * g + i, :],
                                  start=True, stop=True)
                    last.then_inc(sk_done, 1)

            eng.wait_ge(normed, 6)
            turn("gmix", norm)
            eng.wait_ge(tmp_split, BQ["gmix"] + 16)
            feature("in2", 32, a1)
            row_units("v2", 1, a1)
            eng.wait_ge(s_rel, 32)
            mm(bank[5][0:ATTN_HEADS, 0:REL], rel_sb[:, :], oneh_sb[:, :], start=True, stop=True).then_inc(s_relT, 1)
            eng.wait_ge(cv_done, 1)
            for i in range(CONV_TILES):
                last = mm(bank[4][:, 0:T], C("ones"), conv[:, i, :], start=i == 0, stop=i == CONV_TILES - 1)
            last.then_inc(mu_done, 1)
            eng.wait_ge(cen_done, 1)
            for i in range(CONV_TILES):
                eng.wait_ge(csq_done, i + 1)
                mm(bank[4][:, 0:T], C("ones"), tmp[:, i % 4, :], start=i == 0, stop=i == CONV_TILES - 1).then_inc(var_done, 1)

            def moba_scores(i, b):
                q, k = inT2[:, 16 + i, :], inT2[:, 24 + i, :]
                mm(b[:, 0:P], q[:, 0:P], k[:, 0:P], start=True, stop=False)
                mm(b[:, 0:P], C("flip"), brev[:, i, P:T], start=False, stop=True)
                mm(b[:, P:3 * P], q[:, P:T], k, start=True, stop=False)
                return mm(b[:, P:3 * P], C("flip"), brev[:, i, :], start=False, stop=True)

            eng.wait_ge(s_brev, 16)
            eng.wait_ge(rv_done, 3)
            eng.wait_ge(a2_ready, Z_TILES + CONV_TILES)
            attention("moba", ATTN_HEADS, CAUSAL, moba_scores, lambda i, kb: v2[:, kb, i * P:i * P + P], P)
            eng.wait_ge(at_oc, FOX_HEADS // 2 + ATTN_HEADS)
            row_units("out2", 2, a2)

            eng.wait_ge(normed, 8)
            turn("gmem", norm)
            eng.wait_ge(tmp_split, BQ["gmem"] + 16)
            feature("ck", 4, a1)
            u0, r0 = UNIT0["cv"], ROUND0["cv"]
            eng.wait_ge(bank_free, 4 * r0 + 2)
            for j in range(4):
                eng.wait_ge(split_done, u0 + j + 1)
                row_unit(j, bank[0:2], a1, 4 * j, j == 0, j == 3)
            eng.wait_ge(normed, 10)
            turn("gcross", norm)
            eng.wait_ge(tmp_split, BQ["gcross"] + 16)
            feature("cq", 4, a1)

            def cross_scores(i, b):
                mm(b[:, 0:T], cqT[:, i, 0:P], ckT[:, i, :], start=True, stop=True)
                return mm(b[:, T:2 * T], cqT[:, i, P:T], ckT[:, i, :], start=True, stop=True)

            eng.wait_ge(bank_free, 4 * ROUND0["co"] + 4)
            attention("cross", CROSS_HEADS, FULL, cross_scores, lambda i, kb: cv[:, kb, i * P:i * P + P], P)
            eng.wait_ge(at_oc, FOX_HEADS // 2 + ATTN_HEADS + CROSS_HEADS)
            u0, r0 = UNIT0["co"], ROUND0["co"]
            for j in range(4):
                eng.wait_ge(split_done, u0 + j + 1)
                eng.wait_ge(bank_free, 4 * r0 + 2 * j + 2)
                row_unit(j, bank[2 * (j % 2):2 * (j % 2) + 2], a2, 0, True, True)

            eng.wait_ge(normed, 12)
            turn("gmlp", norm)
            eng.wait_ge(tmp_split, BQ["gmlp"] + 16)
            for r in range(FF_ROUNDS):
                feature(f"up{r}", 16, a1)
                eng.wait_ge(tmp_split, BQ[f"up{r}"] + 16)
                row_units(f"down{r}", 2, a2)


def _feature_units(w):
    k, n = w.shape
    return w.reshape(KT, P, n // P, P).transpose(2, 1, 0, 3).reshape(n // P, P, UNIT)


def _row_units(w):
    k, n = w.shape
    return w.reshape(k // 512, 4, P, n // 512, 512).transpose(3, 0, 2, 1, 4).reshape(-1, P, UNIT)


def _cols(v):
    return v.reshape(-1, P).T


def _bucket(dist):
    dist = np.asarray(dist)
    exact = BUCKETS // 2
    nf = np.maximum(dist, exact).astype(np.float32)
    large = exact + (np.log(nf / np.float32(exact)) / np.float32(np.log(2048 / exact)) * np.float32(BUCKETS - exact)).astype(np.int32)
    return np.where(dist < exact, dist, np.minimum(large, BUCKETS - 1))


def _constants():
    p, c = np.arange(P)[:, None], np.arange(P)[None, :]
    tri = (p <= c).astype(np.float32)
    causal = np.where(p >= c, 0.0, NEG).astype(np.float32)
    consts = np.concatenate([
        np.eye(P, dtype=np.float32), tri, np.ones((P, P), np.float32), -tri, 1 - tri,
        (p + c == P - 1).astype(np.float32), np.zeros((P, P), np.float32), causal,
        np.broadcast_to(np.arange(TOPK, dtype=np.float32), (P, TOPK))], axis=1)
    onehot = np.zeros((BUCKETS, REL), np.float32)
    j = np.arange(REL)
    onehot[_bucket(np.maximum(T - 1 - j, 0)), j] = 1.0
    return np.ascontiguousarray(consts), onehot


def kernel(**inputs):
    import concourse.bacc as bacc
    from concourse.bass_utils import run_bass_kernel_spmd as run

    a = {k: np.asarray(v) for k, v in inputs.items()}
    w_in = a["w_in"]
    z, xbc, dt, q, k, v, f = np.split(w_in, np.cumsum([1024, 1536, 16, 1024, 1024, 1024]), axis=1)
    w2 = a["w_in_2"][0]
    q2, k2, v2, val2, gate2 = np.split(w2, [1024, 2048, 3072, 4096], axis=1)
    up, down = a["w1_2"][0], a["w2_2"][0]
    units = [_feature_units(m) for m in (xbc, z, q, k)] + [_row_units(v), _row_units(a["w_out"]), _feature_units(a["peer_wq"])]
    units += [_feature_units(m) for m in (val2, gate2, q2, k2)] + [_row_units(v2), _row_units(a["w_out_2"][0])]
    units += [_feature_units(a["wk_c_2"][0]), _row_units(a["wv_c_2"][0]), _feature_units(a["wq_c_2"][0]), _row_units(a["wo_c_2"][0])]
    for r in range(FF_ROUNDS):
        units += [_feature_units(up[:, r * D:(r + 1) * D]), _row_units(down[r * D:(r + 1) * D])]
    stream = np.concatenate(units, axis=0)
    assert stream.shape[0] == UNITS
    cols = np.concatenate([
        _cols(a["ln1_w"]), _cols(a["g_mix_2"][0]), _cols(a["g_cross_2"][0]), _cols(a["g_mem_2"][0]), _cols(a["g_mlp_2"][0]),
        a["conv_w"].reshape(SSD_CONV, XBC_TILES, P).transpose(2, 1, 0).reshape(P, -1), _cols(a["conv_b"]),
        _cols(a["ssd_norm_w"]), _cols(np.repeat(a["d_skip"], 64)),
        a["conv_w_2"][0].reshape(CONV_K, CONV_TILES, P).transpose(2, 0, 1).reshape(P, -1), _cols(a["conv_b_2"][0]),
        _cols(a["conv_ln_g_2"][0]), _cols(a["conv_ln_b_2"][0])], axis=1)
    consts, onehot = _constants()
    keys = np.stack([a["peer_k1"], a["peer_k2"]], axis=1).reshape(16, PEER_KEYS, P).transpose(2, 0, 1)
    arrays = {
        "x": a["x"].reshape(T, D), "mem": a["mem_2"].reshape(T, D), "stream": stream, "cols": cols, "consts": consts,
        "rows": np.concatenate([a["dt_bias"], a["fox_f_bias"], a["a_log"]])[None, :],
        "wide": np.stack([a["ln2_w"], a["lnf_w"], a["g_final_2"]]),
        "wdtf": np.concatenate([dt, f], axis=1).reshape(KT, P, 32).transpose(1, 0, 2),
        "keys": keys, "rel": a["rel_bias_2"], "onehot": onehot, "peer_u": a["peer_u"], "peer_v": a["peer_v"],
    }
    arrays = {f"{n}_dram": np.ascontiguousarray(v) for n, v in arrays.items()}
    nc = bacc.Bacc("TRN2", target_bir_lowering=False, num_devices=1)
    aps = [nc.dram_tensor(n, v.shape, mybir.dt.from_np(v.dtype), kind="ExternalInput").ap() for n, v in arrays.items()]
    aps.append(nc.dram_tensor("out_dram", (T, D), F32, kind="ExternalOutput").ap())
    build(nc, *aps)
    got = run(nc, [arrays], core_ids=[0])
    return got.results[0]["out_dram"].reshape(1, T, D)
```

```python
import numpy as np
import concourse.bass as bass
from concourse import mybir
from concourse.alu_op_type import AluOpType as ALU
from contextlib import ExitStack

F32 = mybir.dt.float32
F32R = mybir.dt.float32r
U32 = mybir.dt.uint32
ACT = mybir.ActivationFunctionType
AX = mybir.AxisListType

P = 128
D = 2048
T = 256
TT = T // P
KT = D // P
UNIT = 2048
EPS = 1e-6
RAW = 4
SPLIT = 2
NEG = -3.0e38

SSD_INNER, SSD_HEADS, SSD_CONV, XBC_TILES, Z_TILES = 1024, 16, 4, 12, 8
FOX_HEADS = 16
PEER_HEADS, PEER_KEYS, TOPK = 8, 128, 16
PICKS = PEER_HEADS * TOPK
TBLOCK, TBLOCKS = 32, T // 32
ATTN_HEADS, CONV_TILES, CONV_K, CROSS_HEADS = 8, 8, 31, 4
BUCKETS, REL = 32, 2 * T - 1
FF_ROUNDS = 4

PEER_ROUNDS = 8
STREAM = [("in1", "F", 36), ("v1", "R", 8), ("out1", "R", 16), ("wq", "F", 16)]
for _r in range(PEER_ROUNDS):
    STREAM += [(f"u{_r}", "F", 16), (f"e{_r}", "R", 16)]
STREAM += [("in2", "F", 32), ("v2", "R", 8), ("out2", "R", 16),
          ("ck", "F", 4), ("cv", "C", 4), ("cq", "F", 4), ("co", "O", 4)]
for _r in range(FF_ROUNDS):
    STREAM += [(f"up{_r}", "F", 16), (f"down{_r}", "R", 16)]
UNIT0, ROUND0 = {}, {}
_u = _g = 0
for _name, _kind, _n in STREAM:
    UNIT0[_name], ROUND0[_name] = _u, _g
    _u += _n
    _g += {"F": _n // 4, "R": _n // 8, "C": 1, "O": 2}[_kind]
UNITS = _u

COLS = {}
_c = 0
for _name, _n in [("ln1", KT), ("gmix", KT), ("gcross", KT), ("gmem", KT), ("gmlp", KT),
                  ("cw1", XBC_TILES * SSD_CONV), ("cb1", XBC_TILES), ("nw1", Z_TILES), ("dskip", Z_TILES),
                  ("cw2", CONV_K * CONV_TILES), ("cb2", CONV_TILES), ("lg2", CONV_TILES), ("lb2", CONV_TILES)]:
    COLS[_name] = (_c, _c + _n)
    _c += _n
NCOLS = _c
CONSTS = {}
_c = 0
for _name, _n in [("ident", P), ("tri", P), ("ones", P), ("ntri", P), ("gt", P), ("flip", P),
                  ("mask", 2 * P), ("iota", P)]:
    CONSTS[_name] = (_c, _c + _n)
    _c += _n
NCONST = _c


class Steps:

    def __init__(self, eng, sem):
        self.eng, self.sem, self.n, self.loops = eng, sem, 0, []

    def did(self, inst):
        inst.then_inc(self.sem, 1)
        self.n += 1

    def wait(self):
        self.eng.wait_ge(self.sem, lin(self.n, *((var, per) for var, per, _ in self.loops)))

    def do(self, inst):
        self.did(inst)
        self.wait()

    def enter(self, var, per):
        self.loops.append((var, per, self.n))

    def leave(self, times):
        _, per, first = self.loops.pop()
        assert self.n - first == per, (self.n - first, per)
        self.n = first + per * times


def lin(const, *terms):
    value = None
    for var, factor in terms:
        if var is None or factor == 0:
            continue
        term = var * factor if factor != 1 else var
        value = term if value is None else value + term
    return const if value is None else value + const


def build(nc, x_in, mem_in, stream, cols_in, consts_in, rows_in, wide_in, wdtf_in, keys_in,
          rel_in, onehot_in, out):
    ctx = ExitStack()
    with ctx:
        base = [-(-nc.sbuf_base // 32) * 32]

        def at(name, shape, dt, offset):
            return nc.alloc_sbuf_tensor_at(name, shape, dt, offset=offset)

        def sb(name, shape, dt=F32):
            size = int(np.prod(shape[1:])) * 4
            t = at(name, shape, dt, base[0])
            base[0] += -(-size // 32) * 32
            return t

        def psum(name):
            return ctx.enter_context(nc.psum_tensor(name, [P, 512], F32))

        def sem(name):
            return ctx.enter_context(nc.semaphore(name))

        raw = sb("raw", [P, RAW, UNIT])
        w_hi = [sb(f"w_hi{i}", [P, UNIT], F32R) for i in range(SPLIT)]
        w_lo = [sb(f"w_lo{i}", [P, UNIT], F32R) for i in range(SPLIT)]
        a1_at = base[0]
        a1 = [sb("a1_hi", [P, KT, T], F32R), sb("a1_lo", [P, KT, T], F32R)]
        a2_at = base[0]
        a2 = [sb("a2_hi", [P, KT, T], F32R), sb("a2_lo", [P, KT, T], F32R)]
        x = sb("x", [P, TT, D])
        work_at = base[0]
        WORK = 47104
        base[0] += WORK
        consts = sb("consts", [P, NCONST])
        cols = sb("cols", [P, NCOLS])
        rows = sb("rows", [P, 48])
        wdtf = sb("wdtf", [P, KT, 32])
        tmp = sb("tmp", [P, 4, T])
        sp = sb("sp", [P, 6, TT, 32])
        acum = sb("acum", [P, 4, SSD_HEADS])
        stat = sb("stat", [P, 16])
        amax = sb("amax", [P, 2, TT])
        asum = sb("asum", [P, 2, TT])
        assert base[0] <= nc.sbuf_usable_end, (base[0], nc.sbuf_usable_end)

        def C(name, a=0, b=None):
            lo, hi = CONSTS[name]
            return consts[:, lo + a:(hi if b is None else lo + b)]

        def col(name, i):
            return cols[:, COLS[name][0] + i:COLS[name][0] + i + 1]

        inT = at("inT", [P, 36, T], F32, work_at)
        v1 = at("v1", [P, TT, 1024], F32, work_at + 36864)
        xdt = at("xdt", [P, TT, SSD_INNER], F32, a1_at)
        yT = at("yT", [P, Z_TILES, T], F32, a1_at + 8192)
        cbm = at("cbm", [P, 2, 384], F32, a1_at + 16384)
        seg = at("seg", [P, 2, 384], F32, a1_at + 19456)
        seg_m = at("seg_m", [P, 2, 384], F32, a1_at + 22528)
        pbuf = at("pbuf", [P, 2, 512], F32, a1_at + 16384)
        ptbuf = at("ptbuf", [P, 2, 512], F32, a1_at + 20480)
        brev = at("brev", [P, ATTN_HEADS, T], F32, a1_at + 24576)
        h2 = at("h2", [P, TT, D], F32, work_at)
        act0 = at("act0", [P, KT, T], F32, work_at)
        wide = at("wide", [P, D], F32, work_at + 16384)
        cand = at("cand", [P, PEER_HEADS, 256], F32, work_at + 24576)
        onehot = at("onehot", [P, PICKS, TOPK], F32, work_at + 24576)
        pick_a = at("pick_a", [P, 8, P], F32, work_at + 24576)
        pick_b = at("pick_b", [P, 8, P], F32, work_at + 28672)
        gbuf = at("gbuf", [P, 4, TBLOCKS, 4 * TBLOCK], F32, work_at + 16384)
        pk = work_at + 32768
        top_v = at("top_v", [P, 16, TOPK], F32, pk)
        top_i = at("top_i", [P, 16, TOPK], U32, pk + 1024)
        top_f = at("top_f", [P, 16, TOPK], F32, pk + 2048)
        sc = at("sc", [P, TT, PEER_HEADS, TOPK], F32, pk + 3072)
        pos = at("pos", [P, PEER_HEADS, TOPK], U32, pk + 4096)
        posab = at("posab", [P, 2, PICKS], U32, pk + 4608)
        posf = at("posf", [P, 2, PICKS], F32, pk + 5632)
        picked = at("picked", [P, TT, 3, PICKS], F32, pk + 6656)
        pickT = at("pickT", [P, 3, T], F32, pk + 9728)
        gsum = at("gsum", [P, TT, PEER_HEADS], F32, pk + 12800)
        first = at("first", [P, PEER_HEADS], F32, pk + 12864)
        qT = at("qT", [P, 16, T], F32, a2_at)
        keys = at("keys", [P, 16, P], F32, a2_at + 16384)
        s_sb = [at("s_sb0", [P, 16, P], F32, a2_at + 24576), at("s_sb1", [P, 16, P], F32, work_at + 16384)]
        stage = at("stage", [P, 2, PEER_KEYS, TBLOCK], F32, a2_at)
        inT2 = at("inT2", [P, 32, T], F32, work_at)
        v2 = at("v2", [P, TT, 1024], F32, work_at + 32768)
        padded = at("padded", [P, CONV_TILES, T + CONV_K - 1], F32, a2_at)
        conv = at("conv", [P, CONV_TILES, T], F32, a1_at)
        relT = at("relT", [ATTN_HEADS, REL + 1], F32, a1_at + 16384)
        rel_sb = at("rel_sb", [BUCKETS, ATTN_HEADS], F32, a1_at + 18496)
        oneh_sb = at("oneh_sb", [BUCKETS, REL], F32, a1_at + 20480)
        mem = at("mem", [P, TT, D], F32, work_at)
        ckT = at("ckT", [P, 4, T], F32, work_at + 16384)
        cqT = at("cqT", [P, 4, T], F32, work_at + 20480)
        cv = at("cv", [P, TT, 512], F32, work_at + 24576)
        norm = at("norm", [P, TT, D], F32, work_at)

        bank = [psum(f"bank{i}") for i in range(8)]

        raw_full = [sem(f"raw_full{i}") for i in range(RAW)]
        hi_done = sem("hi_done")
        split_done = sem("split_done")
        mm_done = sem("mm_done")
        bank_free = sem("bank_free")
        act_own = sem("act_own")
        dve_own = sem("dve_own")
        pool_own = sem("pool_own")
        s_x = sem("s_x")
        s_small = sem("s_small")
        s_rel = sem("s_rel")
        sq_done = sem("sq_done")
        rs_done = sem("rs_done")
        normed = sem("normed")
        tr_done = sem("tr_done")
        tmp_full = sem("tmp_full")
        tmp_split = sem("tmp_split")
        a2_ready = sem("a2_ready")
        s_sp = sem("s_sp")
        sp_dve = sem("sp_dve")
        sp_act = sem("sp_act")
        s_cum = sem("s_cum")
        cum_dve = sem("cum_dve")
        conv_done = sem("conv_done")
        xbc_done = sem("xbc_done")
        cb_done = sem("cb_done")
        cbm_done = sem("cbm_done")
        xs_done = sem("xs_done")
        xdt_done = sem("xdt_done")
        arow_done = sem("arow_done")
        seg_done = sem("seg_done")
        exp_done = sem("exp_done")
        m_done = sem("m_done")
        y_done = sem("y_done")
        y_out = sem("y_out")
        ysq_done = sem("ysq_done")
        ms_done = sem("ms_done")
        rv_done = sem("rv_done")
        rt_done = sem("rt_done")
        at_s = sem("at_s")
        at_max = sem("at_max")
        at_exp = sem("at_exp")
        at_p = sem("at_p")
        at_t = sem("at_t")
        at_tc = sem("at_tc")
        at_o = sem("at_o")
        at_oc = sem("at_oc")
        resid = sem("resid")
        s_wide = sem("s_wide")
        s_keys = sem("s_keys")
        sk_done = sem("sk_done")
        sk_copied = sem("sk_copied")
        sm_dve = sem("sm_dve")
        sm_act = sem("sm_act")
        picks_done = sem("picks_done")
        pickT_psum = sem("pickT_psum")
        oh_done = sem("oh_done")
        g_mm = sem("g_mm")
        g_evict = sem("g_evict")
        g_write = [sem(f"g_write{i}") for i in range(2)]
        g_full = sem("g_full")
        g_used = sem("g_used")
        hidden_seen = sem("hidden_seen")
        s_relT = sem("s_relT")
        relT_done = sem("relT_done")
        s_relw = sem("s_relw")
        s_brev = sem("s_brev")
        sig_done = sem("sig_done")
        pad_zero = sem("pad_zero")
        cv_done = sem("cv_done")
        mu_done = sem("mu_done")
        cen_done = sem("cen_done")
        csq_done = sem("csq_done")
        var_done = sem("var_done")
        cn_done = sem("cn_done")
        cn_done2 = sem("cn_done2")
        seg_raw = sem("seg_raw")
        idx_taken = sem("idx_taken")
        s_mem = sem("s_mem")
        ck_done = sem("ck_done")
        cq_done = sem("cq_done")
        cv_copied = sem("cv_copied")
        in1_copied = sem("in1_copied")
        in2_copied = sem("in2_copied")
        wq_copied = sem("wq_copied")
        mix_free = sem("mix_free")
        s_out = sem("s_out")
        fin = sem("fin")

        gates_d = nc.dram_tensor("gates_scratch", (TBLOCKS, P, PEER_KEYS * TBLOCK), F32, kind="Internal").ap()
        rel_d = nc.dram_tensor("rel_scratch", (ATTN_HEADS, 512), F32, kind="Internal").ap()

        NORMS = ["ln1", "ln2", "lnf", "gmix", "gmem", "gcross", "gmlp", "final"]
        NQ = {n: i for i, n in enumerate(NORMS)}
        BUILDS = ["ln1", "ln2"] + [f"u{r}" for r in range(1, PEER_ROUNDS)] + ["gmix", "gmem", "gcross", "gmlp"]
        BUILDS += [f"up{r}" for r in range(FF_ROUNDS)]
        BQ = {n: 16 * i for i, n in enumerate(BUILDS)}
        TRQ = {n: 16 * i for i, n in enumerate(n for n in BUILDS if n[0] != "u")}
        RU, RB, RT = 32, 24, 16
        HEAD0 = {"fox": 0, "moba": FOX_HEADS, "cross": FOX_HEADS + ATTN_HEADS}
        CAUSAL = dict(segs=[(0, P), (P, 2 * P)], turns=[(0, 0), (P, P), (2 * P, 2 * P)],
                      pv=[(0, 0, 2 * P, 0), (1, 2 * P, P, P)])
        FULL = dict(segs=[(0, 2 * P), (2 * P, 2 * P)], turns=[(0, 0), (2 * P, P), (P, 2 * P), (3 * P, 3 * P)],
                    pv=[(0, 0, 2 * P, 0), (1, 2 * P, 2 * P, 0)])

        block = ctx.enter_context(nc.Block())

        @block.sync
        def _(sp_eng):
            eng = nc.sync
            for tt in range(TT):
                eng.dma_start(x[:, tt, :], x_in[tt * P:(tt + 1) * P, :]).then_inc(s_x, 16)
            for j in range(RAW):
                eng.dma_start(raw[:, j, :], stream[j, :, :]).then_inc(raw_full[j], 16)
            with eng.Fori(1, UNITS // RAW) as g:
                for j in range(RAW):
                    eng.wait_ge(split_done, g * RAW + (j - RAW + 1))
                    eng.dma_start(raw[:, j, :], stream[bass.ds(g * RAW + j, 1), :, :].rearrange("a p n -> p (a n)"))\
                        .then_inc(raw_full[j], 16)
            for tt in range(TT):
                eng.wait_ge(fin, tt + 1)
                eng.dma_start(out[tt * P:(tt + 1) * P, :], x[:, tt, :]).then_inc(s_out, 16)
            eng.wait_ge(s_out, 32)

        @block.gpsimd
        def _(pool):
            eng = nc.gpsimd
            own = Steps(eng, pool_own)
            eng.dma_start(consts[:, :], consts_in).then_inc(s_small, 16)
            eng.dma_start(cols[:, :], cols_in).then_inc(s_small, 16)
            eng.dma_start(rows[:, :], rows_in.partition_broadcast(P)).then_inc(s_small, 16)
            eng.dma_start(wdtf[:, :, :], wdtf_in).then_inc(s_small, 16)
            own.do(eng.memset(stat[:, 12:14], -0.5))

            def rsqrt(name):
                eng.wait_ge(sq_done, TT * (NQ[name] + 1))
                own.do(eng.tensor_scalar(stat[:, 4:6], stat[:, 0:2], 1.0 / D, EPS, ALU.mult, ALU.add))
                eng.tensor_tensor(stat[:, 2:4], stat[:, 4:6], stat[:, 12:14], ALU.pow).then_inc(rs_done, 1)

            rsqrt("ln1")
            eng.wait_ge(mm_done, UNIT0["out1"] + 4)
            eng.dma_start(wide[:, :], wide_in[0:1, :].partition_broadcast(P)).then_inc(s_wide, 16)
            rsqrt("ln2")
            eng.wait_ge(mm_done, UNIT0["wq"])
            eng.dma_start(keys[:, :, :], keys_in).then_inc(s_keys, 16)

            def load_gates(r, g):
                src = gates_d[:, :, bass.ds(lin(0, (r, 16 * TBLOCK), (g, 4 * TBLOCK)), 4 * TBLOCK)]
                eng.dma_start(gbuf[:, bass.ds(g, 1), :, :].rearrange("p a b n -> p (a b) n"),
                              src.rearrange("b p n -> p b n")).then_inc(g_full, 16)

            for i in range(2):
                eng.wait_ge(g_write[i], 16 * (TBLOCKS // 2 + 1))
            with eng.Fori(0, 4) as g:
                load_gates(None, g)
                eng.wait_ge(g_full, lin(16, (g, 16)))
            with eng.Fori(1, PEER_ROUNDS) as r:
                with eng.Fori(0, 4) as g:
                    eng.wait_ge(g_used, lin(4 - 16, (r, 16), (g, 4)))
                    load_gates(r, g)
                    eng.wait_ge(g_full, lin(16, (r, 64), (g, 16)))
            eng.wait_ge(g_used, 16 * PEER_ROUNDS)
            eng.dma_start(wide[:, :], wide_in[1:2, :].partition_broadcast(P)).then_inc(s_wide, 16)
            rsqrt("lnf")
            rsqrt("gmix")
            eng.wait_ge(mm_done, UNIT0["in2"] + 1)
            eng.memset(padded[:, :, 0:CONV_K - 1], 0.0).then_inc(pad_zero, 1)
            eng.wait_ge(mm_done, UNIT0["out2"])
            eng.dma_start(rel_sb[:, :], rel_in).then_inc(s_rel, 16)
            eng.dma_start(oneh_sb[:, :], onehot_in).then_inc(s_rel, 16)
            eng.wait_ge(relT_done, 1)
            eng.dma_start(rel_d[:, 0:REL], relT[:, 0:REL]).then_inc(s_relw, 16)
            eng.wait_ge(s_relw, 16)
            hankel = bass.AP(tensor=rel_d.tensor, offset=0, ap=[[1, P], [512, ATTN_HEADS], [1, T]])
            eng.dma_start(brev[:, :, :], hankel).then_inc(s_brev, 16)
            eng.wait_ge(mm_done, UNIT0["out2"] + 1)
            eng.dma_start(mem[:, :, :], mem_in.rearrange("(t p) d -> p t d", p=P)).then_inc(s_mem, 16)
            rsqrt("gmem")
            rsqrt("gcross")
            rsqrt("gmlp")
            eng.wait_ge(mm_done, UNIT0["up0"] + 1)
            eng.dma_start(wide[:, :], wide_in[2:3, :].partition_broadcast(P)).then_inc(s_wide, 16)
            rsqrt("final")

        @block.scalar
        def _(act):
            eng = nc.scalar
            own = Steps(eng, act_own)

            def hi(landed, k):
                eng.wait_ge(raw_full[k % RAW], landed)
                eng.activation(w_hi[k % SPLIT][:, :], raw[:, k % RAW, :], ACT.Copy).then_inc(hi_done, 1)

            def ahead(u, *loops):
                k = u + 2
                eng.wait_ge(mm_done, lin(u + 1, *loops))
                hi(lin(16 * (k // RAW + 1), *((v, n * 16 // RAW) for v, n in loops)), k)

            def feature(name, n, first, evict, r=None):
                u0 = UNIT0[name] + first
                with eng.Fori(0, n // 4) as g:
                    for j in range(4):
                        ahead(u0 + j, (r, RU), (g, 4))
                        evict(g, j)

            def row_units(name, pairs, evict=None, last=False, r=None):
                u0 = UNIT0[name]
                loops = pairs - 1 if last else pairs
                with eng.Fori(0, loops) as g:
                    for j in range(8):
                        ahead(u0 + j, (r, RU), (g, 8))
                        if evict and j % 4 == 3:
                            evict(g, j // 4)
                if last:
                    for j in range(6):
                        ahead(u0 + 8 * loops + j)

            def squares(name, src):
                for tt in range(TT):
                    eng.activation(junk_act[:, :], src[:, tt, :], ACT.Square, accum_out=stat[:, tt:tt + 1])\
                        .then_inc(sq_done, 1)
                    eng.wait_ge(sq_done, TT * NQ[name] + tt + 1)

            def scaled_tiles(name, weight):
                for kt in range(KT):
                    eng.wait_ge(tr_done, TRQ[name] + kt + 1)
                    n = BQ[name] + kt
                    if n >= 4:
                        eng.wait_ge(tmp_split, n - 3)
                    if weight is None:
                        eng.activation(tmp[:, n % 4, :], bank[4 + kt % 4][:, 0:T], ACT.Copy).then_inc(tmp_full, 1)
                    else:
                        eng.activation(tmp[:, n % 4, :], bank[4 + kt % 4][:, 0:T], ACT.Copy,
                                       scale=col(weight, kt)).then_inc(tmp_full, 1)

            def attention(name, heads, plan, masked):
                width = plan["turns"][-1][1] + P
                for i in range(heads + 1):
                    if i < heads:
                        h = HEAD0[name] + i
                        eng.wait_ge(at_max, h + 1)
                        for q, (c, n) in enumerate(plan["segs"]):
                            src = pbuf[:, h % 2, c:c + n] if masked else bank[4 + h % 2][:, c:c + n]
                            last = eng.activation(pbuf[:, h % 2, c:c + n], src, ACT.Exp, bias=amax[:, h % 2, q:q + 1],
                                                  accum_out=asum[:, h % 2, q:q + 1])
                            last.then_inc(at_exp, 1)
                    if i >= 1:
                        h = HEAD0[name] + i - 1
                        eng.wait_ge(at_t, h + 1)
                        if h >= 2:
                            eng.wait_ge(at_o, h - 1)
                        eng.activation(ptbuf[:, h % 2, 0:width], bank[6][:, 0:width], ACT.Copy).then_inc(at_tc, 1)

            junk_act = at("junk_act", [P, D], F32, work_at + 36864)
            eng.wait_ge(s_x, 32)
            squares("ln1", x)
            eng.sem_inc(bank_free, 4)
            for j in range(SPLIT):
                hi(16, j)
            eng.wait_ge(s_small, 64)
            scaled_tiles("ln1", "ln1")

            eng.wait_ge(sp_dve, 1)
            eng.activation(sp[:, 1, :, :], sp[:, 2, :, :], ACT.Exp).then_inc(sp_act, 1)
            eng.activation(rows[:, 32:48], rows[:, 32:48], ACT.Exp).then_inc(sp_act, 1)
            eng.wait_ge(sp_dve, 2)
            eng.activation(sp[:, 3, :, :], sp[:, 2, :, :], ACT.Ln).then_inc(sp_act, 1)

            def copy_in(first, scale=1.0, func=ACT.Copy):
                def evict(g, j):
                    eng.activation(inT[:, bass.ds(g * 4 + (first + j), 1), :].rearrange("p a t -> p (a t)"),
                                   bank[j][:, 0:T], func, scale=scale).then_inc(bank_free, 1)
                return evict
            feature("in1", 12, 0, copy_in(0))
            feature("in1", 8, 12, copy_in(12, func=ACT.Silu))
            feature("in1", 8, 20, copy_in(20, scale=64 ** -0.5))
            feature("in1", 8, 28, copy_in(28))

            def copy_v(dst):
                def evict(g, c):
                    for tt in range(TT):
                        eng.activation(dst[:, tt, bass.ds(g * 1024 + c * 512, 512)], bank[2 * c + tt][:, :],
                                       ACT.Copy).then_inc(bank_free, 1)
                return evict
            row_units("v1", 1, copy_v(v1))

            for i in range(XBC_TILES):
                eng.wait_ge(conv_done, i + 1)
                eng.activation(inT[:, i, :], tmp[:, i % 4, :], ACT.Silu, bias=col("cb1", i)).then_inc(xbc_done, 1)
            for h in range(SSD_HEADS):
                eng.wait_ge(seg_done, h + 1)
                eng.activation(seg[:, h % 2, :], seg[:, h % 2, :], ACT.Exp).then_inc(exp_done, 1)
            for i in range(Z_TILES):
                eng.wait_ge(y_out, i + 1)
                if i >= 4:
                    eng.wait_ge(ms_done, i - 3)
                eng.activation(tmp[:, i % 4, :], yT[:, i, :], ACT.Square).then_inc(ysq_done, 1)
            for g in range(2):
                eng.wait_ge(rv_done, g + 1)
                eng.activation(seg[:, g, 0:T], seg[:, g, 0:T], ACT.Sqrt).then_inc(rt_done, 1)

            attention("fox", FOX_HEADS, CAUSAL, True)

            row_units("out1", 2)

            eng.wait_ge(resid, 2)
            squares("ln2", x)
            scaled_tiles("ln2", None)

            def copy_q(g, j):
                eng.activation(qT[:, bass.ds(g * 4 + j, 1), :].rearrange("p a t -> p (a t)"),
                               bank[j][:, 0:T], ACT.Copy).then_inc(bank_free, 1)
            feature("wq", 16, 0, copy_q)
            for tt in range(TT):
                for g in range(4):
                    eng.wait_ge(sk_done, 4 * tt + g + 1)
                    eng.activation(s_sb[tt][:, 4 * g:4 * g + 4, :], bank[4 + g][:, :].rearrange("p (a n) -> p a n", a=4),
                                   ACT.Copy).then_inc(sk_copied, 1)

            def gelu0(g, j):
                eng.activation(act0[:, bass.ds(g * 4 + j, 1), :].rearrange("p a t -> p (a t)"),
                               bank[j][:, 0:T], ACT.Gelu).then_inc(bank_free, 1)
            feature("u0", 16, 0, gelu0)
            for tt in range(TT):
                eng.wait_ge(sm_dve, tt + 1)
                eng.activation(sc[:, tt, :, :], sc[:, tt, :, :], ACT.Exp).then_inc(sm_act, 1)

            for i in range(2):
                eng.sem_inc(g_write[i], 16)
            eng.sem_inc(g_evict, 2)
            with eng.Fori(0, TBLOCKS // 2) as pair:
                for half in range(2):
                    eng.wait_ge(g_write[half], lin(16, (pair, 16)))
                    with eng.Fori(0, TBLOCK // 8) as b:
                        for k in range(2):
                            eng.wait_ge(g_mm, lin(8 + half * TBLOCK + 4 * k + 4, (pair, 2 * TBLOCK), (b, 8)))
                            eng.activation(stage[:, half, :, bass.ds(lin(4 * k, (b, 8)), 4)].rearrange("p n t -> p t n"),
                                           bank[4 + k][:, :].rearrange("p (t n) -> p t n", t=4), ACT.Copy)\
                                .then_inc(g_evict, 1)
                    eng.wait_ge(g_evict, lin(2 + (half + 1) * (TBLOCK // 4), (pair, TBLOCK // 2)))
                    eng.dma_start(gates_d[bass.ds(lin(half, (pair, 2)), 1), :, :].rearrange("b p n -> p (b n)"),
                                  stage[:, half, :, :].rearrange("p n t -> p (n t)")).then_inc(g_write[half], 16)
            row_units("e0", 2)

            def gelu(r):
                def evict(g, j):
                    eng.wait_ge(tmp_split, lin(BQ["u1"] + j - 3, (r, RT), (g, 4)))
                    eng.activation(tmp[:, j, :], bank[j][:, 0:T], ACT.Gelu).then_inc(tmp_full, 1)
                    eng.wait_ge(tmp_full, lin(BQ["u1"] + j + 1, (r, RT), (g, 4)))
                    eng.sem_inc(bank_free, 1)
                return evict
            with eng.Fori(0, PEER_ROUNDS - 1) as r:
                feature("u1", 16, 0, gelu(r), r)
                row_units("e1", 2, r=r)
            eng.wait_ge(resid, 4)
            squares("lnf", x)
            eng.wait_ge(resid, 6)
            squares("gmix", x)
            scaled_tiles("gmix", "gmix")

            def copy2(first, scale=1.0, func=ACT.Copy):
                def evict(g, j):
                    eng.activation(inT2[:, bass.ds(g * 4 + (first + j), 1), :].rearrange("p a t -> p (a t)"),
                                   bank[j][:, 0:T], func, scale=scale).then_inc(bank_free, 1)
                return evict
            feature("in2", 8, 0, copy2(0))
            feature("in2", 8, 8, copy2(8, func=ACT.Sigmoid))
            feature("in2", 8, 16, copy2(16, scale=128 ** -0.5))
            feature("in2", 8, 24, copy2(24))
            row_units("v2", 1, copy_v(v2))
            eng.wait_ge(s_relT, 1)
            eng.activation(relT[:, 0:REL], bank[5][0:ATTN_HEADS, 0:REL], ACT.Copy).then_inc(relT_done, 1)
            for i in range(CONV_TILES):
                eng.wait_ge(cen_done, i + 1)
                if i >= 4:
                    eng.wait_ge(var_done, i - 3)
                eng.activation(tmp[:, i % 4, :], conv[:, i, :], ACT.Square).then_inc(csq_done, 1)
            eng.wait_ge(rv_done, 3)
            eng.activation(pbuf[:, 0, 0:T], pbuf[:, 0, 0:T], ACT.Sqrt).then_inc(rt_done, 1)
            for i in range(CONV_TILES):
                eng.wait_ge(cn_done, i + 1)
                eng.activation(conv[:, i, :], conv[:, i, :], ACT.Silu, scale=col("lg2", i), bias=col("lb2", i))\
                    .then_inc(cn_done2, 1)
            attention("moba", ATTN_HEADS, CAUSAL, True)
            row_units("out2", 2)

            eng.wait_ge(s_mem, 16)
            squares("gmem", mem)
            scaled_tiles("gmem", "gmem")

            def copy_small(dst, scale=1.0):
                def evict(g, j):
                    eng.activation(dst[:, bass.ds(g * 4 + j, 1), :].rearrange("p a t -> p (a t)"),
                                   bank[j][:, 0:T], ACT.Copy, scale=scale).then_inc(bank_free, 1)
                return evict
            feature("ck", 4, 0, copy_small(ckT))
            for j in range(4):
                ahead(UNIT0["cv"] + j)
            for tt in range(TT):
                eng.activation(cv[:, tt, :], bank[tt][:, :], ACT.Copy).then_inc(bank_free, 2)
            squares("gcross", x)
            scaled_tiles("gcross", "gcross")
            feature("cq", 4, 0, copy_small(cqT, 128 ** -0.5))
            attention("cross", CROSS_HEADS, FULL, False)
            for j in range(4):
                ahead(UNIT0["co"] + j)
            eng.wait_ge(resid, 10)
            squares("gmlp", x)
            scaled_tiles("gmlp", "gmlp")

            def relu(r, n0):
                def evict(g, j):
                    eng.wait_ge(tmp_split, lin(n0 + j - 3, (r, RT), (g, 4)))
                    eng.activation(tmp[:, j, :], bank[j][:, 0:T], ACT.Relu).then_inc(tmp_full, 1)
                    eng.wait_ge(tmp_full, lin(n0 + j + 1, (r, RT), (g, 4)))
                    eng.sem_inc(bank_free, 1)
                return evict
            with eng.Fori(0, FF_ROUNDS - 1) as r:
                feature("up0", 16, 0, relu(r, BQ["up0"]), r)
                row_units("down0", 2, r=r)
            feature(f"up{FF_ROUNDS - 1}", 16, 0, relu(None, BQ[f"up{FF_ROUNDS - 1}"]))
            row_units(f"down{FF_ROUNDS - 1}", 2, last=True)
            eng.wait_ge(resid, 12)
            squares("final", x)

        @block.vector
        def _(dve):
            eng = nc.vector
            own = Steps(eng, dve_own)

            def lo(done, k):
                eng.wait_ge(hi_done, done)
                eng.tensor_tensor(w_lo[k % SPLIT][:, :], raw[:, k % RAW, :], w_hi[k % SPLIT][:, :].bitcast(F32),
                                  ALU.subtract).then_inc(split_done, 1)

            def ahead(u, *loops):
                lo(lin(u + 3, *loops), u + 2)

            def split(dst, kt, src, sig, ap=None):
                h = dst[0][:, kt, :] if ap is None else dst[0][:, ap, :].rearrange("p a t -> p (a t)")
                l = dst[1][:, kt, :] if ap is None else dst[1][:, ap, :].rearrange("p a t -> p (a t)")
                own.do(eng.tensor_copy(h, src))
                eng.tensor_tensor(l, src, h.bitcast(F32), ALU.subtract).then_inc(sig, 1)

            def from_tmp(name, dst):
                for kt in range(KT):
                    n = BQ[name] + kt
                    eng.wait_ge(tmp_full, n + 1)
                    split(dst, kt, tmp[:, n % 4, :], tmp_split)

            def feature(name, n, first=0, extra=None, steps=0, r=None):
                u0 = UNIT0[name] + first
                with eng.Fori(0, n // 4) as g:
                    own.enter(g, steps)
                    for j in range(4):
                        ahead(u0 + j, (r, RU), (g, 4))
                        if extra:
                            extra(g, j)
                    own.leave(n // 4)

            def add_chunk(c, pair, done):
                eng.wait_ge(mm_done, done)
                for tt in range(TT):
                    xs = x[:, tt, bass.ds(c, 512)]
                    eng.tensor_tensor(xs, bank[2 * pair + tt][:, :], xs, ALU.add).then_inc(bank_free, 1)

            def row_units(name, pairs, add=True, last=False, r=None):
                u0 = UNIT0[name]
                loops = pairs - 1 if last else pairs
                with eng.Fori(0, loops) as g:
                    for j in range(8):
                        ahead(u0 + j, (r, RU), (g, 8))
                        if add and j % 4 == 3:
                            add_chunk(lin((j // 4) * 512, (g, 1024)), j // 4, lin(u0 + j + 1, (r, RU), (g, 8)))
                if last:
                    for j in range(8):
                        if j < 6:
                            ahead(u0 + 8 * loops + j)
                        if j % 4 == 3:
                            add_chunk(loops * 1024 + (j // 4) * 512, j // 4, u0 + 8 * loops + j + 1)

            def resid_ready():
                own.do(eng.memset(stat[:, 8:9], 0.0))
                eng.memset(stat[:, 9:10], 0.0).then_inc(resid, 2)

            def normalise(name, src, dst, wide_n=None):
                eng.wait_ge(rs_done, NQ[name] + 1)
                if wide_n:
                    eng.wait_ge(s_wide, 16 * wide_n)
                for tt in range(TT):
                    if wide_n:
                        i = eng.scalar_tensor_tensor(dst[:, tt, :], src[:, tt, :], stat[:, 2 + tt:3 + tt], wide[:, :],
                                                     ALU.mult, ALU.mult)
                    else:
                        i = eng.tensor_scalar(dst[:, tt, :], src[:, tt, :], stat[:, 2 + tt:3 + tt], None, ALU.mult)
                    i.then_inc(fin if name == "final" else (resid if name == "lnf" else normed), 1)

            def attention(name, heads, plan, masked):
                pair = name == "fox"
                for i in range(heads + 2):
                    if i < heads:
                        h = HEAD0[name] + i
                        s = bank[4 + h % 2]
                        eng.wait_ge(at_s, h + 1)
                        for q, (c, n) in enumerate(plan["segs"]):
                            m = amax[:, h % 2, q:q + 1]
                            if masked:
                                own.did(eng.tensor_tensor_reduce(pbuf[:, h % 2, c:c + n], s[:, c:c + n], C("mask", 2 * P - n),
                                                                 1.0, NEG, ALU.add, ALU.max, m))
                            else:
                                own.did(eng.tensor_reduce(m, s[:, c:c + n], AX.X, ALU.max))
                        own.wait()
                        eng.tensor_scalar(amax[:, h % 2, :], amax[:, h % 2, :], -1.0, None, ALU.mult).then_inc(at_max, 1)
                    if 1 <= i <= heads:
                        h = HEAD0[name] + i - 1
                        eng.wait_ge(at_exp, 2 * (h + 1))
                        own.do(eng.reciprocal(asum[:, h % 2, :], asum[:, h % 2, :]))
                        for q, (c, n) in enumerate(plan["segs"]):
                            eng.tensor_scalar(pbuf[:, h % 2, c:c + n], pbuf[:, h % 2, c:c + n], asum[:, h % 2, q:q + 1],
                                              None, ALU.mult).then_inc(at_p, 1)
                    if i >= 2:
                        h = HEAD0[name] + i - 2
                        if pair and h % 2 == 0:
                            continue
                        eng.wait_ge(at_o, h + 1)
                        kt = Z_TILES + (i - 2) // 2 if pair else i - 2
                        split(a2, kt, bank[7][:, 0:T], at_oc)

            for j in range(SPLIT):
                lo(j + 1, j)
            eng.wait_ge(s_x, 32)
            normalise("ln1", x, norm)
            eng.wait_ge(s_small, 64)
            from_tmp("ln1", a1)

            eng.wait_ge(s_sp, 2)
            for tt in range(TT):
                own.did(eng.tensor_tensor(sp[:, 0, tt, :], bank[6 + tt][:, 0:32], rows[:, 0:32], ALU.add))
            own.wait()
            own.do(eng.tensor_scalar(sp[:, 0, :, 16:32], sp[:, 0, :, 16:32], -1.0, None, ALU.mult))
            eng.scalar_tensor_tensor(sp[:, 2, :, :], sp[:, 0, :, :], -1.0, sp[:, 0, :, :], ALU.mult, ALU.min).then_inc(sp_dve, 1)
            eng.wait_ge(sp_act, 1)
            eng.tensor_scalar(sp[:, 2, :, :], sp[:, 1, :, :], 1.0, None, ALU.add).then_inc(sp_dve, 1)
            eng.wait_ge(sp_dve, 2)
            own.do(eng.tensor_scalar(sp[:, 4, :, :], sp[:, 2, :, :], -1.0, None, ALU.add))
            own.did(eng.tensor_scalar(sp[:, 5, :, :], sp[:, 4, :, :], 1e-30, None, ALU.max))
            own.wait()
            own.do(eng.reciprocal(sp[:, 5, :, :], sp[:, 5, :, :]))
            own.do(eng.tensor_tensor(sp[:, 5, :, :], sp[:, 5, :, :], sp[:, 1, :, :], ALU.mult))
            eng.wait_ge(sp_act, 3)
            own.do(eng.tensor_tensor(sp[:, 5, :, :], sp[:, 5, :, :], sp[:, 3, :, :], ALU.mult))
            own.do(eng.scalar_tensor_tensor(sp[:, 4, :, :], sp[:, 4, :, :], 0.0, sp[:, 1, :, :], ALU.is_equal, ALU.mult))
            own.do(eng.tensor_tensor(sp[:, 5, :, :], sp[:, 5, :, :], sp[:, 4, :, :], ALU.add))
            own.do(eng.scalar_tensor_tensor(sp[:, 0, :, :], sp[:, 0, :, :], 0.0, sp[:, 5, :, :], ALU.max, ALU.add))
            own.did(eng.tensor_scalar(sp[:, 1, :, 16:32], sp[:, 0, :, 16:32], -1.0, None, ALU.mult))
            for tt in range(TT):
                own.did(eng.scalar_tensor_tensor(sp[:, 1, tt, 0:16], sp[:, 0, tt, 0:16], -1.0, rows[:, 32:48],
                                                 ALU.mult, ALU.mult))
            own.wait()
            eng.memset(stat[:, 10:11], 0.0).then_inc(sp_dve, 1)

            feature("in1", 36)
            row_units("v1", 1, add=False)

            eng.wait_ge(s_cum, 1)
            for tt in range(TT):
                own.did(eng.tensor_scalar(acum[:, tt, :], bank[7][:, 16 * tt:16 * tt + 16], -1.0, None, ALU.mult))
            own.wait()
            own.did(eng.tensor_tensor(acum[:, 2, :], bank[7][:, 32:48], acum[:, 0, :], ALU.add))
            own.wait()
            eng.memset(stat[:, 11:12], 0.0).then_inc(cum_dve, 1)

            eng.wait_ge(mm_done, UNIT0["out1"])
            eng.wait_ge(bank_free, 4 * ROUND0["out1"] + 4)
            for i in range(XBC_TILES):
                t = tmp[:, i % 4, :]
                if i >= 4:
                    eng.wait_ge(xbc_done, i - 3)
                w = [cols[:, COLS["cw1"][0] + i * SSD_CONV + k:COLS["cw1"][0] + i * SSD_CONV + k + 1] for k in range(SSD_CONV)]
                own.do(eng.tensor_scalar(t, inT[:, i, :], w[3], None, ALU.mult))
                for s in (1, 2, 3):
                    inst = eng.scalar_tensor_tensor(t[:, s:T], inT[:, i, 0:T - s], w[3 - s], t[:, s:T], ALU.mult, ALU.add)
                    if s < 3:
                        own.do(inst)
                    else:
                        inst.then_inc(conv_done, 1)

            for g in range(2):
                eng.wait_ge(cb_done, g + 1)
                own.did(eng.tensor_tensor(cbm[:, g, 0:T], bank[4 + g][:, 0:T], C("tri", 0, T), ALU.mult))
                own.did(eng.tensor_tensor(cbm[:, g, T:T + P], bank[4 + g][:, T:T + P], C("tri"), ALU.mult))
            own.wait()
            eng.memset(stat[:, 11:12], 0.0).then_inc(cbm_done, 1)
            for n in range(4):
                tt, half = n // 2, n % 2
                eng.wait_ge(xs_done, n + 1)
                eng.tensor_tensor(xdt[:, tt, half * 512:half * 512 + 512].rearrange("p (h c) -> p h c", c=64),
                                  bank[6 + n % 2][:, :].rearrange("p (h c) -> p h c", c=64),
                                  sp[:, 0, tt, half * 8:half * 8 + 8].unsqueeze(2).to_broadcast([P, 8, 64]),
                                  ALU.mult).then_inc(xdt_done, 1)

            def segments(h):
                b, c = bank[4 + (h // 2) % 2], (h % 2) * T
                eng.wait_ge(arow_done, h // 2 + 1)
                if h >= 2:
                    eng.wait_ge(m_done, h - 1)
                for k, (dst, src, bias) in enumerate([(0, 0, 0), (P, P, 2), (T, P, 1)]):
                    eng.tensor_scalar(seg[:, h % 2, dst:dst + P], b[:, c + src:c + src + P], acum[:, bias, h:h + 1], 0.0,
                                      ALU.add, ALU.min).then_inc(seg_raw, 1)
                eng.wait_ge(seg_raw, 3 * (h + 1))
                eng.memset(stat[:, 11:12], 0.0).then_inc(seg_done, 1)

            def decay(h):
                eng.wait_ge(exp_done, h + 1)
                if h >= 2:
                    eng.wait_ge(y_done, h - 1)
                eng.tensor_tensor(seg_m[:, h % 2, :], seg[:, h % 2, :], cbm[:, h // 8, :], ALU.mult).then_inc(m_done, 1)

            def gated(i):
                eng.wait_ge(y_done, 2 * i + 2)
                own.do(eng.scalar_tensor_tensor(yT[:, i, :], inT[:, i, :], col("dskip", i), bank[6 + i % 2][:, 0:T],
                                                ALU.mult, ALU.add))
                eng.tensor_tensor(yT[:, i, :], yT[:, i, :], inT[:, XBC_TILES + i, :], ALU.mult).then_inc(y_out, 1)

            for h in range(SSD_HEADS + 2):
                if h < SSD_HEADS:
                    segments(h)
                if 1 <= h <= SSD_HEADS:
                    decay(h - 1)
                if h >= 3 and h % 2 == 1:
                    gated((h - 3) // 2)
            for g in range(2):
                eng.wait_ge(ms_done, 4 * (g + 1))
                eng.tensor_scalar(seg[:, g, 0:T], bank[4 + g][:, 0:T], 1.0 / 512, EPS, ALU.mult, ALU.add).then_inc(rv_done, 1)
            for g in range(2):
                eng.wait_ge(rt_done, g + 1)
                own.do(eng.reciprocal(seg[:, g, 0:T], seg[:, g, 0:T]))
            for i in range(Z_TILES):
                own.do(eng.scalar_tensor_tensor(yT[:, i, :], yT[:, i, :], col("nw1", i), seg[:, i // 4, 0:T], ALU.mult, ALU.mult))
                split(a2, i, yT[:, i, :], a2_ready)

            attention("fox", FOX_HEADS, CAUSAL, True)

            row_units("out1", 2)
            resid_ready()

            normalise("ln2", x, h2, 1)
            from_tmp("ln2", a1)
            feature("wq", 16)
            waiting = [UNIT0["u0"] + j for j in range(16)]

            def fill(n=1):
                for _ in range(n):
                    if waiting:
                        ahead(waiting.pop(0))

            def best(n, src, v, i):
                for k in range(2):
                    ks = slice(8 * k, 8 * k + 8)
                    for h in range(n):
                        own.did(eng.max(v[:, h, ks], src[:, h, :]))
                    own.wait()
                    fill()
                    for h in range(n):
                        own.did(eng.max_index(i[:, h, ks], v[:, h, ks], src[:, h, :]))
                    own.wait()
                    if k == 0:
                        for h in range(n):
                            own.did(eng.match_replace(src[:, h, :], v[:, h, ks], src[:, h, :], NEG))
                        own.wait()
                        fill()

            for tt in range(TT):
                eng.wait_ge(sk_copied, 4 * (tt + 1))
                best(16, s_sb[tt], top_v, top_i)
                own.did(eng.tensor_copy(top_f[:, :, :], top_i[:, :, :]))
                tv = top_v[:, :, :].rearrange("p (h two) k -> p h two k", two=2)
                tf = top_f[:, :, :].rearrange("p (h two) k -> p h two k", two=2)
                own.did(eng.tensor_tensor(cand[:, :, :].rearrange("p h (a b) -> p h a b", a=TOPK),
                                          tv[:, :, 0, :].unsqueeze(3).to_broadcast([P, PEER_HEADS, TOPK, TOPK]),
                                          tv[:, :, 1, :].unsqueeze(2).to_broadcast([P, PEER_HEADS, TOPK, TOPK]), ALU.add))
                own.wait()
                best(PEER_HEADS, cand, sc[:, tt, :, :], pos)
                own.did(eng.tensor_copy(first[:, :], sc[:, tt, :, 0]))
                pf = pos[:, :, :].rearrange("p h k -> p (h k)")
                own.did(eng.tensor_scalar(posab[:, 0, :], pf, 4, None, ALU.logical_shift_right))
                own.did(eng.tensor_scalar(posab[:, 1, :], pf, 15, None, ALU.bitwise_and))
                own.wait()
                eng.tensor_tensor(sc[:, tt, :, :], sc[:, tt, :, :],
                                  first[:, :].unsqueeze(2).to_broadcast([P, PEER_HEADS, TOPK]),
                                  ALU.subtract).then_inc(sm_dve, 1)
                own.do(eng.tensor_copy(posf[:, :, :], posab[:, :, :]))
                for half in range(2):
                    fill()
                    own.do(eng.tensor_tensor(onehot[:, :, :], C("iota", 0, TOPK).unsqueeze(1).to_broadcast([P, PICKS, TOPK]),
                                             posf[:, half, :].unsqueeze(2).to_broadcast([P, PICKS, TOPK]), ALU.is_equal))
                    oh = onehot[:, :, :].rearrange("p (h k) a -> p h k a", h=PEER_HEADS)
                    own.do(eng.tensor_tensor(oh, oh, tf[:, :, half, :].unsqueeze(2).to_broadcast([P, PEER_HEADS, TOPK, TOPK]),
                                             ALU.mult))
                    own.do(eng.tensor_reduce(picked[:, tt, half, :], onehot[:, :, :], AX.X, ALU.add))
            fill(16)
            for tt in range(TT):
                eng.wait_ge(sm_act, tt + 1)
                own.do(eng.tensor_reduce(gsum[:, tt, :], sc[:, tt, :, :], AX.X, ALU.add))
                own.do(eng.reciprocal(gsum[:, tt, :], gsum[:, tt, :]))
                eng.tensor_tensor(picked[:, tt, 2, :].rearrange("p (h k) -> p h k", h=PEER_HEADS), sc[:, tt, :, :],
                                  gsum[:, tt, :].unsqueeze(2).to_broadcast([P, PEER_HEADS, TOPK]), ALU.mult)\
                    .then_inc(picks_done, 1)
            eng.wait_ge(pickT_psum, 1)
            own.did(eng.tensor_copy(pickT[:, 0:2, :].rearrange("p a t -> p (a t)"), bank[6][:, :]))
            own.did(eng.tensor_copy(pickT[:, 2, :], bank[7][:, 0:T]))
            own.wait()
            with eng.Fori(0, T // 8) as b:
                for j in range(8):
                    t = lin(j, (b, 8))
                    eng.wait_ge(g_mm, lin(j + 1, (b, 8)))
                    eng.tensor_scalar(pick_a[:, j, :], C("iota"), pickT[:, 0, bass.ds(t, 1)], pickT[:, 2, bass.ds(t, 1)],
                                      ALU.is_equal, ALU.mult).then_inc(oh_done, 1)
                    eng.tensor_scalar(pick_b[:, j, :], C("iota"), pickT[:, 1, bass.ds(t, 1)], None,
                                      ALU.is_equal).then_inc(oh_done, 1)

            def gates_of(slot, j):
                return gbuf[:, bass.ds(slot, 1), :, j * TBLOCK:(j + 1) * TBLOCK].rearrange("p a b t -> p (a b) t")

            def blocks(ap):
                return ap.rearrange("p (b t) -> p b t", t=TBLOCK)

            with eng.Fori(0, 4) as g:
                own.enter(g, 4)
                for j in range(4):
                    if j == 0:
                        eng.wait_ge(g_full, lin(16, (g, 16)))
                    tile0 = act0[:, bass.ds(lin(j, (g, 4)), 1), :].rearrange("p a t -> p (a t)")
                    eng.tensor_tensor(blocks(tile0), blocks(tile0), gates_of(g, j), ALU.mult).then_inc(g_used, 1)
                    eng.wait_ge(g_used, lin(j + 1, (g, 4)))
                    split(a2, None, tile0, a2_ready, ap=bass.ds(lin(j, (g, 4)), 1))
                own.leave(4)
            row_units("e0", 2)
            with eng.Fori(0, PEER_ROUNDS - 1) as r:
                own.enter(r, 16)

                def gated(g, j):
                    if j == 0:
                        eng.wait_ge(g_full, lin(16 * 5, (r, 64), (g, 16)))
                    eng.wait_ge(tmp_full, lin(BQ["u1"] + j + 1, (r, RT), (g, 4)))
                    eng.tensor_tensor(blocks(tmp[:, j, :]), blocks(tmp[:, j, :]), gates_of(g, j), ALU.mult).then_inc(g_used, 1)
                    eng.wait_ge(g_used, lin(16 + j + 1, (r, 16), (g, 4)))
                    split(a2, None, tmp[:, j, :], tmp_split, ap=bass.ds(lin(j, (g, 4)), 1))
                feature("u1", 16, 0, gated, 4, r)
                row_units("e1", 2, r=r)
                own.leave(PEER_ROUNDS - 1)
            resid_ready()
            normalise("lnf", x, x, 2)

            eng.wait_ge(resid, 6)
            normalise("gmix", x, norm)
            from_tmp("gmix", a1)
            feature("in2", 32)
            row_units("v2", 1, add=False)
            eng.wait_ge(pad_zero, 1)
            eng.wait_ge(bank_free, 4 * ROUND0["out2"] + 4)
            for i in range(CONV_TILES):
                own.did(eng.tensor_tensor(padded[:, i, CONV_K - 1:], inT2[:, i, :], inT2[:, CONV_TILES + i, :], ALU.mult))
            own.wait()
            for i in range(CONV_TILES):
                own.did(eng.tensor_scalar(conv[:, i, :], padded[:, i, 0:T], col("cw2", i), col("cb2", i), ALU.mult, ALU.add))
            own.wait()
            with eng.Fori(1, CONV_K) as k:
                own.enter(k - 1, CONV_TILES)
                for i in range(CONV_TILES):
                    if i == 0:
                        own.wait()
                    own.did(eng.scalar_tensor_tensor(
                        conv[:, i, :], padded[:, i, bass.ds(k, T)],
                        cols[:, bass.ds(k * CONV_TILES + (COLS["cw2"][0] + i), 1)], conv[:, i, :], ALU.mult, ALU.add))
                own.leave(CONV_K - 1)
            own.wait()
            eng.sem_inc(cv_done, 1)
            eng.wait_ge(mu_done, 1)
            eng.wait_ge(s_brev, 16)
            own.do(eng.tensor_scalar(pbuf[:, 1, 0:T], bank[4][:, 0:T], 1.0 / 1024, None, ALU.mult))
            for i in range(CONV_TILES):
                eng.tensor_tensor(conv[:, i, :], conv[:, i, :], pbuf[:, 1, 0:T], ALU.subtract).then_inc(cen_done, 1)
            eng.wait_ge(var_done, CONV_TILES)
            eng.tensor_scalar(pbuf[:, 0, 0:T], bank[4][:, 0:T], 1.0 / 1024, EPS, ALU.mult, ALU.add).then_inc(rv_done, 1)
            eng.wait_ge(rt_done, 3)
            own.do(eng.reciprocal(pbuf[:, 0, 0:T], pbuf[:, 0, 0:T]))
            for i in range(CONV_TILES):
                eng.tensor_tensor(conv[:, i, :], conv[:, i, :], pbuf[:, 0, 0:T], ALU.mult).then_inc(cn_done, 1)
            for i in range(CONV_TILES):
                eng.wait_ge(cn_done2, i + 1)
                split(a2, ATTN_HEADS + i, conv[:, i, :], a2_ready)
            attention("moba", ATTN_HEADS, CAUSAL, True)
            row_units("out2", 2)
            resid_ready()

            normalise("gmem", mem, norm)
            from_tmp("gmem", a1)
            feature("ck", 4)
            for j in range(4):
                ahead(UNIT0["cv"] + j)
            normalise("gcross", x, norm)
            from_tmp("gcross", a1)
            feature("cq", 4)
            attention("cross", CROSS_HEADS, FULL, False)
            for j in range(4):
                ahead(UNIT0["co"] + j)
                add_chunk(j * 512, j % 2, UNIT0["co"] + j + 1)
            resid_ready()

            normalise("gmlp", x, norm)
            from_tmp("gmlp", a1)
            def square(r, n0):
                def extra(g, j):
                    eng.wait_ge(tmp_full, lin(n0 + j + 1, (r, RT), (g, 4)))
                    own.do(eng.tensor_tensor(tmp[:, j, :], tmp[:, j, :], tmp[:, j, :], ALU.mult))
                    split(a2, None, tmp[:, j, :], tmp_split, ap=bass.ds(lin(j, (g, 4)), 1))
                return extra
            with eng.Fori(0, FF_ROUNDS - 1) as r:
                own.enter(r, 32)
                feature("up0", 16, 0, square(r, BQ["up0"]), 8, r)
                row_units("down0", 2, r=r)
                own.leave(FF_ROUNDS - 1)
            feature(f"up{FF_ROUNDS - 1}", 16, 0, square(None, BQ[f"up{FF_ROUNDS - 1}"]), 8)
            row_units(f"down{FF_ROUNDS - 1}", 2, last=True)
            resid_ready()
            normalise("final", x, x, 3)

        @block.tensor
        def _(pe):
            eng = nc.tensor
            mm = nc.tensor.matmul

            def feature(name, n, act_t, r=None):
                u0, b0 = UNIT0[name], 4 * ROUND0[name]
                with eng.Fori(0, n // 4) as g:
                    for j in range(4):
                        eng.wait_ge(split_done, lin(u0 + j + 1, (r, RU), (g, 4)))
                        eng.wait_ge(bank_free, lin(b0 + j + 1, (r, RB), (g, 4)))
                        hi, lo = w_hi[j % SPLIT], w_lo[j % SPLIT]
                        for kt in range(KT):
                            ks = slice(kt * P, kt * P + P)
                            o = bank[j][:, 0:T]
                            mm(o, hi[:, ks], act_t[0][:, kt, :], start=kt == 0, stop=False)
                            mm(o, hi[:, ks], act_t[1][:, kt, :], start=False, stop=False)
                            last = mm(o, lo[:, ks], act_t[0][:, kt, :], start=False, stop=kt == KT - 1)
                        last.then_inc(mm_done, 1)

            def row_unit(j, banks, act_t, k0, first, end):
                hi, lo = w_hi[j % SPLIT], w_lo[j % SPLIT]
                for k in range(4):
                    ns = slice(k * 512, k * 512 + 512)
                    for tt in range(TT):
                        o = banks[tt][:, :]
                        ts = slice(tt * P, tt * P + P)
                        mm(o, act_t[0][:, k0 + k, ts], hi[:, ns], start=first and k == 0, stop=False)
                        mm(o, act_t[0][:, k0 + k, ts], lo[:, ns], start=False, stop=False)
                        last = mm(o, act_t[1][:, k0 + k, ts], hi[:, ns], start=False, stop=end and k == 3)
                last.then_inc(mm_done, 1)

            def row_units(name, pairs, act_t, r=None):
                u0, b0 = UNIT0[name], 4 * ROUND0[name]
                with eng.Fori(0, pairs) as g:
                    for j in range(8):
                        c = j // 4
                        eng.wait_ge(split_done, lin(u0 + j + 1, (r, RU), (g, 8)))
                        if j % 4 == 0:
                            eng.wait_ge(bank_free, lin(b0 + 2 * c + 2, (r, RB), (g, 4)))
                        row_unit(j, bank[2 * c:2 * c + 2], act_t, 4 * (j % 4), j % 4 == 0, j % 4 == 3)

            def turn(name, src):
                if name != "ln1" :
                    pass
                for kt in range(KT):
                    if kt >= 4:
                        eng.wait_ge(tmp_full, BQ[name] + kt - 3)
                    for tt in range(TT):
                        last = eng.transpose(bank[4 + kt % 4][:, tt * P:tt * P + P], src[:, tt, kt * P:kt * P + P], C("ident"))
                    last.then_inc(tr_done, 1)

            def attention(name, heads, plan, scores, values, d):
                for i in range(heads + 2):
                    if i < heads:
                        h = HEAD0[name] + i
                        if i >= 2:
                            eng.wait_ge(at_exp, 2 * (h - 1))
                        scores(i, bank[4 + h % 2]).then_inc(at_s, 1)
                    if 1 <= i <= heads:
                        h = HEAD0[name] + i - 1
                        eng.wait_ge(at_p, 2 * (h + 1))
                        if h >= 1:
                            eng.wait_ge(at_tc, h)
                        for src, dst in plan["turns"]:
                            last = eng.transpose(bank[6][:, dst:dst + P], pbuf[:, h % 2, src:src + P], C("ident"))
                        last.then_inc(at_t, 1)
                    if i >= 2:
                        h = HEAD0[name] + i - 2
                        eng.wait_ge(at_tc, h + 1)
                        if d == P or h % 2 == 0:
                            done = h // 2 if d == 64 else FOX_HEADS // 2 + (h - FOX_HEADS)
                            if done > 0:
                                eng.wait_ge(at_oc, done)
                        p0 = 64 * (h % 2) if d == 64 else 0
                        for n, (kb, src, w, dst) in enumerate(plan["pv"]):
                            last = mm(bank[7][p0:p0 + d, dst:dst + w], values(i - 2, kb), ptbuf[:, h % 2, src:src + w],
                                      start=n == 0, stop=n == len(plan["pv"]) - 1)
                        last.then_inc(at_o, 1)

            eng.wait_ge(s_small, 64)
            eng.wait_ge(normed, 2)
            turn("ln1", norm)
            eng.wait_ge(tmp_split, 16)
            for tt in range(TT):
                for kt in range(KT):
                    for part in range(2):
                        last = mm(bank[6 + tt][:, 0:32], a1[part][:, kt, tt * P:tt * P + P].bitcast(F32), wdtf[:, kt, :],
                                  start=kt == 0 and part == 0, stop=kt == KT - 1 and part == 1)
                last.then_inc(s_sp, 1)
            feature("in1", 36, a1)
            row_units("v1", 1, a1)

            eng.wait_ge(sp_dve, 3)
            for tt in range(TT):
                mm(bank[7][:, 16 * tt:16 * tt + 16], C("tri"), sp[:, 1, tt, 0:16], start=True, stop=True)
            mm(bank[7][:, 32:48], C("ones"), sp[:, 1, 0, 0:16], start=True, stop=True).then_inc(s_cum, 1)

            eng.wait_ge(xbc_done, XBC_TILES)
            for g in range(2):
                bT, cT = inT[:, 8 + g, :], inT[:, 10 + g, :]
                mm(bank[4 + g][:, 0:T], bT[:, 0:P], cT, start=True, stop=True)
                mm(bank[4 + g][:, T:T + P], bT[:, P:T], cT[:, P:T], start=True, stop=True).then_inc(cb_done, 1)
            eng.wait_ge(cum_dve, 1)
            for n in range(4):
                tt, half = n // 2, n % 2
                if n >= 2:
                    eng.wait_ge(xdt_done, n - 1)
                for i in range(4):
                    last = eng.transpose(bank[6 + n % 2][:, i * P:i * P + P], inT[:, half * 4 + i, tt * P:tt * P + P], C("ident"))
                last.then_inc(xs_done, 1)

            def arow(n):
                if n == 0:
                    eng.wait_ge(cbm_done, 1)
                if n >= 2:
                    eng.wait_ge(seg_done, 2 * n - 2)
                for h in range(2):
                    for tt in range(TT):
                        last = mm(bank[4 + n % 2][:, h * T + tt * P:h * T + tt * P + P],
                                  sp[:, 1, tt, 2 * n + h:2 * n + h + 1].to_broadcast([P, P]), C("tri"), start=True, stop=True)
                last.then_inc(arow_done, 1)

            def ssd_head(h):
                i, p0 = h // 2, 64 * (h % 2)
                if h == 0:
                    eng.wait_ge(xdt_done, 4)
                if h % 2 == 0 and i >= 2:
                    eng.wait_ge(y_out, i - 1)
                eng.wait_ge(m_done, h + 1)
                o = bank[6 + i % 2]
                mm(o[p0:p0 + 64, 0:T], xdt[:, 0, h * 64:h * 64 + 64], seg_m[:, h % 2, 0:T], start=True, stop=False)
                mm(o[p0:p0 + 64, P:T], xdt[:, 1, h * 64:h * 64 + 64], seg_m[:, h % 2, T:T + P], start=False, stop=True)\
                    .then_inc(y_done, 1)

            arow(0)
            for n in range(SSD_HEADS // 2):
                if n + 1 < SSD_HEADS // 2:
                    arow(n + 1)
                ssd_head(2 * n)
                ssd_head(2 * n + 1)
            for i in range(Z_TILES):
                eng.wait_ge(ysq_done, i + 1)
                mm(bank[4 + i // 4][:, 0:T], C("ones"), tmp[:, i % 4, :], start=i % 4 == 0, stop=i % 4 == 3).then_inc(ms_done, 1)

            def fox_scores(i, b):
                t, p0 = i // 2, 64 * (i % 2)
                q, k = inT[p0:p0 + 64, 20 + t, :], inT[p0:p0 + 64, 28 + t, :]
                f = [sp[:, 1, tt, 16 + i:17 + i] for tt in range(TT)]
                mm(b[:, 0:P], q[:, 0:P], k[:, 0:P], start=True, stop=False)
                mm(b[:, 0:P], C("tri"), f[0].to_broadcast([P, P]), start=False, stop=False)
                mm(b[:, 0:P], f[0].to_broadcast([P, P]), C("ntri"), start=False, stop=True)
                mm(b[:, P:3 * P], q[:, P:T], k, start=True, stop=False)
                mm(b[:, P:2 * P], f[0].to_broadcast([P, P]), C("gt"), start=False, stop=False, skip_group_check=True)
                mm(b[:, 2 * P:3 * P], f[1].to_broadcast([P, P]), C("ntri"), start=False, stop=False, skip_group_check=True)
                return mm(b[:, P:3 * P], C("tri"), f[1].to_broadcast([P, T]), start=False, stop=True)

            eng.wait_ge(rv_done, 2)
            eng.wait_ge(a2_ready, Z_TILES)
            attention("fox", FOX_HEADS, CAUSAL, fox_scores, lambda i, kb: v1[:, kb, i * 64:i * 64 + 64], 64)

            eng.wait_ge(at_oc, FOX_HEADS // 2)
            row_units("out1", 2, a2)

            eng.wait_ge(normed, 4)
            turn("ln2", h2)
            eng.wait_ge(tmp_split, BQ["ln2"] + 16)
            feature("wq", 16, a1)
            eng.wait_ge(s_keys, 16)
            eng.wait_ge(bank_free, 4 * ROUND0["u0"] + 4)
            for tt in range(TT):
                for g in range(4):
                    if tt:
                        eng.wait_ge(sk_copied, 4 * (tt - 1) + g + 1)
                    for i in range(4):
                        last = mm(bank[4 + g][:, i * P:i * P + P], qT[:, 4 * g + i, tt * P:tt * P + P], keys[:, 4 * g + i, :],
                                  start=True, stop=True)
                    last.then_inc(sk_done, 1)
            feature("u0", 16, a1)
            eng.wait_ge(picks_done, TT)
            for n in range(3):
                for tt in range(TT):
                    o = bank[6 + n // 2][:, (n % 2) * T + tt * P:(n % 2) * T + tt * P + P]
                    last = eng.transpose(o, picked[:, tt, n, :], C("ident"))
            last.then_inc(pickT_psum, 1)
            eng.sem_inc(g_mm, 8)
            with eng.Fori(0, T // 8) as b:
                for j in range(8):
                    k = j // 4
                    eng.wait_ge(oh_done, lin(2 * j + 2, (b, 16)))
                    if j % 4 == 0:
                        eng.wait_ge(g_evict, lin(k + 1, (b, 2)))
                    mm(bank[4 + k][:, (j % 4) * P:(j % 4) * P + P], pick_b[:, j, :], pick_a[:, j, :], start=True, stop=True)\
                        .then_inc(g_mm, 1)
            eng.wait_ge(a2_ready, Z_TILES + 16)
            row_units("e0", 2, a2)
            with eng.Fori(0, PEER_ROUNDS - 1) as r:
                feature("u1", 16, a1, r)
                eng.wait_ge(tmp_split, lin(BQ["u1"] + 16, (r, RT)))
                eng.sem_inc(hidden_seen, 1)
                row_units("e1", 2, a2, r)

            eng.wait_ge(normed, 6)
            turn("gmix", norm)
            eng.wait_ge(tmp_split, BQ["gmix"] + 16)
            feature("in2", 32, a1)
            row_units("v2", 1, a1)
            eng.wait_ge(s_rel, 32)
            mm(bank[5][0:ATTN_HEADS, 0:REL], rel_sb[:, :], oneh_sb[:, :], start=True, stop=True).then_inc(s_relT, 1)
            eng.wait_ge(cv_done, 1)
            for i in range(CONV_TILES):
                last = mm(bank[4][:, 0:T], C("ones"), conv[:, i, :], start=i == 0, stop=i == CONV_TILES - 1)
            last.then_inc(mu_done, 1)
            eng.wait_ge(cen_done, 1)
            for i in range(CONV_TILES):
                eng.wait_ge(csq_done, i + 1)
                mm(bank[4][:, 0:T], C("ones"), tmp[:, i % 4, :], start=i == 0, stop=i == CONV_TILES - 1).then_inc(var_done, 1)

            def moba_scores(i, b):
                q, k = inT2[:, 16 + i, :], inT2[:, 24 + i, :]
                mm(b[:, 0:P], q[:, 0:P], k[:, 0:P], start=True, stop=False)
                mm(b[:, 0:P], C("flip"), brev[:, i, P:T], start=False, stop=True)
                mm(b[:, P:3 * P], q[:, P:T], k, start=True, stop=False)
                return mm(b[:, P:3 * P], C("flip"), brev[:, i, :], start=False, stop=True)

            eng.wait_ge(s_brev, 16)
            eng.wait_ge(rv_done, 3)
            eng.wait_ge(a2_ready, Z_TILES + 16 + CONV_TILES)
            attention("moba", ATTN_HEADS, CAUSAL, moba_scores, lambda i, kb: v2[:, kb, i * P:i * P + P], P)
            eng.wait_ge(at_oc, FOX_HEADS // 2 + ATTN_HEADS)
            row_units("out2", 2, a2)

            eng.wait_ge(normed, 8)
            turn("gmem", norm)
            eng.wait_ge(tmp_split, BQ["gmem"] + 16)
            feature("ck", 4, a1)
            u0, r0 = UNIT0["cv"], ROUND0["cv"]
            eng.wait_ge(bank_free, 4 * r0 + 2)
            for j in range(4):
                eng.wait_ge(split_done, u0 + j + 1)
                row_unit(j, bank[0:2], a1, 4 * j, j == 0, j == 3)
            eng.wait_ge(normed, 10)
            turn("gcross", norm)
            eng.wait_ge(tmp_split, BQ["gcross"] + 16)
            feature("cq", 4, a1)

            def cross_scores(i, b):
                mm(b[:, 0:T], cqT[:, i, 0:P], ckT[:, i, :], start=True, stop=True)
                return mm(b[:, T:2 * T], cqT[:, i, P:T], ckT[:, i, :], start=True, stop=True)

            eng.wait_ge(bank_free, 4 * ROUND0["co"] + 4)
            attention("cross", CROSS_HEADS, FULL, cross_scores, lambda i, kb: cv[:, kb, i * P:i * P + P], P)
            eng.wait_ge(at_oc, FOX_HEADS // 2 + ATTN_HEADS + CROSS_HEADS)
            u0, r0 = UNIT0["co"], ROUND0["co"]
            for j in range(4):
                eng.wait_ge(split_done, u0 + j + 1)
                eng.wait_ge(bank_free, 4 * r0 + 2 * j + 2)
                row_unit(j, bank[2 * (j % 2):2 * (j % 2) + 2], a2, 0, True, True)

            eng.wait_ge(normed, 12)
            turn("gmlp", norm)
            eng.wait_ge(tmp_split, BQ["gmlp"] + 16)
            with eng.Fori(0, FF_ROUNDS) as r:
                feature("up0", 16, a1, r)
                eng.wait_ge(tmp_split, lin(BQ["up0"] + 16, (r, RT)))
                eng.sem_inc(hidden_seen, 1)
                row_units("down0", 2, a2, r)


def _feature_units(w):
    k, n = w.shape
    return w.reshape(KT, P, n // P, P).transpose(2, 1, 0, 3).reshape(n // P, P, UNIT)


def _row_units(w):
    k, n = w.shape
    return w.reshape(k // 512, 4, P, n // 512, 512).transpose(3, 0, 2, 1, 4).reshape(-1, P, UNIT)


def _cols(v):
    return v.reshape(-1, P).T


def _bucket(dist):
    dist = np.asarray(dist)
    exact = BUCKETS // 2
    nf = np.maximum(dist, exact).astype(np.float32)
    large = exact + (np.log(nf / np.float32(exact)) / np.float32(np.log(2048 / exact)) * np.float32(BUCKETS - exact)).astype(np.int32)
    return np.where(dist < exact, dist, np.minimum(large, BUCKETS - 1))


def _constants():
    p, c = np.arange(P)[:, None], np.arange(P)[None, :]
    tri = (p <= c).astype(np.float32)
    causal = np.where(p >= c, 0.0, NEG).astype(np.float32)
    consts = np.concatenate([
        np.eye(P, dtype=np.float32), tri, np.ones((P, P), np.float32), -tri, 1 - tri,
        (p + c == P - 1).astype(np.float32), np.zeros((P, P), np.float32), causal,
        np.broadcast_to(np.arange(P, dtype=np.float32), (P, P))], axis=1)
    onehot = np.zeros((BUCKETS, REL), np.float32)
    j = np.arange(REL)
    onehot[_bucket(np.maximum(T - 1 - j, 0)), j] = 1.0
    return np.ascontiguousarray(consts), onehot


def kernel(**inputs):
    import concourse.bacc as bacc
    from concourse.bass_utils import run_bass_kernel_spmd as run

    a = {k: np.asarray(v) for k, v in inputs.items()}
    w_in = a["w_in"]
    z, xbc, dt, q, k, v, f = np.split(w_in, np.cumsum([1024, 1536, 16, 1024, 1024, 1024]), axis=1)
    w2 = a["w_in_2"][0]
    q2, k2, v2, val2, gate2 = np.split(w2, [1024, 2048, 3072, 4096], axis=1)
    up, down = a["w1_2"][0], a["w2_2"][0]
    units = [_feature_units(m) for m in (xbc, z, q, k)] + [_row_units(v), _row_units(a["w_out"]), _feature_units(a["peer_wq"])]
    for r in range(PEER_ROUNDS):
        es = slice(r * D, (r + 1) * D)
        units += [_feature_units(a["peer_u"][es].T), _row_units(a["peer_v"][es])]
    units += [_feature_units(m) for m in (val2, gate2, q2, k2)] + [_row_units(v2), _row_units(a["w_out_2"][0])]
    units += [_feature_units(a["wk_c_2"][0]), _row_units(a["wv_c_2"][0]), _feature_units(a["wq_c_2"][0]), _row_units(a["wo_c_2"][0])]
    for r in range(FF_ROUNDS):
        units += [_feature_units(up[:, r * D:(r + 1) * D]), _row_units(down[r * D:(r + 1) * D])]
    stream = np.concatenate(units, axis=0)
    assert stream.shape[0] == UNITS
    cols = np.concatenate([
        _cols(a["ln1_w"]), _cols(a["g_mix_2"][0]), _cols(a["g_cross_2"][0]), _cols(a["g_mem_2"][0]), _cols(a["g_mlp_2"][0]),
        a["conv_w"].reshape(SSD_CONV, XBC_TILES, P).transpose(2, 1, 0).reshape(P, -1), _cols(a["conv_b"]),
        _cols(a["ssd_norm_w"]), _cols(np.repeat(a["d_skip"], 64)),
        a["conv_w_2"][0].reshape(CONV_K, CONV_TILES, P).transpose(2, 0, 1).reshape(P, -1), _cols(a["conv_b_2"][0]),
        _cols(a["conv_ln_g_2"][0]), _cols(a["conv_ln_b_2"][0])], axis=1)
    consts, onehot = _constants()
    keys = np.stack([a["peer_k1"], a["peer_k2"]], axis=1).reshape(16, PEER_KEYS, P).transpose(2, 0, 1)
    arrays = {
        "x": a["x"].reshape(T, D), "mem": a["mem_2"].reshape(T, D), "stream": stream, "cols": cols, "consts": consts,
        "rows": np.concatenate([a["dt_bias"], a["fox_f_bias"], a["a_log"]])[None, :],
        "wide": np.stack([a["ln2_w"], a["lnf_w"], a["g_final_2"]]),
        "wdtf": np.concatenate([dt, f], axis=1).reshape(KT, P, 32).transpose(1, 0, 2),
        "keys": keys, "rel": a["rel_bias_2"], "onehot": onehot,
    }
    arrays = {f"{n}_dram": np.ascontiguousarray(v) for n, v in arrays.items()}
    nc = bacc.Bacc("TRN2", target_bir_lowering=False, num_devices=1)
    aps = [nc.dram_tensor(n, v.shape, mybir.dt.from_np(v.dtype), kind="ExternalInput").ap() for n, v in arrays.items()]
    aps.append(nc.dram_tensor("out_dram", (T, D), F32, kind="ExternalOutput").ap())
    build(nc, *aps)
    got = run(nc, [arrays], core_ids=[0])
    return got.results[0]["out_dram"].reshape(1, T, D)
```

```python
import numpy as np
import concourse.bass as bass
from concourse import mybir
from concourse.alu_op_type import AluOpType as ALU
from contextlib import ExitStack

F32 = mybir.dt.float32
F32R = mybir.dt.float32r
U32 = mybir.dt.uint32
ACT = mybir.ActivationFunctionType
AX = mybir.AxisListType

P = 128
D = 2048
T = 256
TT = T // P
KT = D // P
UNIT = 2048
EPS = 1e-6
RAW = 4
SPLIT = 2
NEG = -3.0e38

SSD_INNER, SSD_HEADS, SSD_CONV, XBC_TILES, Z_TILES = 1024, 16, 4, 12, 8
FOX_HEADS = 16
PEER_HEADS, PEER_KEYS, TOPK = 8, 128, 16
PICKS = PEER_HEADS * TOPK
TBLOCK, TBLOCKS = 32, T // 32
ATTN_HEADS, CONV_TILES, CONV_K, CROSS_HEADS = 8, 8, 31, 4
BUCKETS, REL = 32, 2 * T - 1
FF_ROUNDS = 4

PEER_ROUNDS = 8
STREAM = [("xbc", "F", 12), ("v1", "R", 8), ("z", "F", 8), ("qk1", "F", 16), ("out1", "R", 16), ("wq", "F", 16)]
for _r in range(PEER_ROUNDS):
    STREAM += [(f"u{_r}", "F", 16), (f"e{_r}", "R", 16)]
STREAM += [("ck", "F", 4), ("cv", "C", 4), ("vg", "F", 16), ("qk2", "F", 16), ("v2", "R", 8), ("out2", "R", 16),
           ("cq", "F", 4), ("co", "O", 4)]
for _r in range(FF_ROUNDS):
    STREAM += [(f"up{_r}", "F", 16), (f"down{_r}", "R", 16)]
OUT2_ORDER = [(0, 0), (1, 0), (0, 1), (1, 1), (0, 2), (1, 2), (0, 3), (1, 3)]
OUT1_ORDER = [(0, 0), (0, 1), (0, 2), (1, 0), (1, 1), (1, 2), (0, 3), (1, 3)]
UNIT0, ROUND0 = {}, {}
_u = _g = 0
for _name, _kind, _n in STREAM:
    UNIT0[_name], ROUND0[_name] = _u, _g
    _u += _n
    _g += {"F": _n // 4, "R": _n // 8, "C": 1, "O": 2}[_kind]
UNITS = _u

COLS = {}
_c = 0
for _name, _n in [(n, KT) for n in ("ln1", "ln2", "gmix", "gcross", "gmem", "gmlp")] + [
                  ("cw1", XBC_TILES * SSD_CONV), ("cb1", XBC_TILES), ("nw1", Z_TILES), ("dskip", Z_TILES),
                  ("cw2", CONV_K * CONV_TILES), ("cb2", CONV_TILES), ("lg2", CONV_TILES), ("lb2", CONV_TILES)]:
    COLS[_name] = (_c, _c + _n)
    _c += _n
NCOLS = _c
CONSTS = {}
_c = 0
for _name, _n in [("ident", P), ("tri", P), ("ones", P), ("ntri", P), ("gt", P), ("flip", P),
                  ("mask", 2 * P), ("iota", P)]:
    CONSTS[_name] = (_c, _c + _n)
    _c += _n
NCONST = _c


class Steps:

    def __init__(self, eng, sem):
        self.eng, self.sem, self.n, self.loops = eng, sem, 0, []

    def did(self, inst):
        inst.then_inc(self.sem, 1)
        self.n += 1

    def wait(self):
        self.eng.wait_ge(self.sem, lin(self.n, *((var, per) for var, per, _ in self.loops)))

    def do(self, inst):
        self.did(inst)
        self.wait()

    def enter(self, var, per):
        self.loops.append((var, per, self.n))

    def leave(self, times):
        _, per, first = self.loops.pop()
        assert self.n - first == per, (self.n - first, per)
        self.n = first + per * times


def lin(const, *terms):
    value = None
    for var, factor in terms:
        if var is None or factor == 0:
            continue
        term = var * factor if factor != 1 else var
        value = term if value is None else value + term
    return const if value is None else value + const


def build(nc, x_in, mem_in, stream, cols_in, consts_in, rows_in, wide_in, wdtf_in, keys_in,
          rel_in, onehot_in, out):
    ctx = ExitStack()
    with ctx:
        base = [-(-nc.sbuf_base // 32) * 32]

        def at(name, shape, dt, offset):
            return nc.alloc_sbuf_tensor_at(name, shape, dt, offset=offset)

        def sb(name, shape, dt=F32):
            size = int(np.prod(shape[1:])) * 4
            t = at(name, shape, dt, base[0])
            base[0] += -(-size // 32) * 32
            return t

        def psum(name):
            return ctx.enter_context(nc.psum_tensor(name, [P, 512], F32))

        def sem(name):
            return ctx.enter_context(nc.semaphore(name))

        raw = sb("raw", [P, RAW, UNIT])
        w_hi = [sb(f"w_hi{i}", [P, UNIT], F32R) for i in range(SPLIT)]
        w_lo = [sb(f"w_lo{i}", [P, UNIT], F32R) for i in range(SPLIT)]
        a1_at = base[0]
        a1 = [sb("a1_hi", [P, KT, T], F32R), sb("a1_lo", [P, KT, T], F32R)]
        a2_at = base[0]
        a2 = [sb("a2_hi", [P, KT, T], F32R), sb("a2_lo", [P, KT, T], F32R)]
        x = sb("x", [P, TT, D])
        work_at = base[0]
        WORK = 47104
        base[0] += WORK
        consts = sb("consts", [P, NCONST])
        cols = sb("cols", [P, NCOLS])
        rows = sb("rows", [P, 48])
        wdtf_at = base[0]
        wdtf = sb("wdtf", [P, KT, 32])
        tmp = sb("tmp", [P, 4, T])
        sp = sb("sp", [P, 6, TT, 32])
        acum = sb("acum", [P, 4, SSD_HEADS])
        stat = sb("stat", [P, 16])
        amax = sb("amax", [P, 4, TT])
        asum = sb("asum", [P, 4, TT])
        assert base[0] <= nc.sbuf_usable_end, (base[0], nc.sbuf_usable_end)

        def C(name, a=0, b=None):
            lo, hi = CONSTS[name]
            return consts[:, lo + a:(hi if b is None else lo + b)]

        def col(name, i):
            return cols[:, COLS[name][0] + i:COLS[name][0] + i + 1]

        inT = at("inT", [P, 36, T], F32, work_at)
        v1 = at("v1", [P, TT, 1024], F32, work_at + 36864)
        rms = at("rms", [P, 2, T], F32, work_at + 45056)
        wd = [at("wd_hi", [P, KT, 32], F32R, work_at + 20480), at("wd_lo", [P, KT, 32], F32R, work_at + 22528)]
        dtf = at("dtf", [32, T], F32, work_at + 24576)
        xdt = at("xdt", [P, TT, SSD_INNER], F32, a2_at)
        cbm = at("cbm", [P, 2, 384], F32, a2_at + 16384)
        seg = at("seg", [P, 2, 384], F32, a2_at + 19456)
        seg_m = at("seg_m", [P, 6, 384], F32, a2_at + 22528)
        fox_p = at("fox_p", [P, 4, 384], F32, work_at + 8192)
        fox_t = at("fox_t", [P, 2, 384], F32, work_at + 14336)
        moba_t = at("moba_t", [P, ATTN_HEADS, 384], F32, work_at + 16384)
        moba_p = at("moba_p", [P, 3, 384], F32, work_at + 28672)
        cross_p = at("cross_p", [P, 2, 512], F32, work_at + 16384)
        cross_t = at("cross_t", [P, 2, 512], F32, work_at + 20480)
        act0 = at("act0", [P, KT, T], F32, work_at)
        wide = at("wide", [P, D], F32, work_at + 16384)
        cand = at("cand", [P, 2, TT, 256], F32, work_at + 24576)
        onehot = at("onehot", [P, PICKS, TOPK], F32, work_at + 24576)
        pick_a = at("pick_a", [P, 8, P], F32, work_at + 24576)
        pick_b = at("pick_b", [P, 8, P], F32, work_at + 28672)
        gbuf = at("gbuf", [P, 4, TBLOCKS, 4 * TBLOCK], F32, work_at + 16384)
        pk = work_at + 32768
        top_v = [at(f"top_v{tt}", [P, 16, TOPK], F32, o) for tt, o in enumerate((pk, wdtf_at))]
        top_i = [at(f"top_i{tt}", [P, 16, TOPK], U32, o + 1024) for tt, o in enumerate((pk, wdtf_at))]
        top_f = at("top_f", [P, 16, TOPK], F32, pk + 2048)
        sc = at("sc", [P, TT, PEER_HEADS, TOPK], F32, pk + 3072)
        pos = [at(f"pos{tt}", [P, PEER_HEADS, TOPK], U32, pk + o) for tt, o in enumerate((4096, 12928))]
        posab = at("posab", [P, 2, PICKS], U32, pk + 4608)
        posf = at("posf", [P, 2, PICKS], F32, pk + 5632)
        picked = at("picked", [P, TT, 3, PICKS], F32, pk + 6656)
        pickT = at("pickT", [P, 3, T], F32, pk + 9728)
        gsum = at("gsum", [P, TT, PEER_HEADS], F32, pk + 12800)
        first = at("first", [P, PEER_HEADS], F32, pk + 12864)
        qT = at("qT", [P, 16, T], F32, a2_at)
        keys = at("keys", [P, 16, P], F32, a2_at + 16384)
        s_sb = [at("s_sb0", [P, 16, P], F32, a2_at + 24576), at("s_sb1", [P, 16, P], F32, work_at + 16384)]
        stage = at("stage", [P, 2, PEER_KEYS, TBLOCK], F32, a2_at)
        brev = at("brev", [P, ATTN_HEADS, T], F32, a1_at)
        gate = at("gate", [P, 2, T], F32, a1_at + 8192)
        relT = at("relT", [ATTN_HEADS, REL + 1], F32, a1_at + 10240)
        oneh_sb = at("oneh_sb", [BUCKETS, REL], F32, a1_at + 12288)
        rel_sb = at("rel_sb", [BUCKETS, ATTN_HEADS], F32, a1_at + 14336)
        q2 = at("q2", [P, ATTN_HEADS, T], F32, a1_at + 16384)
        val = at("val", [P, CONV_TILES, T], F32, a1_at + 24576)
        conv = at("conv", [P, CONV_TILES, T], F32, work_at)
        k2 = at("k2", [P, ATTN_HEADS, T], F32, work_at + 8192)
        v2 = at("v2", [P, TT, 1024], F32, work_at + 8192)
        ln_buf = at("ln_buf", [P, 2, T], F32, wdtf_at)
        mem = at("mem", [P, TT, D], F32, work_at)
        ckT = at("ckT", [P, 4, T], F32, work_at + 34816)
        cv = at("cv", [P, TT, 512], F32, work_at + 38912)
        cqT = at("cqT", [P, 4, T], F32, work_at + 24576)
        norm = at("norm", [P, TT, D], F32, work_at)

        bank = [psum(f"bank{i}") for i in range(8)]

        raw_full = [sem(f"raw_full{i}") for i in range(RAW)]
        hi_done = sem("hi_done")
        split_done = sem("split_done")
        mm_done = sem("mm_done")
        bank_free = sem("bank_free")
        dve_own = sem("dve_own")
        pool_own = sem("pool_own")
        s_x = [sem(f"s_x{tt}") for tt in range(TT)]
        s_small = sem("s_small")
        s_rel = sem("s_rel")
        sq_done = sem("sq_done")
        rs_done = sem("rs_done")
        normed = sem("normed")
        tr_done = sem("tr_done")
        tmp_full = sem("tmp_full")
        tmp_split = sem("tmp_split")
        a2_ready = sem("a2_ready")
        wd_done = sem("wd_done")
        s_sp = sem("s_sp")
        dtf_done = sem("dtf_done")
        sp_dve = sem("sp_dve")
        sp_act = sem("sp_act")
        s_cum = sem("s_cum")
        cum_dve = sem("cum_dve")
        conv_done = sem("conv_done")
        xbc_done = sem("xbc_done")
        cb_done = sem("cb_done")
        cbm_done = sem("cbm_done")
        xs_done = sem("xs_done")
        xdt_done = sem("xdt_done")
        arow_done = sem("arow_done")
        seg_done = sem("seg_done")
        exp_done = sem("exp_done")
        m_done = sem("m_done")
        y_done = sem("y_done")
        y_out = sem("y_out")
        ysq_done = sem("ysq_done")
        ms_done = sem("ms_done")
        rv_done = sem("rv_done")
        rt_done = sem("rt_done")
        at_s = sem("at_s")
        at_max = sem("at_max")
        at_exp = sem("at_exp")
        at_p = sem("at_p")
        at_t = sem("at_t")
        at_tc = sem("at_tc")
        at_o = sem("at_o")
        at_oc = sem("at_oc")
        resid = sem("resid")
        s_wide = sem("s_wide")
        s_keys = sem("s_keys")
        sk_done = sem("sk_done")
        sk_copied = sem("sk_copied")
        sm_dve = sem("sm_dve")
        sm_act = sem("sm_act")
        picks_done = sem("picks_done")
        pickT_psum = sem("pickT_psum")
        oha_done = sem("oha_done")
        ohb_done = sem("ohb_done")
        g_mm = sem("g_mm")
        g_evict = sem("g_evict")
        g_write = [sem(f"g_write{i}") for i in range(2)]
        g_early = sem("g_early")
        g_full = sem("g_full")
        g_used = sem("g_used")
        s_relT = sem("s_relT")
        relT_done = sem("relT_done")
        s_relw = sem("s_relw")
        s_brev = sem("s_brev")
        gated = sem("gated")
        cv_done = sem("cv_done")
        mu_done = sem("mu_done")
        cen_done = sem("cen_done")
        csq_done = sem("csq_done")
        var_done = sem("var_done")
        cn_done = sem("cn_done")
        cn_silu = sem("cn_silu")
        cn_hi = sem("cn_hi")
        seg_raw = sem("seg_raw")
        s_mem = sem("s_mem")
        s_out = sem("s_out")
        fin = sem("fin")

        gates_d = nc.dram_tensor("gates_scratch", (TBLOCKS, P, PEER_KEYS * TBLOCK), F32, kind="Internal").ap()
        rel_d = nc.dram_tensor("rel_scratch", (ATTN_HEADS, 512), F32, kind="Internal").ap()

        NORMS = ["ln1", "ln2", "gmem", "lnf", "gmix", "gcross", "gmlp", "final"]
        NQ = {n: i for i, n in enumerate(NORMS)}
        BUILDS = ["ln1", "ln2"] + [f"u{r}" for r in range(1, PEER_ROUNDS)] + ["gmem", "gmix", "gcross", "gmlp"]
        BUILDS += [f"up{r}" for r in range(FF_ROUNDS)]
        BQ = {n: 16 * i for i, n in enumerate(BUILDS)}
        TRQ = {n: 16 * i for i, n in enumerate(n for n in BUILDS if n[0] != "u")}
        BUILT = {n: a2 if n == "gmix" else a1 for n in NORMS}
        RU, RB, RT = 32, 24, 16
        HEAD0 = {"fox": 0, "moba": FOX_HEADS, "cross": FOX_HEADS + ATTN_HEADS}
        CAUSAL = dict(segs=[(0, P), (P, 2 * P)], turns=[(0, 0), (P, P), (2 * P, 2 * P)],
                      pv=[(0, 0, 2 * P, 0), (1, 2 * P, P, P)], width=3 * P)
        FULL = dict(segs=[(0, 2 * P), (2 * P, 2 * P)], turns=[(0, 0), (2 * P, P), (P, 2 * P), (3 * P, 3 * P)],
                    pv=[(0, 0, 2 * P, 0), (1, 2 * P, 2 * P, 0)], width=4 * P)
        FOX = dict(CAUSAL, name="fox", heads=FOX_HEADS, d=64, masked=True, p=fox_p, slots=4, t=fox_t, t_slots=2,
                   s_banks=[4], o_banks=[7, 5], heads_out=2, dst=a2, kt=Z_TILES)
        MOBA = dict(CAUSAL, name="moba", heads=ATTN_HEADS, d=P, masked=True, p=moba_p, slots=3, t=moba_t, t_slots=8,
                    s_banks=[4], o_banks=[7, 4], heads_out=1, dst=a1, kt=0)
        CROSS = dict(FULL, name="cross", heads=CROSS_HEADS, d=P, masked=False, p=cross_p, slots=2, t=cross_t, t_slots=2,
                     s_banks=[4, 5], o_banks=[7], heads_out=1, dst=a2, kt=0)
        OUT0 = {"fox": 0, "moba": FOX_HEADS // 2, "cross": FOX_HEADS // 2 + ATTN_HEADS}

        MIX_STEPS = 38
        MIX_ORDER = [8, 9, 10, 11, 0, 1, 2, 3, 4, 5, 6, 7]
        SSD_AT = 8
        FOX_AT = 19

        MIX2_STEPS = 48
        HEAD2_AT = 18
        OUT2_AT = {37: (0, 1), 38: (2, 3), 41: (4, 5, 6, 7)}
        KEYS_AT = {2 * h + 3: h for h in range(PEER_HEADS)}
        WQ_STEPS = 18
        CROSS_STEPS = CROSS_HEADS + 4
        TAP_ORDER = [(i, d) for p in range(0, CONV_TILES, 2) for d in range(CONV_K) for i in (p, p + 1)]
        TAPS = [0] * 4 + [8] * 14 + [6] * 16 + [8] * 5 + [0] * 9
        assert len(TAPS) == MIX2_STEPS and sum(TAPS) == CONV_TILES * CONV_K
        TAPS_TO = [sum(TAPS[:s]) for s in range(MIX2_STEPS + 1)]
        CONV_END = [next(s for s in range(MIX2_STEPS) if TAPS_TO[s + 1] > TAP_ORDER.index((i, CONV_K - 1)))
                    for i in range(CONV_TILES)]
        LN_AT = CONV_END[-1] + 1

        block = ctx.enter_context(nc.Block())

        @block.sync
        def _(sp_eng):
            eng = nc.sync
            for tt in range(TT):
                eng.dma_start(x[:, tt, :], x_in[tt * P:(tt + 1) * P, :]).then_inc(s_x[tt], 16)
            for j in range(RAW):
                eng.dma_start(raw[:, j, :], stream[j, :, :]).then_inc(raw_full[j], 16)
            with eng.Fori(1, UNITS // RAW) as g:
                for j in range(RAW):
                    eng.wait_ge(split_done, g * RAW + (j - RAW + 1))
                    eng.dma_start(raw[:, j, :], stream[bass.ds(g * RAW + j, 1), :, :].rearrange("a p n -> p (a n)"))\
                        .then_inc(raw_full[j], 16)
            for tt in range(TT):
                eng.wait_ge(fin, tt + 1)
                eng.dma_start(out[tt * P:(tt + 1) * P, :], x[:, tt, :]).then_inc(s_out, 16)
            eng.wait_ge(s_out, 32)

        @block.gpsimd
        def _(pool):
            eng = nc.gpsimd
            own = Steps(eng, pool_own)
            eng.dma_start(consts[:, :], consts_in).then_inc(s_small, 16)
            eng.dma_start(cols[:, :], cols_in).then_inc(s_small, 16)
            eng.dma_start(rows[:, :], rows_in.partition_broadcast(P)).then_inc(s_small, 16)
            eng.dma_start(wdtf[:, :, :], wdtf_in).then_inc(s_small, 16)
            own.do(eng.memset(stat[:, 12:14], -0.5))

            def rsqrt(name):
                eng.wait_ge(sq_done, TT * (NQ[name] + 1))
                own.do(eng.tensor_scalar(stat[:, 4:6], stat[:, 0:2], 1.0 / D, EPS, ALU.mult, ALU.add))
                eng.tensor_tensor(stat[:, 2:4], stat[:, 4:6], stat[:, 12:14], ALU.pow).then_inc(rs_done, 1)

            rsqrt("ln1")
            rsqrt("ln2")
            eng.wait_ge(mm_done, UNIT0["wq"])
            eng.dma_start(keys[:, :, :], keys_in).then_inc(s_keys, 16)

            def load_gates(r, g):
                src = gates_d[:, :, bass.ds(lin(0, (r, 16 * TBLOCK), (g, 4 * TBLOCK)), 4 * TBLOCK)]
                eng.dma_start(gbuf[:, bass.ds(g, 1), :, :].rearrange("p a b n -> p (a b) n"),
                              src.rearrange("b p n -> p b n")).then_inc(g_full, 16)

            for i in range(2):
                eng.wait_ge(g_write[i], 16 * (TBLOCKS // 2 + 1))
            with eng.Fori(2, 4) as g:
                load_gates(None, g)
                eng.wait_ge(g_full, lin(-16, (g, 16)))
            with eng.Fori(1, PEER_ROUNDS) as r:
                with eng.Fori(0, 4) as g:
                    eng.wait_ge(g_used, lin(4 - 16, (r, 16), (g, 4)))
                    load_gates(r, g)
                    eng.wait_ge(g_full, lin(-16, (r, 64), (g, 16)))
            eng.dma_start(mem[:, :, :], mem_in.rearrange("(t p) d -> p t d", p=P)).then_inc(s_mem, 16)
            eng.wait_ge(g_used, 16 * PEER_ROUNDS)
            eng.dma_start(wide[:, :], wide_in[0:1, :].partition_broadcast(P)).then_inc(s_wide, 16)
            rsqrt("gmem")
            rsqrt("lnf")
            rsqrt("gmix")
            eng.wait_ge(mm_done, UNIT0["vg"] + 1)
            eng.dma_start(rel_sb[:, :], rel_in).then_inc(s_rel, 16)
            eng.dma_start(oneh_sb[:, :], onehot_in).then_inc(s_rel, 16)
            eng.wait_ge(relT_done, 1)
            eng.dma_start(rel_d[:, 0:REL], relT[:, 0:REL]).then_inc(s_relw, 16)
            eng.wait_ge(s_relw, 16)
            hankel = bass.AP(tensor=rel_d.tensor, offset=0, ap=[[1, P], [512, ATTN_HEADS], [1, T]])
            eng.dma_start(brev[:, :, :], hankel).then_inc(s_brev, 16)
            rsqrt("gcross")
            rsqrt("gmlp")
            eng.wait_ge(mm_done, UNIT0["up0"] + 1)
            eng.dma_start(wide[:, :], wide_in[1:2, :].partition_broadcast(P)).then_inc(s_wide, 16)
            rsqrt("final")

        @block.scalar
        def _(act):
            eng = nc.scalar

            def hi(landed, k):
                eng.wait_ge(raw_full[k % RAW], landed)
                eng.activation(w_hi[k % SPLIT][:, :], raw[:, k % RAW, :], ACT.Copy).then_inc(hi_done, 1)

            def ahead(u, *loops):
                k = u + 2
                eng.wait_ge(mm_done, lin(u + 1, *loops))
                hi(lin(16 * (k // RAW + 1), *((v, n * 16 // RAW) for v, n in loops)), k)

            def feature(name, n, first, evict, r=None, unroll=False):
                u0 = UNIT0[name] + first
                if unroll:
                    for k in range(n):
                        eng.wait_ge(mm_done, lin(u0 + k + 1, (r, RU)))
                        if k == 0:
                            ahead(u0 + k, (r, RU))
                        evict(k // 4, k % 4)
                        if k > 0:
                            ahead(u0 + k, (r, RU))
                    return
                with eng.Fori(0, n // 4) as g:
                    for j in range(4):
                        eng.wait_ge(mm_done, lin(u0 + j + 1, (r, RU), (g, 4)))
                        evict(g, j)
                        ahead(u0 + j, (r, RU), (g, 4))

            def row_units(name, pairs, evict=None, last=False, r=None, skip=0):
                u0 = UNIT0[name] + 8 * skip
                loops = pairs - 1 if last else pairs
                with eng.Fori(0, loops) as g:
                    for j in range(8):
                        ahead(u0 + j, (r, RU), (g, 8))
                        if evict and j % 4 == 3:
                            evict(g, j // 4)
                if last:
                    for j in range(6):
                        ahead(u0 + 8 * loops + j)

            def square(name, src, tt):
                junk = junk_early if name in ("ln1", "ln2", "gmem") else junk_late
                eng.activation(junk[:, :], src[:, tt, :], ACT.Square, accum_out=stat[:, tt:tt + 1]).then_inc(sq_done, 1)
                eng.wait_ge(sq_done, TT * NQ[name] + tt + 1)

            def squares(name, src):
                for tt in range(TT):
                    square(name, src, tt)

            def scaled_tile(name, kt):
                eng.wait_ge(tr_done, TRQ[name] + kt + 1)
                eng.activation(BUILT[name][0][:, kt, :], bank[4 + kt % 4][:, 0:T], ACT.Copy, scale=col(name, kt))\
                    .then_inc(tmp_full, 1)

            def scaled_tiles(name):
                for kt in range(KT):
                    scaled_tile(name, kt)

            def head_exp(a, i):
                h = HEAD0[a["name"]] + i
                eng.wait_ge(at_max, h + 1)
                for q, (c, n) in enumerate(a["segs"]):
                    dst = a["p"][:, i % a["slots"], c:c + n]
                    src = dst if a["masked"] else bank[a["s_banks"][i % 2]][:, c:c + n]
                    eng.activation(dst, src, ACT.Exp, bias=amax[:, i % 4, q:q + 1],
                                   accum_out=asum[:, i % 4, q:q + 1]).then_inc(at_exp, 1)

            def head_copy(a, i):
                h = HEAD0[a["name"]] + i
                eng.wait_ge(at_t, h + 1)
                if i >= a["t_slots"]:
                    eng.wait_ge(at_o, h - a["t_slots"] + 1)
                eng.activation(a["t"][:, i % a["t_slots"], 0:a["width"]], bank[6][:, 0:a["width"]], ACT.Copy).then_inc(at_tc, 1)

            junk_early = at("junk_early", [P, D], F32, work_at + 36864)
            junk_late = at("junk_late", [P, D], F32, a2_at)
            for tt in range(TT):
                eng.wait_ge(s_x[tt], 16)
                square("ln1", x, tt)
            eng.sem_inc(bank_free, 4)
            for j in range(SPLIT):
                hi(16, j)
            eng.wait_ge(s_small, 64)
            eng.activation(wd[0][:, :, :], wdtf[:, :, :], ACT.Copy).then_inc(wd_done, 1)
            scaled_tiles("ln1")
            eng.wait_ge(s_sp, 1)
            eng.activation(dtf[:, :], bank[6][0:32, 0:T], ACT.Copy).then_inc(dtf_done, 1)

            eng.wait_ge(sp_dve, 1)
            eng.activation(sp[:, 1, :, :], sp[:, 2, :, :], ACT.Exp).then_inc(sp_act, 1)
            eng.activation(rows[:, 32:48], rows[:, 32:48], ACT.Exp).then_inc(sp_act, 1)
            eng.wait_ge(sp_dve, 2)
            eng.activation(sp[:, 3, :, :], sp[:, 2, :, :], ACT.Ln).then_inc(sp_act, 1)

            feature("xbc", 12, 0, lambda g, j: eng.activation(
                inT[:, bass.ds(g * 4 + j, 1), :].rearrange("p a t -> p (a t)"), bank[j][:, 0:T], ACT.Copy)
                .then_inc(bank_free, 1))

            def mix_unit(s):
                u = UNIT0["v1"] + s
                eng.wait_ge(mm_done, u + 1)
                if s < 8:
                    if s % 4 == 3:
                        for tt in range(TT):
                            eng.activation(v1[:, tt, (s // 4) * 512:(s // 4) * 512 + 512], bank[2 * (s // 4) + tt][:, :],
                                           ACT.Copy).then_inc(bank_free, 1)
                elif s < 16:
                    eng.activation(inT[:, 4 + s, :], bank[s % 4][:, 0:T], ACT.Silu).then_inc(bank_free, 1)
                elif s < 32:
                    eng.activation(inT[:, 4 + s, :], bank[s % 4][:, 0:T], ACT.Copy, scale=64 ** -0.5 if s % 2 == 0 else 1.0)\
                        .then_inc(bank_free, 1)
                ahead(u)

            for s in range(MIX_STEPS):
                if 1 <= s <= 6:
                    for n in (2 * s - 2, 2 * s - 1):
                        i = MIX_ORDER[n]
                        eng.wait_ge(conv_done, n + 1)
                        eng.activation(inT[:, i, :], tmp[:, n % 4, :], ACT.Silu, bias=col("cb1", i)).then_inc(xbc_done, 1)
                n = s - SSD_AT - 1
                if 0 <= n < SSD_HEADS // 2:
                    for h in (2 * n, 2 * n + 1):
                        eng.wait_ge(seg_done, h + 1)
                        eng.activation(seg[:, h % 2, :], seg[:, h % 2, :], ACT.Exp).then_inc(exp_done, 1)
                i = s - 14
                if 0 <= i < Z_TILES:
                    eng.wait_ge(y_out, i + 1)
                    if i >= 4:
                        eng.wait_ge(ms_done, i - 3)
                    eng.activation(tmp[:, i % 4, :], inT[:, i, :], ACT.Square).then_inc(ysq_done, 1)
                if s == 24:
                    for g in range(2):
                        eng.wait_ge(rv_done, g + 1)
                        eng.activation(rms[:, g, :], rms[:, g, :], ACT.Sqrt).then_inc(rt_done, 1)
                if 0 <= s - FOX_AT - 1 < FOX_HEADS:
                    head_exp(FOX, s - FOX_AT - 1)
                if 0 <= s - FOX_AT - 2 < FOX_HEADS:
                    head_copy(FOX, s - FOX_AT - 2)
                mix_unit(s)
            for j in range(6, 8):
                ahead(UNIT0["out1"] + j)
            for j in range(8, 15):
                ahead(UNIT0["out1"] + j)

            eng.wait_ge(resid, 2)
            squares("ln2", x)
            ahead(UNIT0["out1"] + 15)
            scaled_tiles("ln2")

            for s in range(WQ_STEPS):
                if s in KEYS_AT:
                    h = KEYS_AT[s]
                    eng.wait_ge(sk_done, h + 1)
                    for tt in range(TT):
                        eng.activation(s_sb[tt][:, 2 * h:2 * h + 2, :], bank[4 + h % 4][:, tt * T:tt * T + T]
                                       .rearrange("p (a n) -> p a n", a=2), ACT.Copy).then_inc(sk_copied, 1)
                if s < 16:
                    eng.wait_ge(mm_done, UNIT0["wq"] + s + 1)
                    eng.activation(qT[:, s, :], bank[s % 4][:, 0:T], ACT.Copy).then_inc(bank_free, 1)
                    ahead(UNIT0["wq"] + s)

            def gelu0(g, j):
                eng.activation(act0[:, bass.ds(g * 4 + j, 1), :].rearrange("p a t -> p (a t)"),
                               bank[j][:, 0:T], ACT.Gelu).then_inc(bank_free, 1)
            feature("u0", 16, 0, gelu0, unroll=True)
            for tt in range(TT):
                eng.wait_ge(sm_dve, tt + 1)
                eng.activation(sc[:, tt, :, :], sc[:, tt, :, :], ACT.Exp).then_inc(sm_act, 1)

            for i in range(2):
                eng.sem_inc(g_write[i], 16)
            eng.sem_inc(g_evict, 2)
            with eng.Fori(0, TBLOCKS // 2) as pair:
                for half in range(2):
                    eng.wait_ge(g_write[half], lin(16, (pair, 16)))
                    with eng.Fori(0, TBLOCK // 8) as b:
                        for k in range(2):
                            eng.wait_ge(g_mm, lin(8 + half * TBLOCK + 4 * k + 4, (pair, 2 * TBLOCK), (b, 8)))
                            eng.activation(stage[:, half, :, bass.ds(lin(4 * k, (b, 8)), 4)].rearrange("p n t -> p t n"),
                                           bank[4 + k][:, :].rearrange("p (t n) -> p t n", t=4), ACT.Copy)\
                                .then_inc(g_evict, 1)
                    eng.wait_ge(g_evict, lin(2 + (half + 1) * (TBLOCK // 4), (pair, TBLOCK // 2)))
                    eng.dma_start(gates_d[bass.ds(lin(half, (pair, 2)), 1), :, :].rearrange("b p n -> p (b n)"),
                                  stage[:, half, :, :].rearrange("p n t -> p (n t)")).then_inc(g_write[half], 16)
                    eng.activation(gbuf[:, 0:2, bass.ds(lin(half, (pair, 2)), 1), :].rearrange("p g b n -> p (g b) n"),
                                   stage[:, half, 0:8, :].rearrange("p (g n) t -> p g (n t)", g=2), ACT.Copy)\
                        .then_inc(g_early, 1)
            row_units("e0", 2)

            def gelu(r):
                def evict(g, j):
                    eng.wait_ge(tmp_split, lin(BQ["u1"] + j - 3, (r, RT), (g, 4)))
                    eng.activation(tmp[:, j, :], bank[j][:, 0:T], ACT.Gelu).then_inc(tmp_full, 1)
                    eng.wait_ge(tmp_full, lin(BQ["u1"] + j + 1, (r, RT), (g, 4)))
                    eng.sem_inc(bank_free, 1)
                return evict
            with eng.Fori(0, PEER_ROUNDS - 2) as r:
                feature("u1", 16, 0, gelu(r), r, unroll=True)
                row_units("e1", 2, r=r)
            feature("u7", 16, 0, gelu(PEER_ROUNDS - 2), unroll=True)
            for j in range(16):
                if j in (1, 2):
                    eng.wait_ge(s_mem, 16)
                    square("gmem", mem, j - 1)
                if 5 <= j < 13:
                    scaled_tile("gmem", 2 * (j - 5))
                    scaled_tile("gmem", 2 * (j - 5) + 1)
                ahead(UNIT0["e7"] + j)

            eng.wait_ge(resid, 4)
            squares("lnf", x)
            for j in range(8):
                if j == 2:
                    eng.wait_ge(resid, 6)
                    squares("gmix", x)
                if j >= 4:
                    for kt in range(4 * (j - 4), 4 * (j - 4) + 4):
                        scaled_tile("gmix", kt)
                eng.wait_ge(mm_done, UNIT0["ck"] + j + 1)
                if j < 4:
                    eng.activation(ckT[:, j, :], bank[j][:, 0:T], ACT.Copy).then_inc(bank_free, 1)
                ahead(UNIT0["ck"] + j)
            for tt in range(TT):
                eng.activation(cv[:, tt, :], bank[tt][:, :], ACT.Copy).then_inc(bank_free, 1 + 2 * tt)

            def mix2_unit(s):
                u = UNIT0["vg"] + s
                eng.wait_ge(mm_done, u + 1)
                i = (s % 16) // 2
                if s < 16 and s % 2 == 0:
                    eng.activation(val[:, i, :], bank[s % 4][:, 0:T], ACT.Copy).then_inc(bank_free, 1)
                elif s < 16:
                    if i >= 2:
                        eng.wait_ge(gated, i - 1)
                    eng.activation(gate[:, i % 2, :], bank[s % 4][:, 0:T], ACT.Sigmoid).then_inc(bank_free, 1)
                elif s < 32 and s % 2 == 0:
                    eng.activation(q2[:, i, :], bank[s % 4][:, 0:T], ACT.Copy, scale=128 ** -0.5).then_inc(bank_free, 1)
                elif s < 32:
                    eng.activation(k2[:, i, :], bank[s % 4][:, 0:T], ACT.Copy).then_inc(bank_free, 1)
                elif s in (35, 39):
                    c = (s - 32) // 4
                    if c == 0:
                        eng.wait_ge(at_s, HEAD0["moba"] + ATTN_HEADS)
                    for tt in range(TT):
                        eng.activation(v2[:, tt, c * 512:c * 512 + 512], bank[2 * c + tt][:, :], ACT.Copy)\
                            .then_inc(bank_free, 1)
                ahead(u)

            for s in range(MIX2_STEPS):
                if s == 5:
                    eng.wait_ge(s_relT, 1)
                    eng.activation(relT[:, 0:REL], bank[5][0:ATTN_HEADS, 0:REL], ACT.Copy).then_inc(relT_done, 1)
                i = s - HEAD2_AT
                if i % 2 == 1 and 0 <= i // 2 < ATTN_HEADS:
                    head_exp(MOBA, i // 2)
                if i % 2 == 0 and 0 <= i // 2 - 1 < ATTN_HEADS:
                    head_copy(MOBA, i // 2 - 1)
                if s == LN_AT + 1:
                    for i in range(CONV_TILES):
                        eng.wait_ge(cen_done, i + 1)
                        eng.activation(val[:, i, :], conv[:, i, :], ACT.Square).then_inc(csq_done, 1)
                if s == LN_AT + 2:
                    eng.wait_ge(rv_done, 3)
                    eng.activation(ln_buf[:, 0, :], ln_buf[:, 0, :], ACT.Sqrt).then_inc(rt_done, 1)
                for n in (3, 4):
                    for i in range(4 * (n - 3), 4 * (n - 3) + 4) if s == LN_AT + n else ():
                        eng.wait_ge(cn_done, i + 1)
                        eng.activation(conv[:, i, :], conv[:, i, :], ACT.Silu, scale=col("lg2", i), bias=col("lb2", i))\
                            .then_inc(cn_silu, 1)
                for n in (4, 5):
                    for i in range(4 * (n - 4), 4 * (n - 4) + 4) if s == LN_AT + n else ():
                        eng.wait_ge(cn_silu, i + 1)
                        eng.activation(a1[0][:, ATTN_HEADS + i, :], conv[:, i, :], ACT.Copy).then_inc(cn_hi, 1)
                mix2_unit(s)
            for j in range(8, 15):
                ahead(UNIT0["out2"] + j)

            eng.wait_ge(resid, 8)
            squares("gcross", x)
            ahead(UNIT0["out2"] + 15)
            scaled_tiles("gcross")
            for s in range(CROSS_STEPS):
                if 0 <= s - 2 < CROSS_HEADS:
                    head_exp(CROSS, s - 2)
                if 0 <= s - 3 < CROSS_HEADS:
                    head_copy(CROSS, s - 3)
                if s < CROSS_HEADS:
                    eng.wait_ge(mm_done, UNIT0["cq"] + s + 1)
                    eng.activation(cqT[:, s, :], bank[s][:, 0:T], ACT.Copy, scale=128 ** -0.5).then_inc(bank_free, 1)
                    ahead(UNIT0["cq"] + s)
            for j in range(4):
                if j == 3:
                    eng.wait_ge(resid, 10)
                    squares("gmlp", x)
                ahead(UNIT0["co"] + j)
            scaled_tiles("gmlp")

            def relu(r, n0):
                def evict(g, j):
                    eng.wait_ge(tmp_split, lin(n0 + j - 3, (r, RT), (g, 4)))
                    eng.activation(tmp[:, j, :], bank[j][:, 0:T], ACT.Relu).then_inc(tmp_full, 1)
                    eng.wait_ge(tmp_full, lin(n0 + j + 1, (r, RT), (g, 4)))
                    eng.sem_inc(bank_free, 1)
                return evict
            with eng.Fori(0, FF_ROUNDS - 1) as r:
                feature("up0", 16, 0, relu(r, BQ["up0"]), r)
                row_units("down0", 2, r=r)
            feature(f"up{FF_ROUNDS - 1}", 16, 0, relu(None, BQ[f"up{FF_ROUNDS - 1}"]))
            row_units(f"down{FF_ROUNDS - 1}", 2, last=True)
            eng.wait_ge(resid, 12)
            squares("final", x)

        @block.vector
        def _(dve):
            eng = nc.vector
            own = Steps(eng, dve_own)

            def lo(done, k):
                eng.wait_ge(hi_done, done)
                eng.tensor_tensor(w_lo[k % SPLIT][:, :], raw[:, k % RAW, :], w_hi[k % SPLIT][:, :].bitcast(F32),
                                  ALU.subtract).then_inc(split_done, 1)

            def ahead(u, *loops):
                lo(lin(u + 3, *loops), u + 2)

            def split(dst, kt, src, sig, ap=None):
                h = dst[0][:, kt, :] if ap is None else dst[0][:, ap, :].rearrange("p a t -> p (a t)")
                l = dst[1][:, kt, :] if ap is None else dst[1][:, ap, :].rearrange("p a t -> p (a t)")
                own.do(eng.tensor_copy(h, src))
                eng.tensor_tensor(l, src, h.bitcast(F32), ALU.subtract).then_inc(sig, 1)

            def scaled_lo(name, kt):
                dst = BUILT[name]
                eng.wait_ge(tmp_full, BQ[name] + kt + 1)
                eng.scalar_tensor_tensor(dst[1][:, kt, :], bank[4 + kt % 4][:, 0:T], col(name, kt),
                                         dst[0][:, kt, :].bitcast(F32), ALU.mult, ALU.subtract).then_inc(tmp_split, 1)

            def scaled_los(name):
                for kt in range(KT):
                    scaled_lo(name, kt)

            def feature(name, n, first=0, extra=None, steps=0, r=None):
                u0 = UNIT0[name] + first
                with eng.Fori(0, n // 4) as g:
                    own.enter(g, steps)
                    for j in range(4):
                        if j == 0:
                            ahead(u0 + j, (r, RU), (g, 4))
                        if extra:
                            extra(g, j)
                        if j > 0:
                            ahead(u0 + j, (r, RU), (g, 4))
                    own.leave(n // 4)

            def add_chunk(c, pair, done):
                eng.wait_ge(mm_done, done)
                for tt in range(TT):
                    xs = x[:, tt, bass.ds(c, 512)]
                    eng.tensor_tensor(xs, bank[2 * pair + tt][:, :], xs, ALU.add).then_inc(bank_free, 1)

            def row_units(name, pairs, add=True, last=False, r=None, skip=0):
                u0 = UNIT0[name] + 8 * skip
                loops = pairs - 1 if last else pairs
                with eng.Fori(0, loops) as g:
                    for j in range(8):
                        if add and j % 4 == 3:
                            add_chunk(lin((j // 4) * 512 + 1024 * skip, (g, 1024)), j // 4, lin(u0 + j + 1, (r, RU), (g, 8)))
                        ahead(u0 + j, (r, RU), (g, 8))
                if last:
                    for j in range(8):
                        if j < 6:
                            ahead(u0 + 8 * loops + j)
                        if j % 4 == 3:
                            add_chunk(loops * 1024 + (j // 4) * 512, j // 4, u0 + 8 * loops + j + 1)

            def resid_ready():
                own.do(eng.memset(stat[:, 8:9], 0.0))
                eng.memset(stat[:, 9:10], 0.0).then_inc(resid, 2)

            def normalise(name, src, dst, wide_n=None):
                eng.wait_ge(rs_done, NQ[name] + 1)
                if wide_n:
                    eng.wait_ge(s_wide, 16 * wide_n)
                for tt in range(TT):
                    if wide_n:
                        i = eng.scalar_tensor_tensor(dst[:, tt, :], src[:, tt, :], stat[:, 2 + tt:3 + tt], wide[:, :],
                                                     ALU.mult, ALU.mult)
                    else:
                        i = eng.tensor_scalar(dst[:, tt, :], src[:, tt, :], stat[:, 2 + tt:3 + tt], None, ALU.mult)
                    i.then_inc(fin if name == "final" else (resid if name == "lnf" else normed), 1)

            def head_max(a, i):
                h, slot = HEAD0[a["name"]] + i, i % a["slots"]
                b = bank[a["s_banks"][i % len(a["s_banks"])]]
                eng.wait_ge(at_s, h + 1)
                if i >= a["slots"]:
                    eng.wait_ge(at_t, h - a["slots"] + 1)
                for q, (c, n) in enumerate(a["segs"]):
                    m = amax[:, i % 4, q:q + 1]
                    if a["masked"]:
                        own.did(eng.tensor_tensor_reduce(a["p"][:, slot, c:c + n], b[:, c:c + n], C("mask", 2 * P - n),
                                                         1.0, NEG, ALU.add, ALU.max, m))
                    else:
                        own.did(eng.tensor_reduce(m, b[:, c:c + n], AX.X, ALU.max))
                own.wait()
                eng.tensor_scalar(amax[:, i % 4, :], amax[:, i % 4, :], -1.0, None, ALU.mult).then_inc(at_max, 1)

            def head_norm(a, i):
                h, slot = HEAD0[a["name"]] + i, i % a["slots"]
                eng.wait_ge(at_exp, 2 * (h + 1))
                own.do(eng.reciprocal(asum[:, i % 4, :], asum[:, i % 4, :]))
                for q, (c, n) in enumerate(a["segs"]):
                    eng.tensor_scalar(a["p"][:, slot, c:c + n], a["p"][:, slot, c:c + n], asum[:, i % 4, q:q + 1],
                                      None, ALU.mult).then_inc(at_p, 1)

            def out_split(a, k):
                eng.wait_ge(at_o, HEAD0[a["name"]] + (k + 1) * a["heads_out"])
                split(a["dst"], a["kt"] + k, bank[a["o_banks"][k % len(a["o_banks"])]][:, 0:T], at_oc)

            for j in range(SPLIT):
                lo(j + 1, j)
            normalise("ln1", x, norm)
            eng.wait_ge(wd_done, 1)
            eng.tensor_tensor(wd[1][:, :, :], wdtf[:, :, :], wd[0][:, :, :].bitcast(F32), ALU.subtract).then_inc(wd_done, 1)
            scaled_los("ln1")

            eng.wait_ge(s_sp, 2)
            for tt in range(TT):
                own.did(eng.tensor_tensor(sp[:, 0, tt, :], bank[7][:, 32 * tt:32 * tt + 32], rows[:, 0:32], ALU.add))
            own.wait()
            own.do(eng.tensor_scalar(sp[:, 0, :, 16:32], sp[:, 0, :, 16:32], -1.0, None, ALU.mult))
            eng.scalar_tensor_tensor(sp[:, 2, :, :], sp[:, 0, :, :], -1.0, sp[:, 0, :, :], ALU.mult, ALU.min).then_inc(sp_dve, 1)
            eng.wait_ge(sp_act, 1)
            eng.tensor_scalar(sp[:, 2, :, :], sp[:, 1, :, :], 1.0, None, ALU.add).then_inc(sp_dve, 1)
            eng.wait_ge(sp_dve, 2)
            own.do(eng.tensor_scalar(sp[:, 4, :, :], sp[:, 2, :, :], -1.0, None, ALU.add))
            own.did(eng.tensor_scalar(sp[:, 5, :, :], sp[:, 4, :, :], 1e-30, None, ALU.max))
            own.wait()
            own.do(eng.reciprocal(sp[:, 5, :, :], sp[:, 5, :, :]))
            own.do(eng.tensor_tensor(sp[:, 5, :, :], sp[:, 5, :, :], sp[:, 1, :, :], ALU.mult))
            eng.wait_ge(sp_act, 3)
            own.do(eng.tensor_tensor(sp[:, 5, :, :], sp[:, 5, :, :], sp[:, 3, :, :], ALU.mult))
            own.do(eng.scalar_tensor_tensor(sp[:, 4, :, :], sp[:, 4, :, :], 0.0, sp[:, 1, :, :], ALU.is_equal, ALU.mult))
            own.do(eng.tensor_tensor(sp[:, 5, :, :], sp[:, 5, :, :], sp[:, 4, :, :], ALU.add))
            own.do(eng.scalar_tensor_tensor(sp[:, 0, :, :], sp[:, 0, :, :], 0.0, sp[:, 5, :, :], ALU.max, ALU.add))
            own.did(eng.tensor_scalar(sp[:, 1, :, 16:32], sp[:, 0, :, 16:32], -1.0, None, ALU.mult))
            for tt in range(TT):
                own.did(eng.scalar_tensor_tensor(sp[:, 1, tt, 0:16], sp[:, 0, tt, 0:16], -1.0, rows[:, 32:48],
                                                 ALU.mult, ALU.mult))
            own.wait()
            eng.memset(stat[:, 10:11], 0.0).then_inc(sp_dve, 1)

            feature("xbc", 12)

            def cumulative():
                eng.wait_ge(s_cum, 1)
                for tt in range(TT):
                    own.did(eng.tensor_scalar(acum[:, tt, :], bank[7][:, 16 * tt:16 * tt + 16], -1.0, None, ALU.mult))
                own.wait()
                own.do(eng.tensor_tensor(acum[:, 2, :], bank[7][:, 32:48], acum[:, 0, :], ALU.add))
                eng.memset(stat[:, 11:12], 0.0).then_inc(cum_dve, 1)

            def convolve(n):
                i = MIX_ORDER[n]
                t = tmp[:, n % 4, :]
                if n >= 4:
                    eng.wait_ge(xbc_done, n - 3)
                lo_w = COLS["cw1"][0] + i * SSD_CONV
                w = [cols[:, lo_w + k:lo_w + k + 1] for k in range(SSD_CONV)]
                own.do(eng.tensor_scalar(t, inT[:, i, :], w[3], None, ALU.mult))
                for d in (1, 2, 3):
                    inst = eng.scalar_tensor_tensor(t[:, d:T], inT[:, i, 0:T - d], w[3 - d], t[:, d:T], ALU.mult, ALU.add)
                    if d < 3:
                        own.do(inst)
                    else:
                        inst.then_inc(conv_done, 1)

            def masked_cb():
                for g in range(2):
                    eng.wait_ge(cb_done, g + 1)
                    own.did(eng.tensor_tensor(cbm[:, g, 0:T], bank[4 + g][:, 0:T], C("tri", 0, T), ALU.mult))
                    own.did(eng.tensor_tensor(cbm[:, g, T:T + P], bank[4 + g][:, T:T + P], C("tri"), ALU.mult))
                own.wait()
                eng.memset(stat[:, 11:12], 0.0).then_inc(cbm_done, 1)

            def values_dt(n):
                half, tt = n // 2, n % 2
                eng.wait_ge(xs_done, n + 1)
                eng.tensor_tensor(xdt[:, tt, half * 512:half * 512 + 512].rearrange("p (h c) -> p h c", c=64),
                                  bank[6 + n % 2][:, :].rearrange("p (h c) -> p h c", c=64),
                                  sp[:, 0, tt, half * 8:half * 8 + 8].unsqueeze(2).to_broadcast([P, 8, 64]),
                                  ALU.mult).then_inc(xdt_done, 1)

            def segments(h):
                b, c = bank[4 + (h // 2) % 2], (h % 2) * T
                eng.wait_ge(arow_done, h // 2 + 1)
                if h >= 2:
                    eng.wait_ge(m_done, h - 1)
                for k, (dst, src, bias) in enumerate([(0, 0, 0), (P, P, 2), (T, P, 1)]):
                    eng.tensor_scalar(seg[:, h % 2, dst:dst + P], b[:, c + src:c + src + P], acum[:, bias, h:h + 1], 0.0,
                                      ALU.add, ALU.min).then_inc(seg_raw, 1)
                eng.wait_ge(seg_raw, 3 * (h + 1))
                eng.sem_inc(seg_done, 1)

            def decay(h):
                eng.wait_ge(exp_done, h + 1)
                if h >= 6:
                    eng.wait_ge(y_done, h - 5)
                eng.tensor_tensor(seg_m[:, h % 6, :], seg[:, h % 2, :], cbm[:, h // 8, :], ALU.mult).then_inc(m_done, 1)

            def gated_y(i):
                eng.wait_ge(y_done, 2 * i + 2)
                own.do(eng.scalar_tensor_tensor(inT[:, i, :], inT[:, i, :], col("dskip", i), bank[6 + i % 2][:, 0:T],
                                                ALU.mult, ALU.add))
                eng.tensor_tensor(inT[:, i, :], inT[:, i, :], inT[:, XBC_TILES + i, :], ALU.mult).then_inc(y_out, 1)

            for s in range(MIX_STEPS):
                if s == 0:
                    cumulative()
                    eng.wait_ge(bank_free, 4 * ROUND0["v1"] + 4)
                if s < 6:
                    convolve(2 * s)
                    convolve(2 * s + 1)
                if s == 4:
                    masked_cb()
                if s in (6, 7):
                    values_dt(2 * (s - 6))
                    values_dt(2 * (s - 6) + 1)
                n = s - SSD_AT
                if 1 <= n <= SSD_HEADS // 2:
                    decay(2 * n - 2)
                    decay(2 * n - 1)
                if 0 <= n < SSD_HEADS // 2:
                    segments(2 * n)
                    segments(2 * n + 1)
                if 0 <= n - 3 < Z_TILES:
                    eng.wait_ge(bank_free, 4 * ROUND0["z"] + 4 + n - 3 + 1)
                    gated_y(n - 3)
                if s in (19, 23):
                    g = (s - 19) // 4
                    eng.wait_ge(ms_done, 4 * (g + 1))
                    eng.tensor_scalar(rms[:, g, :], bank[5][:, 0:T], 1.0 / 512, EPS, ALU.mult, ALU.add).then_inc(rv_done, 1)
                if s == 25:
                    eng.wait_ge(rt_done, 2)
                    own.do(eng.reciprocal(rms[:, :, :], rms[:, :, :]))
                if 25 <= s < 29:
                    for i in (2 * (s - 25), 2 * (s - 25) + 1):
                        own.do(eng.scalar_tensor_tensor(inT[:, i, :], inT[:, i, :], col("nw1", i), rms[:, i // 4, :],
                                                        ALU.mult, ALU.mult))
                        split(a2, i, inT[:, i, :], a2_ready)
                i = s - FOX_AT
                if 0 <= i < FOX_HEADS:
                    head_max(FOX, i)
                if 0 <= i - 1 < FOX_HEADS:
                    head_norm(FOX, i - 1)
                if i >= 4 and i % 2 == 0:
                    out_split(FOX, (i - 4) // 2)
                ahead(UNIT0["v1"] + s)
            for j in range(6, 8):
                add_chunk((j - 6) * 512, j - 6, UNIT0["out1"] + j + 1)
                ahead(UNIT0["out1"] + j)
            for j in range(8, 16):
                if j % 4 == 3:
                    add_chunk((j // 4) * 512, (j // 4) % 2, UNIT0["out1"] + j + 1)
                if j < 15:
                    ahead(UNIT0["out1"] + j)
            resid_ready()

            normalise("ln2", x, norm)
            scaled_los("ln2")
            ahead(UNIT0["out1"] + 15)

            def best8(k, jobs):
                ks = slice(8 * k, 8 * k + 8)
                for src, v, i in jobs:
                    own.did(eng.max(v[:, ks], src))
                own.wait()
                for src, v, i in jobs:
                    own.did(eng.max_index(i[:, ks], v[:, ks], src))
                own.wait()
                if k == 0:
                    for src, v, i in jobs:
                        own.did(eng.match_replace(src, v[:, ks], src, NEG))
                    own.wait()

            def key_rows(h):
                return [(s_sb[tt][:, n, :], top_v[tt][:, n, :], top_i[tt][:, n, :]) for tt in range(TT)
                        for n in (2 * h, 2 * h + 1)]

            def pair_rows(h):
                return [(cand[:, h % 2, tt, :], sc[:, tt, h, :], pos[tt][:, h, :]) for tt in range(TT)]

            def sums(h):
                for tt in range(TT):
                    a, b = top_v[tt][:, 2 * h, :], top_v[tt][:, 2 * h + 1, :]
                    own.did(eng.tensor_tensor(cand[:, h % 2, tt, :].rearrange("p (a b) -> p a b", a=TOPK),
                                              a.unsqueeze(2).to_broadcast([P, TOPK, TOPK]),
                                              b.unsqueeze(1).to_broadcast([P, TOPK, TOPK]), ALU.add))
                own.wait()

            waiting = [UNIT0["u0"] + j for j in range(16)]

            def fill():
                ahead(waiting.pop(0))

            for s in range(2 * PEER_HEADS + 6):
                for k in range(2):
                    one, two = KEYS_AT.get(s - 1 - k), KEYS_AT.get(s - 3 - k)
                    if one is None and two is None:
                        continue
                    if one is not None and k == 0:
                        eng.wait_ge(sk_copied, TT * (one + 1))
                    if two is not None and k == 0:
                        sums(two)
                    best8(k, (key_rows(one) if one is not None else []) + (pair_rows(two) if two is not None else []))
                if s < 16:
                    ahead(UNIT0["wq"] + s)
                else:
                    fill()

            for tt in range(TT):
                own.did(eng.tensor_copy(top_f[:, :, :], top_i[tt][:, :, :]))
                tf = top_f[:, :, :].rearrange("p (h two) k -> p h two k", two=2)
                own.did(eng.tensor_copy(first[:, :], sc[:, tt, :, 0]))
                pf = pos[tt][:, :, :].rearrange("p h k -> p (h k)")
                own.did(eng.tensor_scalar(posab[:, 0, :], pf, 4, None, ALU.logical_shift_right))
                own.did(eng.tensor_scalar(posab[:, 1, :], pf, 15, None, ALU.bitwise_and))
                own.wait()
                eng.tensor_tensor(sc[:, tt, :, :], sc[:, tt, :, :],
                                  first[:, :].unsqueeze(2).to_broadcast([P, PEER_HEADS, TOPK]),
                                  ALU.subtract).then_inc(sm_dve, 1)
                own.do(eng.tensor_copy(posf[:, :, :], posab[:, :, :]))
                for half in range(2):
                    if waiting:
                        fill()
                    own.do(eng.tensor_tensor(onehot[:, :, :], C("iota", 0, TOPK).unsqueeze(1).to_broadcast([P, PICKS, TOPK]),
                                             posf[:, half, :].unsqueeze(2).to_broadcast([P, PICKS, TOPK]), ALU.is_equal))
                    oh = onehot[:, :, :].rearrange("p (h k) a -> p h k a", h=PEER_HEADS)
                    own.do(eng.tensor_tensor(oh, oh, tf[:, :, half, :].unsqueeze(2).to_broadcast([P, PEER_HEADS, TOPK, TOPK]),
                                             ALU.mult))
                    if waiting:
                        fill()
                    own.do(eng.tensor_reduce(picked[:, tt, half, :], onehot[:, :, :], AX.X, ALU.add))
            while waiting:
                fill()
            for tt in range(TT):
                eng.wait_ge(sm_act, tt + 1)
                own.do(eng.tensor_reduce(gsum[:, tt, :], sc[:, tt, :, :], AX.X, ALU.add))
                own.do(eng.reciprocal(gsum[:, tt, :], gsum[:, tt, :]))
                eng.tensor_tensor(picked[:, tt, 2, :].rearrange("p (h k) -> p h k", h=PEER_HEADS), sc[:, tt, :, :],
                                  gsum[:, tt, :].unsqueeze(2).to_broadcast([P, PEER_HEADS, TOPK]), ALU.mult)\
                    .then_inc(picks_done, 1)
            eng.wait_ge(pickT_psum, 1)
            own.did(eng.tensor_copy(pickT[:, 0:2, :].rearrange("p a t -> p (a t)"), bank[6][:, :]))
            own.did(eng.tensor_copy(pickT[:, 2, :], bank[7][:, 0:T]))
            own.wait()
            with eng.Fori(0, T // 8) as b:
                for j in range(8):
                    t = lin(j, (b, 8))
                    if j % 4 == 0:
                        eng.wait_ge(g_mm, lin(j + 4, (b, 8)))
                        eng.tensor_tensor(pick_b[:, j:j + 4, :], C("iota").unsqueeze(1).to_broadcast([P, 4, P]),
                                          pickT[:, 1, bass.ds(t, 4)].unsqueeze(2).to_broadcast([P, 4, P]),
                                          ALU.is_equal).then_inc(ohb_done, 1)
                    eng.tensor_scalar(pick_a[:, j, :], C("iota"), pickT[:, 0, bass.ds(t, 1)], pickT[:, 2, bass.ds(t, 1)],
                                      ALU.is_equal, ALU.mult).then_inc(oha_done, 1)

            def gates_of(slot, j):
                return gbuf[:, bass.ds(slot, 1), :, j * TBLOCK:(j + 1) * TBLOCK].rearrange("p a b t -> p (a b) t")

            def blocks(ap):
                return ap.rearrange("p (b t) -> p b t", t=TBLOCK)

            def tile0(n):
                return act0[:, n, :]

            def gated0(g):
                if g >= 2:
                    eng.wait_ge(g_full, 16 * (g - 1))
                for j in range(4):
                    tile = tile0(4 * g + j)
                    eng.tensor_tensor(blocks(tile), blocks(tile), gates_of(g, j), ALU.mult).then_inc(g_used, 1)
                for j in range(4):
                    eng.wait_ge(g_used, 4 * g + j + 1)
                    own.did(eng.tensor_copy(a2[0][:, 4 * g + j, :], tile0(4 * g + j)))
                own.wait()

            def low0(g):
                for n in range(4 * g, 4 * g + 4):
                    eng.tensor_tensor(a2[1][:, n, :], tile0(n), a2[0][:, n, :].bitcast(F32), ALU.subtract)\
                        .then_inc(a2_ready, 1)

            eng.wait_ge(g_early, TBLOCKS)
            eng.wait_ge(g_write[0], 16 * (TBLOCKS // 2 + 1))
            gated0(0)
            gated0(1)
            eng.wait_ge(g_write[1], 16 * (TBLOCKS // 2 + 1))
            low0(0)
            low0(1)
            for j in range(8):
                if j in (1, 2):
                    gated0(j + 1)
                    low0(j + 1)
                if j % 4 == 3:
                    add_chunk((j // 4) * 512, j // 4, UNIT0["e0"] + j + 1)
                ahead(UNIT0["e0"] + j)
            row_units("e0", 1, skip=1)

            def gated_by(r):
                def gated(g, j):
                    if j == 0:
                        eng.wait_ge(g_full, lin(16 * 3, (r, 64), (g, 16)))
                    eng.wait_ge(tmp_full, lin(BQ["u1"] + j + 1, (r, RT), (g, 4)))
                    eng.tensor_tensor(blocks(tmp[:, j, :]), blocks(tmp[:, j, :]), gates_of(g, j), ALU.mult).then_inc(g_used, 1)
                    eng.wait_ge(g_used, lin(16 + j + 1, (r, 16), (g, 4)))
                    split(a2, None, tmp[:, j, :], tmp_split, ap=bass.ds(lin(j, (g, 4)), 1))
                return gated
            with eng.Fori(0, PEER_ROUNDS - 2) as r:
                own.enter(r, 16)
                feature("u1", 16, 0, gated_by(r), 4, r)
                row_units("e1", 2, r=r)
                own.leave(PEER_ROUNDS - 2)
            feature("u7", 16, 0, gated_by(PEER_ROUNDS - 2), 4)
            for j in range(16):
                if j == 4:
                    normalise("gmem", mem, mem)
                if 5 <= j < 13:
                    scaled_lo("gmem", 2 * (j - 5))
                    scaled_lo("gmem", 2 * (j - 5) + 1)
                if j % 4 == 3:
                    add_chunk((j // 4) * 512, (j // 4) % 2, UNIT0["e7"] + j + 1)
                if j < 15:
                    ahead(UNIT0["e7"] + j)
            resid_ready()
            ahead(UNIT0["e7"] + 15)
            for j in range(8):
                if j == 1:
                    normalise("lnf", x, x, 1)
                if j == 3:
                    normalise("gmix", x, norm)
                if j >= 4:
                    for kt in range(4 * (j - 4), 4 * (j - 4) + 4):
                        scaled_lo("gmix", kt)
                ahead(UNIT0["ck"] + j)

            tap_done = [0] * CONV_TILES

            def tap(i, d):
                w = COLS["cw2"][0] + (CONV_K - 1 - d) * CONV_TILES + i
                w = cols[:, w:w + 1]
                if d == 0:
                    inst = eng.tensor_scalar(conv[:, i, :], val[:, i, :], w, col("cb2", i), ALU.mult, ALU.add)
                else:
                    eng.wait_ge(dve_own, tap_done[i])
                    inst = eng.scalar_tensor_tensor(conv[:, i, d:T], val[:, i, 0:T - d], w, conv[:, i, d:T], ALU.mult, ALU.add)
                if d == CONV_K - 1:
                    inst.then_inc(cv_done, 1)
                else:
                    own.did(inst)
                    tap_done[i] = own.n

            for s in range(MIX2_STEPS):
                if s >= 2 and s % 2 == 0 and s // 2 - 1 < CONV_TILES:
                    i = s // 2 - 1
                    eng.wait_ge(bank_free, 4 * ROUND0["vg"] + 4 + 2 * i + 2)
                    eng.tensor_tensor(val[:, i, :], val[:, i, :], gate[:, i % 2, :], ALU.mult).then_inc(gated, 1)
                    eng.wait_ge(gated, i + 1)
                i = s - HEAD2_AT
                if i % 2 == 0 and 0 <= i // 2 < ATTN_HEADS:
                    head_max(MOBA, i // 2)
                for i, d in TAP_ORDER[TAPS_TO[s]:TAPS_TO[s + 1]]:
                    tap(i, d)
                i = s - HEAD2_AT
                if i % 2 == 1 and 0 <= i // 2 < ATTN_HEADS:
                    head_norm(MOBA, i // 2)
                for i in OUT2_AT.get(s, ()):
                    out_split(MOBA, i)
                if s == LN_AT:
                    eng.wait_ge(mu_done, CONV_TILES)
                    own.do(eng.tensor_scalar(ln_buf[:, 1, :], bank[5][:, 0:T], 1.0 / 1024, None, ALU.mult))
                    for i in range(CONV_TILES):
                        eng.tensor_tensor(conv[:, i, :], conv[:, i, :], ln_buf[:, 1, :], ALU.subtract).then_inc(cen_done, 1)
                if s == LN_AT + 2:
                    eng.wait_ge(var_done, CONV_TILES)
                    eng.tensor_scalar(ln_buf[:, 0, :], bank[5][:, 0:T], 1.0 / 1024, EPS, ALU.mult, ALU.add).then_inc(rv_done, 1)
                if s == LN_AT + 3:
                    eng.wait_ge(rt_done, 3)
                    own.do(eng.reciprocal(ln_buf[:, 0, :], ln_buf[:, 0, :]))
                    for i in range(CONV_TILES):
                        eng.tensor_tensor(conv[:, i, :], conv[:, i, :], ln_buf[:, 0, :], ALU.mult).then_inc(cn_done, 1)
                for n in (4, 5):
                    for i in range(4 * (n - 4), 4 * (n - 4) + 4) if s == LN_AT + n else ():
                        eng.wait_ge(cn_hi, i + 1)
                        eng.tensor_tensor(a1[1][:, ATTN_HEADS + i, :], conv[:, i, :],
                                          a1[0][:, ATTN_HEADS + i, :].bitcast(F32), ALU.subtract).then_inc(a2_ready, 1)
                if s >= MIX2_STEPS - 2:
                    c = s - (MIX2_STEPS - 2)
                    add_chunk(c * 512, c, UNIT0["vg"] + s + 1)
                ahead(UNIT0["vg"] + s)
            for j in range(8, 16):
                if j % 4 == 3:
                    add_chunk((j // 4) * 512, (j // 4) % 2, UNIT0["out2"] + j + 1)
                if j < 15:
                    ahead(UNIT0["out2"] + j)
            resid_ready()

            normalise("gcross", x, norm)
            scaled_los("gcross")
            ahead(UNIT0["out2"] + 15)
            for s in range(CROSS_STEPS):
                if 0 <= s - 1 < CROSS_HEADS:
                    head_max(CROSS, s - 1)
                if 0 <= s - 2 < CROSS_HEADS:
                    head_norm(CROSS, s - 2)
                if 0 <= s - 4 < CROSS_HEADS:
                    out_split(CROSS, s - 4)
                if s < CROSS_HEADS:
                    ahead(UNIT0["cq"] + s)
            for j in range(4):
                add_chunk(j * 512, j % 2, UNIT0["co"] + j + 1)
                if j < 3:
                    ahead(UNIT0["co"] + j)
            resid_ready()

            normalise("gmlp", x, norm)
            scaled_los("gmlp")
            ahead(UNIT0["co"] + 3)

            def square(r, n0):
                def extra(g, j):
                    eng.wait_ge(tmp_full, lin(n0 + j + 1, (r, RT), (g, 4)))
                    own.do(eng.tensor_tensor(tmp[:, j, :], tmp[:, j, :], tmp[:, j, :], ALU.mult))
                    split(a2, None, tmp[:, j, :], tmp_split, ap=bass.ds(lin(j, (g, 4)), 1))
                return extra
            with eng.Fori(0, FF_ROUNDS - 1) as r:
                own.enter(r, 32)
                feature("up0", 16, 0, square(r, BQ["up0"]), 8, r)
                row_units("down0", 2, r=r)
                own.leave(FF_ROUNDS - 1)
            feature(f"up{FF_ROUNDS - 1}", 16, 0, square(None, BQ[f"up{FF_ROUNDS - 1}"]), 8)
            row_units(f"down{FF_ROUNDS - 1}", 2, last=True)
            resid_ready()
            normalise("final", x, x, 2)

        @block.tensor
        def _(pe):
            eng = nc.tensor
            mm = nc.tensor.matmul

            def feature_unit(j, act_t, built=None):
                hi, lo = w_hi[j % SPLIT], w_lo[j % SPLIT]
                o = bank[j % 4][:, 0:T]
                for kt in range(KT):
                    if built and kt % 4 == 0:
                        eng.wait_ge(tmp_split, BQ[built] + kt + 4)
                    ks = slice(kt * P, kt * P + P)
                    mm(o, hi[:, ks], act_t[0][:, kt, :], start=kt == 0, stop=False)
                    mm(o, hi[:, ks], act_t[1][:, kt, :], start=False, stop=False)
                    last = mm(o, lo[:, ks], act_t[0][:, kt, :], start=False, stop=kt == KT - 1)
                last.then_inc(mm_done, 1)

            def feature(name, n, act_t, r=None, built=None):
                u0, b0 = UNIT0[name], 4 * ROUND0[name]
                with eng.Fori(0, n // 4) as g:
                    for j in range(4):
                        eng.wait_ge(split_done, lin(u0 + j + 1, (r, RU), (g, 4)))
                        eng.wait_ge(bank_free, lin(b0 + j + 1, (r, RB), (g, 4)))
                        feature_unit(j, act_t, built if j == 0 else None)

            def row_unit(j, banks, act_t, k0, first, end):
                hi, lo = w_hi[j % SPLIT], w_lo[j % SPLIT]
                for k in range(4):
                    ns = slice(k * 512, k * 512 + 512)
                    for tt in range(TT):
                        o = banks[tt][:, :]
                        ts = slice(tt * P, tt * P + P)
                        mm(o, act_t[0][:, k0 + k, ts], hi[:, ns], start=first and k == 0, stop=False)
                        mm(o, act_t[0][:, k0 + k, ts], lo[:, ns], start=False, stop=False)
                        last = mm(o, act_t[1][:, k0 + k, ts], hi[:, ns], start=False, stop=end and k == 3)
                last.then_inc(mm_done, 1)

            def row_units(name, pairs, act_t, r=None, ready=None, skip=0):
                u0, b0 = UNIT0[name] + 8 * skip, 4 * ROUND0[name] + 4 * skip
                with eng.Fori(0, pairs) as g:
                    for j in range(8):
                        c = j // 4
                        eng.wait_ge(split_done, lin(u0 + j + 1, (r, RU), (g, 8)))
                        if j % 4 == 0:
                            eng.wait_ge(bank_free, lin(b0 + 2 * c + 2, (r, RB), (g, 4)))
                        if ready and c == 0:
                            ready(j)
                        row_unit(j, bank[2 * c:2 * c + 2], act_t, 4 * (j % 4), j % 4 == 0, j % 4 == 3)

            def hidden(name, r):
                def ready(j):
                    eng.wait_ge(tmp_split, lin(BQ[name] + 4 * j + 4, (r, RT)))
                return ready

            def turn_tile(name, src, kt):
                if kt >= 4:
                    eng.wait_ge(tmp_split, BQ[name] + kt - 3)
                for tt in range(TT):
                    last = eng.transpose(bank[4 + kt % 4][:, tt * P:tt * P + P], src[:, tt, kt * P:kt * P + P], C("ident"))
                last.then_inc(tr_done, 1)

            def turn(name, src):
                for kt in range(KT):
                    turn_tile(name, src, kt)

            def head_scores(a, i, scores):
                h, n = HEAD0[a["name"]] + i, len(a["s_banks"])
                if i >= n:
                    if a["masked"]:
                        eng.wait_ge(at_max, h - n + 1)
                    else:
                        eng.wait_ge(at_exp, 2 * (h - n + 1))
                scores(i, bank[a["s_banks"][i % n]]).then_inc(at_s, 1)

            def head_turn(a, i):
                h = HEAD0[a["name"]] + i
                eng.wait_ge(at_p, 2 * (h + 1))
                if h >= 1:
                    eng.wait_ge(at_tc, h)
                for src, dst in a["turns"]:
                    last = eng.transpose(bank[6][:, dst:dst + P], a["p"][:, i % a["slots"], src:src + P], C("ident"))
                last.then_inc(at_t, 1)

            def head_out(a, i, values):
                h, d = HEAD0[a["name"]] + i, a["d"]
                k, n = i // a["heads_out"], len(a["o_banks"])
                eng.wait_ge(at_tc, h + 1)
                if i % a["heads_out"] == 0 and k >= n:
                    eng.wait_ge(at_oc, OUT0[a["name"]] + k - n + 1)
                p0 = d * (i % a["heads_out"])
                o = bank[a["o_banks"][k % n]]
                for m, (kb, src, w, dst) in enumerate(a["pv"]):
                    last = mm(o[p0:p0 + d, dst:dst + w], values(i, kb), a["t"][:, i % a["t_slots"], src:src + w],
                              start=m == 0, stop=m == len(a["pv"]) - 1)
                last.then_inc(at_o, 1)

            eng.wait_ge(s_small, 64)
            eng.wait_ge(normed, 2)
            turn("ln1", norm)
            eng.wait_ge(tmp_split, 16)
            eng.wait_ge(wd_done, 2)
            for kt in range(KT):
                for n, (w, h) in enumerate([(0, 0), (0, 1), (1, 0)]):
                    last = mm(bank[6][0:32, 0:T], wd[w][:, kt, :], a1[h][:, kt, :], start=kt == 0 and n == 0,
                              stop=kt == KT - 1 and n == 2)
            last.then_inc(s_sp, 1)
            eng.wait_ge(dtf_done, 1)
            for tt in range(TT):
                last = eng.transpose(bank[7][:, 32 * tt:32 * tt + 32], dtf[:, tt * P:tt * P + P], C("ident")[0:32, 0:32])
            last.then_inc(s_sp, 1)
            feature("xbc", 12, a1)

            def cumulative():
                eng.wait_ge(sp_dve, 3)
                for tt in range(TT):
                    mm(bank[7][:, 16 * tt:16 * tt + 16], C("tri"), sp[:, 1, tt, 0:16], start=True, stop=True)
                mm(bank[7][:, 32:48], C("ones"), sp[:, 1, 0, 0:16], start=True, stop=True).then_inc(s_cum, 1)

            def c_b():
                eng.wait_ge(xbc_done, 4)
                for g in range(2):
                    bT, cT = inT[:, 8 + g, :], inT[:, 10 + g, :]
                    mm(bank[4 + g][:, 0:T], bT[:, 0:P], cT, start=True, stop=True)
                    mm(bank[4 + g][:, T:T + P], bT[:, P:T], cT[:, P:T], start=True, stop=True).then_inc(cb_done, 1)

            def values_turn(n):
                half, tt = n // 2, n % 2
                if n == 0:
                    eng.wait_ge(cum_dve, 1)
                eng.wait_ge(xbc_done, 8 + 4 * half)
                if n >= 2:
                    eng.wait_ge(xdt_done, n - 1)
                for i in range(4):
                    last = eng.transpose(bank[6 + n % 2][:, i * P:i * P + P], inT[:, half * 4 + i, tt * P:tt * P + P], C("ident"))
                last.then_inc(xs_done, 1)

            def arow(n):
                if n == 0:
                    eng.wait_ge(cbm_done, 1)
                if n >= 2:
                    eng.wait_ge(seg_done, 2 * n - 2)
                for h in range(2):
                    for tt in range(TT):
                        last = mm(bank[4 + n % 2][:, h * T + tt * P:h * T + tt * P + P],
                                  sp[:, 1, tt, 2 * n + h:2 * n + h + 1].to_broadcast([P, P]), C("tri"), start=True, stop=True)
                last.then_inc(arow_done, 1)

            def ssd_head(h):
                i, p0 = h // 2, 64 * (h % 2)
                if h == 0:
                    eng.wait_ge(xdt_done, 4)
                if h % 2 == 0 and i >= 2:
                    eng.wait_ge(y_out, i - 1)
                eng.wait_ge(m_done, h + 1)
                o = bank[6 + i % 2]
                mm(o[p0:p0 + 64, 0:T], xdt[:, 0, h * 64:h * 64 + 64], seg_m[:, h % 6, 0:T], start=True, stop=False)
                mm(o[p0:p0 + 64, P:T], xdt[:, 1, h * 64:h * 64 + 64], seg_m[:, h % 6, T:T + P], start=False, stop=True)\
                    .then_inc(y_done, 1)

            def mean_square(i):
                if i == 0:
                    eng.wait_ge(seg_done, SSD_HEADS)
                if i == 4:
                    eng.wait_ge(rv_done, 1)
                eng.wait_ge(ysq_done, i + 1)
                mm(bank[5][:, 0:T], C("ones"), tmp[:, i % 4, :], start=i % 4 == 0, stop=i % 4 == 3).then_inc(ms_done, 1)

            def fox_scores(i, b):
                t, p0 = i // 2, 64 * (i % 2)
                q, k = inT[p0:p0 + 64, 20 + 2 * t, :], inT[p0:p0 + 64, 21 + 2 * t, :]
                f = [sp[:, 1, tt, 16 + i:17 + i] for tt in range(TT)]
                mm(b[:, 0:P], q[:, 0:P], k[:, 0:P], start=True, stop=False)
                mm(b[:, 0:P], C("tri"), f[0].to_broadcast([P, P]), start=False, stop=False)
                mm(b[:, 0:P], f[0].to_broadcast([P, P]), C("ntri"), start=False, stop=True)
                mm(b[:, P:3 * P], q[:, P:T], k, start=True, stop=False)
                mm(b[:, P:2 * P], f[0].to_broadcast([P, P]), C("gt"), start=False, stop=False, skip_group_check=True)
                mm(b[:, 2 * P:3 * P], f[1].to_broadcast([P, P]), C("ntri"), start=False, stop=False, skip_group_check=True)
                return mm(b[:, P:3 * P], C("tri"), f[1].to_broadcast([P, T]), start=False, stop=True)

            def mix_side(s):
                if s == 0:
                    cumulative()
                if s == 4:
                    c_b()
                if s == 6:
                    values_turn(0)
                    values_turn(1)
                if s == 7:
                    values_turn(2)
                    values_turn(3)
                n = s - SSD_AT
                if 0 <= n < SSD_HEADS // 2:
                    arow(n)
                if 0 <= n - 3 < SSD_HEADS // 2:
                    ssd_head(2 * (n - 3))
                    ssd_head(2 * (n - 3) + 1)
                if 0 <= s - 16 < Z_TILES:
                    mean_square(s - 16)
                i = s - FOX_AT
                if 0 <= i < FOX_HEADS:
                    eng.wait_ge(bank_free, 4 * ROUND0["qk1"] + 4 + 2 * (i // 2) + 2)
                    head_scores(FOX, i, fox_scores)
                if 0 <= i - 2 < FOX_HEADS:
                    head_turn(FOX, i - 2)
                if 0 <= i - 3 < FOX_HEADS:
                    head_out(FOX, i - 3, lambda i, kb: v1[:, kb, i * 64:i * 64 + 64])

            def out1_unit(j):
                c, k = OUT1_ORDER[j]
                eng.wait_ge(split_done, UNIT0["out1"] + j + 1)
                if k == 0:
                    eng.wait_ge(bank_free, 4 * ROUND0["out1"] + 2 * c + 2)
                    eng.wait_ge(a2_ready, Z_TILES)
                if k >= 2:
                    eng.wait_ge(at_oc, 4 * (k - 1))
                row_unit(j, bank[2 * c:2 * c + 2], a2, 4 * k, k == 0, k == 3)

            def mix_unit(s):
                if s < 8:
                    c = s // 4
                    eng.wait_ge(split_done, UNIT0["v1"] + s + 1)
                    if s % 4 == 0:
                        eng.wait_ge(bank_free, 4 * ROUND0["v1"] + 2 * c + 2)
                    row_unit(s, bank[2 * c:2 * c + 2], a1, 4 * (s % 4), s % 4 == 0, s % 4 == 3)
                elif s < 32:
                    eng.wait_ge(split_done, UNIT0["v1"] + s + 1)
                    eng.wait_ge(bank_free, 4 * ROUND0["z"] + (s - 8) + 1)
                    feature_unit(s, a1)
                else:
                    out1_unit(s - 32)

            for s in range(MIX_STEPS):
                mix_side(s)
                mix_unit(s)
            for j in range(6, 8):
                out1_unit(j)
            row_units("out1", 1, a2, skip=1)

            eng.wait_ge(normed, 4)
            turn("ln2", norm)
            for s in range(WQ_STEPS):
                if s in KEYS_AT:
                    h = KEYS_AT[s]
                    if h == 0:
                        eng.wait_ge(s_keys, 16)
                    if h >= 4:
                        eng.wait_ge(sk_copied, TT * (h - 3))
                    eng.wait_ge(bank_free, 4 * ROUND0["wq"] + 4 + 2 * h + 2)
                    for tt in range(TT):
                        for n in (2 * h, 2 * h + 1):
                            c = tt * T + (n % 2) * P
                            last = mm(bank[4 + h % 4][:, c:c + P], qT[:, n, tt * P:tt * P + P], keys[:, n, :],
                                      start=True, stop=True)
                    last.then_inc(sk_done, 1)
                if s < 16:
                    eng.wait_ge(split_done, UNIT0["wq"] + s + 1)
                    eng.wait_ge(bank_free, 4 * ROUND0["wq"] + s + 1)
                    feature_unit(s, a1, "ln2" if s == 0 else None)
            feature("u0", 16, a1)
            eng.wait_ge(picks_done, TT)
            for n in range(3):
                for tt in range(TT):
                    o = bank[6 + n // 2][:, (n % 2) * T + tt * P:(n % 2) * T + tt * P + P]
                    last = eng.transpose(o, picked[:, tt, n, :], C("ident"))
            last.then_inc(pickT_psum, 1)
            eng.sem_inc(g_mm, 8)
            with eng.Fori(0, T // 8) as b:
                for j in range(8):
                    k = j // 4
                    eng.wait_ge(oha_done, lin(j + 1, (b, 8)))
                    if j % 4 == 0:
                        eng.wait_ge(ohb_done, lin(k + 1, (b, 2)))
                    if j % 4 == 0:
                        eng.wait_ge(g_evict, lin(k + 1, (b, 2)))
                    mm(bank[4 + k][:, (j % 4) * P:(j % 4) * P + P], pick_b[:, j, :], pick_a[:, j, :], start=True, stop=True)\
                        .then_inc(g_mm, 1)
            row_units("e0", 2, a2, ready=lambda j: eng.wait_ge(a2_ready, Z_TILES + 4 * j + 4))
            with eng.Fori(0, PEER_ROUNDS - 2) as r:
                feature("u1", 16, a1, r)
                row_units("e1", 2, a2, r, hidden("u1", r))
            feature("u7", 16, a1)
            for j in range(16):
                if j == 5:
                    eng.wait_ge(normed, 6)
                if 5 <= j < 13:
                    turn_tile("gmem", mem, 2 * (j - 5))
                    turn_tile("gmem", mem, 2 * (j - 5) + 1)
                c = (j // 4) % 2
                eng.wait_ge(split_done, UNIT0["e7"] + j + 1)
                if j % 4 == 0:
                    eng.wait_ge(bank_free, 4 * ROUND0["e7"] + 2 * (j // 4) + 2)
                if j < 4:
                    eng.wait_ge(tmp_split, BQ["u7"] + 4 * j + 4)
                row_unit(j, bank[2 * c:2 * c + 2], a2, 4 * (j % 4), j % 4 == 0, j % 4 == 3)

            for j in range(8):
                if j == 4:
                    eng.wait_ge(normed, 8)
                if j >= 4:
                    for kt in range(4 * (j - 4), 4 * (j - 4) + 4):
                        turn_tile("gmix", norm, kt)
                eng.wait_ge(split_done, UNIT0["ck"] + j + 1)
                eng.wait_ge(bank_free, 4 * ROUND0["ck"] + j + 1 if j < 4 else 4 * ROUND0["cv"] + 2)
                if j < 4:
                    feature_unit(j, a1, "gmem" if j == 0 else None)
                else:
                    row_unit(j, bank[0:2], a1, 4 * (j - 4), j == 4, j == 7)

            def moba_scores(i, b):
                q, k = q2[:, i, :], k2[:, i, :]
                mm(b[:, 0:P], q[:, 0:P], k[:, 0:P], start=True, stop=False)
                mm(b[:, 0:P], C("flip"), brev[:, i, P:T], start=False, stop=True)
                mm(b[:, P:3 * P], q[:, P:T], k, start=True, stop=False)
                return mm(b[:, P:3 * P], C("flip"), brev[:, i, :], start=False, stop=True)

            def mix2_side(s):
                if s == 4:
                    eng.wait_ge(s_rel, 32)
                    mm(bank[5][0:ATTN_HEADS, 0:REL], rel_sb[:, :], oneh_sb[:, :], start=True, stop=True).then_inc(s_relT, 1)
                i = s - HEAD2_AT
                if i % 2 == 0 and 0 <= i // 2 < ATTN_HEADS:
                    if i == 0:
                        eng.wait_ge(s_brev, 16)
                    eng.wait_ge(bank_free, 4 * ROUND0["qk2"] + 4 + i + 2)
                    head_scores(MOBA, i // 2, moba_scores)
                if i % 2 == 0 and 0 <= i // 2 - 1 < ATTN_HEADS:
                    head_turn(MOBA, i // 2 - 1)
                for h in OUT2_AT.get(s, ()):
                    if h % 4 == 0:
                        eng.wait_ge(bank_free, 4 * ROUND0["v2"] + 4 + 2 * (h // 4) + 2)
                        eng.wait_ge(at_max, HEAD0["moba"] + ATTN_HEADS)
                    head_out(MOBA, h, lambda i, kb: v2[:, kb, i * P:i * P + P])
                for i in range(CONV_TILES):
                    if s == CONV_END[i] + 1:
                        eng.wait_ge(cv_done, i + 1)
                        if i == 0:
                            eng.wait_ge(relT_done, 1)
                        mm(bank[5][:, 0:T], C("ones"), conv[:, i, :], start=i == 0, stop=i == CONV_TILES - 1).then_inc(mu_done, 1)
                if s == LN_AT + 2:
                    eng.wait_ge(cen_done, 1)
                    for i in range(CONV_TILES):
                        eng.wait_ge(csq_done, i + 1)
                        mm(bank[5][:, 0:T], C("ones"), val[:, i, :], start=i == 0, stop=i == CONV_TILES - 1).then_inc(var_done, 1)

            def mix2_unit(s):
                eng.wait_ge(split_done, UNIT0["vg"] + s + 1)
                if s < 32:
                    eng.wait_ge(bank_free, 4 * ROUND0["vg"] + s + 1)
                    feature_unit(s, a2, "gmix" if s == 0 else None)
                elif s < 40:
                    c = (s - 32) // 4
                    if s % 4 == 0:
                        eng.wait_ge(bank_free, 4 * ROUND0["v2"] + 2 * c + 2)
                    row_unit(s, bank[2 * c:2 * c + 2], a2, 4 * (s % 4), s % 4 == 0, s % 4 == 3)
                else:
                    c, k = OUT2_ORDER[s - 40]
                    if k == 0:
                        eng.wait_ge(bank_free, 4 * ROUND0["out2"] + 2 * c + 2)
                    if k < 2:
                        eng.wait_ge(at_oc, FOX_HEADS // 2 + 4 * (k + 1))
                    else:
                        eng.wait_ge(a2_ready, Z_TILES + 16 + 4 * (k - 1))
                    row_unit(s, bank[2 * c:2 * c + 2], a1, 4 * k, k == 0, k == 3)

            for s in range(MIX2_STEPS):
                mix2_side(s)
                mix2_unit(s)
            row_units("out2", 1, a1, skip=1)

            eng.wait_ge(normed, 10)
            turn("gcross", norm)

            def cross_scores(i, b):
                mm(b[:, 0:T], cqT[:, i, 0:P], ckT[:, i, :], start=True, stop=True)
                return mm(b[:, T:2 * T], cqT[:, i, P:T], ckT[:, i, :], start=True, stop=True)

            for s in range(CROSS_STEPS):
                if 0 <= s - 1 < CROSS_HEADS:
                    eng.wait_ge(bank_free, 4 * ROUND0["cq"] + 4 + s)
                    head_scores(CROSS, s - 1, cross_scores)
                if 0 <= s - 3 < CROSS_HEADS:
                    head_turn(CROSS, s - 3)
                if 0 <= s - 4 < CROSS_HEADS:
                    head_out(CROSS, s - 4, lambda i, kb: cv[:, kb, i * P:i * P + P])
                if s < CROSS_HEADS:
                    eng.wait_ge(split_done, UNIT0["cq"] + s + 1)
                    eng.wait_ge(bank_free, 4 * ROUND0["cq"] + s + 1)
                    feature_unit(s, a1, "gcross" if s == 0 else None)
            eng.wait_ge(at_oc, FOX_HEADS // 2 + ATTN_HEADS + CROSS_HEADS)
            u0, r0 = UNIT0["co"], ROUND0["co"]
            for j in range(4):
                eng.wait_ge(split_done, u0 + j + 1)
                eng.wait_ge(bank_free, 4 * r0 + 2 * j + 2)
                row_unit(j, bank[2 * (j % 2):2 * (j % 2) + 2], a2, 0, True, True)

            eng.wait_ge(normed, 12)
            turn("gmlp", norm)
            with eng.Fori(0, FF_ROUNDS) as r:
                feature("up0", 16, a1, r, "gmlp")
                row_units("down0", 2, a2, r, hidden("up0", r))


def _feature_units(w):
    k, n = w.shape
    return w.reshape(KT, P, n // P, P).transpose(2, 1, 0, 3).reshape(n // P, P, UNIT)


def _row_units(w):
    k, n = w.shape
    return w.reshape(k // 512, 4, P, n // 512, 512).transpose(3, 0, 2, 1, 4).reshape(-1, P, UNIT)


def _pairs(a, b):
    return np.stack([_feature_units(a), _feature_units(b)], axis=1).reshape(-1, P, UNIT)


def _ordered(w, order):
    units = _row_units(w)
    return np.concatenate([units[[4 * c + k for c, k in order]], units[8:]])


def _cols(v):
    return v.reshape(-1, P).T


def _bucket(dist):
    dist = np.asarray(dist)
    exact = BUCKETS // 2
    nf = np.maximum(dist, exact).astype(np.float32)
    large = exact + (np.log(nf / np.float32(exact)) / np.float32(np.log(2048 / exact)) * np.float32(BUCKETS - exact)).astype(np.int32)
    return np.where(dist < exact, dist, np.minimum(large, BUCKETS - 1))


def _constants():
    p, c = np.arange(P)[:, None], np.arange(P)[None, :]
    tri = (p <= c).astype(np.float32)
    causal = np.where(p >= c, 0.0, NEG).astype(np.float32)
    consts = np.concatenate([
        np.eye(P, dtype=np.float32), tri, np.ones((P, P), np.float32), -tri, 1 - tri,
        (p + c == P - 1).astype(np.float32), np.zeros((P, P), np.float32), causal,
        np.broadcast_to(np.arange(P, dtype=np.float32), (P, P))], axis=1)
    onehot = np.zeros((BUCKETS, REL), np.float32)
    j = np.arange(REL)
    onehot[_bucket(np.maximum(T - 1 - j, 0)), j] = 1.0
    return np.ascontiguousarray(consts), onehot


def kernel(**inputs):
    import concourse.bacc as bacc
    from concourse.bass_utils import run_bass_kernel_spmd as run

    a = {k: np.asarray(v) for k, v in inputs.items()}
    w_in = a["w_in"]
    z, xbc, dt, q, k, v, f = np.split(w_in, np.cumsum([1024, 1536, 16, 1024, 1024, 1024]), axis=1)
    w2 = a["w_in_2"][0]
    q2, k2, v2, val2, gate2 = np.split(w2, [1024, 2048, 3072, 4096], axis=1)
    up, down = a["w1_2"][0], a["w2_2"][0]
    units = [_feature_units(xbc), _row_units(v), _feature_units(z), _pairs(q, k), _ordered(a["w_out"], OUT1_ORDER),
             _feature_units(a["peer_wq"])]
    for r in range(PEER_ROUNDS):
        es = slice(r * D, (r + 1) * D)
        units += [_feature_units(a["peer_u"][es].T), _row_units(a["peer_v"][es])]
    units += [_feature_units(a["wk_c_2"][0]), _row_units(a["wv_c_2"][0])]
    units += [_pairs(val2, gate2), _pairs(q2, k2), _row_units(v2), _ordered(a["w_out_2"][0], OUT2_ORDER)]
    units += [_feature_units(a["wq_c_2"][0]), _row_units(a["wo_c_2"][0])]
    for r in range(FF_ROUNDS):
        units += [_feature_units(up[:, r * D:(r + 1) * D]), _row_units(down[r * D:(r + 1) * D])]
    stream = np.concatenate(units, axis=0)
    assert stream.shape[0] == UNITS
    cols = np.concatenate([
        _cols(a["ln1_w"]), _cols(a["ln2_w"]), _cols(a["g_mix_2"][0]), _cols(a["g_cross_2"][0]), _cols(a["g_mem_2"][0]), _cols(a["g_mlp_2"][0]),
        a["conv_w"].reshape(SSD_CONV, XBC_TILES, P).transpose(2, 1, 0).reshape(P, -1), _cols(a["conv_b"]),
        _cols(a["ssd_norm_w"]), _cols(np.repeat(a["d_skip"], 64)),
        a["conv_w_2"][0].reshape(CONV_K, CONV_TILES, P).transpose(2, 0, 1).reshape(P, -1), _cols(a["conv_b_2"][0]),
        _cols(a["conv_ln_g_2"][0]), _cols(a["conv_ln_b_2"][0])], axis=1)
    consts, onehot = _constants()
    keys = np.stack([a["peer_k1"], a["peer_k2"]], axis=1).reshape(16, PEER_KEYS, P).transpose(2, 0, 1)
    arrays = {
        "x": a["x"].reshape(T, D), "mem": a["mem_2"].reshape(T, D), "stream": stream, "cols": cols, "consts": consts,
        "rows": np.concatenate([a["dt_bias"], a["fox_f_bias"], a["a_log"]])[None, :],
        "wide": np.stack([a["lnf_w"], a["g_final_2"]]),
        "wdtf": np.concatenate([dt, f], axis=1).reshape(KT, P, 32).transpose(1, 0, 2),
        "keys": keys, "rel": a["rel_bias_2"], "onehot": onehot,
    }
    arrays = {f"{n}_dram": np.ascontiguousarray(v) for n, v in arrays.items()}
    nc = bacc.Bacc("TRN2", target_bir_lowering=False, num_devices=1)
    aps = [nc.dram_tensor(n, v.shape, mybir.dt.from_np(v.dtype), kind="ExternalInput").ap() for n, v in arrays.items()]
    aps.append(nc.dram_tensor("out_dram", (T, D), F32, kind="ExternalOutput").ap())
    build(nc, *aps)
    got = run(nc, [arrays], core_ids=[0])
    return got.results[0]["out_dram"].reshape(1, T, D)
```
